# Optimizing a Trainium2 kernel written in Bass

```python
import jax, jax.numpy as jnp
from jax import lax
import numpy as np
import math

D_MODEL = 1024
BATCH = 1
SEQ = 256
DEPTH = 1

MEM_LEN = 256
HEAD_DIM = 64
LRU_WIDTH = D_MODEL // 2
LRU_BLOCKS = 8
LRU_BLOCK_W = LRU_WIDTH // LRU_BLOCKS
CONV_W = 4
LRU_C = 8.0
MOBA_HEADS = 4
MOBA_WIDTH = MOBA_HEADS * HEAD_DIM
MOBA_BLOCK = 256
MOBA_TOPK = 3
Q_CHUNK = 128
MEM_HEADS = 4
MEM_WIDTH = MEM_HEADS * HEAD_DIM
MIX_WIDTH = LRU_WIDTH + MOBA_WIDTH + MEM_WIDTH
IN_WIDTH = 2 * LRU_WIDTH + 3 * MOBA_WIDTH + MEM_WIDTH
D_FF = ((8 * D_MODEL // 3 + 127) // 128) * 128
NORM_EPS = 1e-6


def rms_norm(x, g):
    xf = x.astype(jnp.float32)
    y = xf * lax.rsqrt(jnp.mean(xf * xf, axis=-1, keepdims=True) + NORM_EPS)
    return (y * g.astype(jnp.float32)).astype(x.dtype)

def swiglu(x, w_in, w_out):
    a, b = jnp.split(x @ w_in, 2, axis=-1)
    return (jax.nn.silu(a) * b) @ w_out

def alibi_slopes(n_heads):
    return 2.0 ** (-8.0 * jnp.arange(1, n_heads + 1, dtype=jnp.float32) / n_heads)

def split_heads(t, n_heads):
    b, s, _ = t.shape
    return t.reshape(b, s, n_heads, HEAD_DIM).transpose(0, 2, 1, 3)

def merge_heads(t):
    b, h, s, d = t.shape
    return t.transpose(0, 2, 1, 3).reshape(b, s, h * d)

def causal_depthwise_conv(x, w, bias):
    c = x.shape[-1]
    y = lax.conv_general_dilated(
        x, w[:, None, :].astype(x.dtype), window_strides=(1,), padding=[(CONV_W - 1, 0)],
        dimension_numbers=("NWC", "WIO", "NWC"), feature_group_count=c)
    return y + bias.astype(x.dtype)

def rg_lru(xb, a_w, a_b, x_w, x_b, lam):
    b, s, c = xb.shape
    xf = xb.astype(jnp.float32)
    xblk = xf.reshape(b, s, LRU_BLOCKS, LRU_BLOCK_W)
    r = jax.nn.sigmoid(jnp.einsum("bsnc,ncd->bsnd", xblk, a_w.astype(jnp.float32)) + a_b.astype(jnp.float32)).reshape(b, s, c)
    i = jax.nn.sigmoid(jnp.einsum("bsnc,ncd->bsnd", xblk, x_w.astype(jnp.float32)) + x_b.astype(jnp.float32)).reshape(b, s, c)
    log_a = -LRU_C * r * jax.nn.softplus(-lam.astype(jnp.float32))
    a = jnp.exp(log_a)
    mult = jnp.sqrt(-jnp.expm1(2.0 * log_a))
    mult = jnp.where(jnp.arange(s)[None, :, None] == 0, 1.0, mult)
    bt = mult * i * xf

    def combine(left, right):
        a1, b1 = left
        a2, b2 = right
        return a1 * a2, a2 * b1 + b2

    _, h = lax.associative_scan(combine, (a, bt), axis=1)
    return h

def moba_attention(q, k, v):
    b, h, s, hd = q.shape
    n_blk = -(-s // MOBA_BLOCK)
    s_pad = n_blk * MOBA_BLOCK
    pad = s_pad - s
    if pad:
        widths = ((0, 0), (0, 0), (0, pad), (0, 0))
        q, k, v = jnp.pad(q, widths), jnp.pad(k, widths), jnp.pad(v, widths)
    kb = k.reshape(b, h, n_blk, MOBA_BLOCK, hd)
    vb = v.reshape(b, h, n_blk, MOBA_BLOCK, hd)
    k_mean = jnp.mean(kb.astype(jnp.float32), axis=3)
    gate = jnp.einsum("bhsd,bhnd->bhsn", q.astype(jnp.float32), k_mean)
    q_blk = jnp.arange(s_pad) // MOBA_BLOCK
    fully_past = jnp.arange(n_blk)[None, :] < q_blk[:, None]
    gate = jnp.where(fully_past, gate, -jnp.inf)
    n_sel = min(MOBA_TOPK, n_blk)
    gate_top, sel = lax.top_k(gate, n_sel)
    sel_ok = gate_top > -jnp.inf
    slopes = alibi_slopes(h)
    scale = hd ** -0.5
    offs = jnp.arange(MOBA_BLOCK)
    gather_blocks = jax.vmap(jax.vmap(lambda blocks, idx: blocks[idx]))

    def chunk(c):
        start = c * Q_CHUNK
        qc = lax.dynamic_slice_in_dim(q, start, Q_CHUNK, axis=2)
        selc = lax.dynamic_slice_in_dim(sel, start, Q_CHUNK, axis=2)
        okc = lax.dynamic_slice_in_dim(sel_ok, start, Q_CHUNK, axis=2)
        own = start // MOBA_BLOCK
        k_own = lax.dynamic_index_in_dim(kb, own, axis=2, keepdims=False)
        v_own = lax.dynamic_index_in_dim(vb, own, axis=2, keepdims=False)
        k_sel = gather_blocks(kb, selc)
        v_sel = gather_blocks(vb, selc)
        t_q = start + jnp.arange(Q_CHUNK)
        s_own = jnp.einsum("bhqd,bhkd->bhqk", qc, k_own).astype(jnp.float32) * scale
        d_own = t_q[:, None] - (own * MOBA_BLOCK + offs)[None, :]
        s_own = jnp.where(d_own >= 0, s_own - slopes[:, None, None] * d_own.astype(jnp.float32), -jnp.inf)
        s_sel = jnp.einsum("bhqd,bhqjkd->bhqjk", qc, k_sel).astype(jnp.float32) * scale
        d_sel = t_q[None, None, :, None, None] - (selc[..., None] * MOBA_BLOCK + offs)
        s_sel = jnp.where(okc[..., None], s_sel - slopes[None, :, None, None, None] * d_sel.astype(jnp.float32), -jnp.inf)
        scores = jnp.concatenate([s_sel.reshape(b, h, Q_CHUNK, n_sel * MOBA_BLOCK), s_own], axis=-1)
        p = jax.nn.softmax(scores, axis=-1)
        p_sel = p[..., :n_sel * MOBA_BLOCK].reshape(b, h, Q_CHUNK, n_sel, MOBA_BLOCK).astype(v.dtype)
        p_own = p[..., n_sel * MOBA_BLOCK:].astype(v.dtype)
        return (jnp.einsum("bhqjk,bhqjkd->bhqd", p_sel, v_sel)
                + jnp.einsum("bhqk,bhkd->bhqd", p_own, v_own))

    out = lax.map(chunk, jnp.arange(s_pad // Q_CHUNK))
    out = out.transpose(1, 2, 0, 3, 4).reshape(b, h, s_pad, hd)
    return out[:, :, :s]

def memory_attention(q, k, v):
    scores = jnp.einsum("bhsd,bhmd->bhsm", q, k).astype(jnp.float32) * (HEAD_DIM ** -0.5)
    p = jax.nn.softmax(scores, axis=-1)
    return jnp.einsum("bhsm,bhmd->bhsd", p.astype(v.dtype), v)

def first_inputs(seed: int = 0) -> dict:
    key = jax.random.key(seed)
    ks = jax.random.split(key, 24)

    def normal(k, shape, scale):
        return jax.random.normal(k, shape, jnp.float32) * scale

    def gain(k, n):
        return 1.0 + 0.02 * jax.random.normal(k, (DEPTH, n), jnp.float32)

    u = jax.random.uniform(ks[12], (DEPTH, LRU_WIDTH), jnp.float32, minval=0.9, maxval=0.999)
    a0 = u ** (1.0 / LRU_C)
    lam = jnp.log(a0) - jnp.log1p(-a0)
    return {
        "x": normal(ks[0], (BATCH, SEQ, D_MODEL), 1.0),
        "mem": normal(ks[1], (BATCH, MEM_LEN, D_MODEL), 1.0),
        "ffn1_norm": gain(ks[2], D_MODEL),
        "ffn1_w_in": normal(ks[3], (DEPTH, D_MODEL, 2 * D_FF), D_MODEL ** -0.5),
        "ffn1_w_out": normal(ks[4], (DEPTH, D_FF, D_MODEL), D_FF ** -0.5),
        "mix_norm": gain(ks[5], D_MODEL),
        "mem_norm": gain(ks[6], D_MODEL),
        "w_in": normal(ks[7], (DEPTH, D_MODEL, IN_WIDTH), D_MODEL ** -0.5),
        "lru_conv_w": normal(ks[8], (DEPTH, CONV_W, LRU_WIDTH), CONV_W ** -0.5),
        "lru_conv_b": normal(ks[9], (DEPTH, LRU_WIDTH), 0.01),
        "lru_a_w": normal(ks[10], (DEPTH, LRU_BLOCKS, LRU_BLOCK_W, LRU_BLOCK_W), LRU_BLOCK_W ** -0.5),
        "lru_a_b": normal(ks[11], (DEPTH, LRU_BLOCKS, LRU_BLOCK_W), 0.01),
        "lru_x_w": normal(ks[13], (DEPTH, LRU_BLOCKS, LRU_BLOCK_W, LRU_BLOCK_W), LRU_BLOCK_W ** -0.5),
        "lru_x_b": normal(ks[14], (DEPTH, LRU_BLOCKS, LRU_BLOCK_W), 0.01),
        "lru_lambda": lam,
        "moba_q_norm": gain(ks[15], HEAD_DIM),
        "moba_k_norm": gain(ks[16], HEAD_DIM),
        "mem_w_kv": normal(ks[17], (DEPTH, D_MODEL, 2 * MEM_WIDTH), D_MODEL ** -0.5),
        "mem_q_norm": gain(ks[18], HEAD_DIM),
        "mem_k_norm": gain(ks[19], HEAD_DIM),
        "w_out": normal(ks[20], (DEPTH, MIX_WIDTH, D_MODEL), MIX_WIDTH ** -0.5),
        "ffn2_norm": gain(ks[21], D_MODEL),
        "ffn2_w_in": normal(ks[22], (DEPTH, D_MODEL, 2 * D_FF), D_MODEL ** -0.5),
        "ffn2_w_out": normal(ks[23], (DEPTH, D_FF, D_MODEL), D_FF ** -0.5),
    }

def first_block(x, mem, ffn1_norm, ffn1_w_in, ffn1_w_out, mix_norm, mem_norm, w_in,
              lru_conv_w, lru_conv_b, lru_a_w, lru_a_b, lru_x_w, lru_x_b, lru_lambda,
              moba_q_norm, moba_k_norm, mem_w_kv, mem_q_norm, mem_k_norm, w_out,
              ffn2_norm, ffn2_w_in, ffn2_w_out):
    split_at = np.cumsum([LRU_WIDTH, LRU_WIDTH, MOBA_WIDTH, MOBA_WIDTH, MOBA_WIDTH])
    for l in range(DEPTH):
        x = x + 0.5 * swiglu(rms_norm(x, ffn1_norm[l]), ffn1_w_in[l], ffn1_w_out[l])

        u = rms_norm(x, mix_norm[l]) @ w_in[l]
        lru_x, lru_g, mq, mk, mv, cq = jnp.split(u, split_at, axis=-1)

        xb = causal_depthwise_conv(lru_x, lru_conv_w[l], lru_conv_b[l])
        h_lru = rg_lru(xb, lru_a_w[l], lru_a_b[l], lru_x_w[l], lru_x_b[l], lru_lambda[l])
        y_lru = (h_lru * jax.nn.gelu(lru_g.astype(jnp.float32))).astype(x.dtype)

        q = rms_norm(split_heads(mq, MOBA_HEADS), moba_q_norm[l])
        k = rms_norm(split_heads(mk, MOBA_HEADS), moba_k_norm[l])
        v = split_heads(mv, MOBA_HEADS)
        y_moba = merge_heads(moba_attention(q, k, v))

        mkv = rms_norm(mem, mem_norm[l]) @ mem_w_kv[l]
        mem_k, mem_v = jnp.split(mkv, 2, axis=-1)
        qc = rms_norm(split_heads(cq, MEM_HEADS), mem_q_norm[l])
        kc = rms_norm(split_heads(mem_k, MEM_HEADS), mem_k_norm[l])
        y_mem = merge_heads(memory_attention(qc, kc, split_heads(mem_v, MEM_HEADS)))

        mixed = jnp.concatenate([y_lru, y_moba.astype(x.dtype), y_mem.astype(x.dtype)], axis=-1)
        x = x + mixed @ w_out[l]

        x = x + 0.5 * swiglu(rms_norm(x, ffn2_norm[l]), ffn2_w_in[l], ffn2_w_out[l])
    return x


DEPTH_2 = 2

CHUNK = 64
Q_BLOCK = 128
EPS = 1e-6
MAX_OFFSET = 4096

HG_HEADS = 4
HG_DK = 128
HG_DV = 128
HG_WIDTH = HG_HEADS * HG_DV

MLA_HEADS = 8
MLA_NOPE = 64
MLA_ROPE = 32
MLA_V = 64
MLA_Q_LORA = 384
MLA_KV_LORA = 256
MLA_DQK = MLA_NOPE + MLA_ROPE
MLA_WIDTH = MLA_HEADS * MLA_V
ROPE_BASE = 10000.0

N_EXPERTS = 16
N_GROUPS = 4
EXPERTS_PER_GROUP = N_EXPERTS // N_GROUPS
TOPK_GROUPS = 1
TOP_K = 2
D_EXPERT = 512

IN_SIZES = (HG_HEADS * HG_DK,
            HG_HEADS * HG_DK,
            HG_HEADS * HG_DV,
            HG_WIDTH,
            MLA_Q_LORA,
            MLA_KV_LORA,
            MLA_ROPE,
            2 * D_MODEL)
IN_COLS = int(sum(IN_SIZES))
IN_SPLITS = tuple(int(v) for v in np.cumsum(IN_SIZES)[:-1])


def rmsnorm(x, g):
    xf = x.astype(jnp.float32)
    y = xf * lax.rsqrt(jnp.mean(xf * xf, axis=-1, keepdims=True) + EPS)
    return (y * g.astype(jnp.float32)).astype(x.dtype)

def rotary(x, pos):
    half = x.shape[-1] // 2
    inv = ROPE_BASE ** (-jnp.arange(half, dtype=jnp.float32) / half)
    ang = pos.astype(jnp.float32)[..., None] * inv
    cos = jnp.cos(ang)[:, :, None, :]
    sin = jnp.sin(ang)[:, :, None, :]
    xf = x.astype(jnp.float32)
    x1, x2 = xf[..., :half], xf[..., half:]
    return jnp.concatenate([x1 * cos - x2 * sin, x1 * sin + x2 * cos], -1).astype(x.dtype)

def hgrn2_mix(q, f_logit, v, lb):
    B, S = q.shape[0], q.shape[1]
    nc = S // CHUNK
    lbh = lb.astype(jnp.float32).reshape(HG_HEADS, HG_DK)
    f = lbh + (1.0 - lbh) * jax.nn.sigmoid(f_logit.astype(jnp.float32))
    log_f = jnp.log(f)
    k = 1.0 - f
    qf = jax.nn.silu(q.astype(jnp.float32)) * (HG_DK ** -0.5)
    vf = v.astype(jnp.float32)

    def to_chunks(t):
        return t.reshape(B, nc, CHUNK, HG_HEADS, t.shape[-1]).transpose(1, 0, 3, 2, 4)

    qc, kc, vc, gc = to_chunks(qf), to_chunks(k), to_chunks(vf), to_chunks(log_f)
    causal = jnp.tril(jnp.ones((CHUNK, CHUNK), dtype=bool))[:, :, None]

    def step(state, inp):
        qb, kb, vb, gb = inp
        b = jnp.cumsum(gb, axis=2)
        rel = b[:, :, :, None, :] - b[:, :, None, :, :]
        decay = jnp.exp(jnp.where(causal, rel, -jnp.inf))
        attn = jnp.einsum('bhtd,bhtsd,bhsd->bhts', qb, decay, kb)
        intra = jnp.einsum('bhts,bhsv->bhtv', attn, vb)
        inter = jnp.einsum('bhtd,bhdv->bhtv', qb * jnp.exp(b), state)
        b_last = b[:, :, -1:, :]
        k_dec = kb * jnp.exp(b_last - b)
        new_state = state * jnp.exp(b_last[:, :, 0, :, None]) + jnp.einsum('bhsd,bhsv->bhdv', k_dec, vb)
        return new_state, intra + inter

    state0 = jnp.zeros((B, HG_HEADS, HG_DK, HG_DV), jnp.float32)
    _, out = lax.scan(step, state0, (qc, kc, vc, gc))
    return out.transpose(1, 0, 3, 2, 4).reshape(B, S, HG_HEADS, HG_DV)

def mla_mix(c_q, c_kv, k_rope, pos, q_norm_g, w_q_up, kv_norm_g, w_kv_up):
    B, S = c_q.shape[0], c_q.shape[1]
    q = (rmsnorm(c_q, q_norm_g) @ w_q_up).reshape(B, S, MLA_HEADS, MLA_DQK)
    q = jnp.concatenate([q[..., :MLA_NOPE], rotary(q[..., MLA_NOPE:], pos)], -1)
    kv = (rmsnorm(c_kv, kv_norm_g) @ w_kv_up).reshape(B, S, MLA_HEADS, MLA_NOPE + MLA_V)
    k_nope, v = kv[..., :MLA_NOPE], kv[..., MLA_NOPE:]
    k_pe = rotary(k_rope[:, :, None, :], pos)
    k = jnp.concatenate([k_nope, jnp.broadcast_to(k_pe, (B, S, MLA_HEADS, MLA_ROPE)).astype(k_nope.dtype)], -1)
    scale = MLA_DQK ** -0.5
    nb = S // Q_BLOCK
    qb = q.reshape(B, nb, Q_BLOCK, MLA_HEADS, MLA_DQK).transpose(1, 0, 2, 3, 4)
    key_chunk = jnp.arange(S) // CHUNK

    def block(args):
        qblk, start = args
        q_chunk = (start + jnp.arange(Q_BLOCK)) // CHUNK
        s = jnp.einsum('bqhd,bkhd->bhqk', qblk, k, preferred_element_type=jnp.float32) * scale
        mask = key_chunk[None, :] <= q_chunk[:, None]
        p = jax.nn.softmax(jnp.where(mask, s, -jnp.inf), axis=-1).astype(v.dtype)
        return jnp.einsum('bhqk,bkhd->bqhd', p, v)

    out = lax.map(block, (qb, jnp.arange(nb, dtype=jnp.int32) * Q_BLOCK))
    return out.transpose(1, 0, 2, 3, 4).reshape(B, S, MLA_WIDTH)

def token_mix(h, pos, w_in, lb, hg_norm_g, q_norm_g, w_q_up, kv_norm_g, w_kv_up, w_br_a, w_br_b, w_out):
    B, S, D = h.shape
    proj = h @ w_in
    hq, hf, hi, hgate, cq, ckv, kr, gates = jnp.split(proj, IN_SPLITS, axis=-1)
    o_a = hgrn2_mix(hq.reshape(B, S, HG_HEADS, HG_DK), hf.reshape(B, S, HG_HEADS, HG_DK),
                    hi.reshape(B, S, HG_HEADS, HG_DV), lb)
    o_a = rmsnorm(o_a, hg_norm_g.reshape(HG_HEADS, HG_DV)).reshape(B, S, HG_WIDTH)
    o_a = (o_a * jax.nn.silu(hgate.astype(jnp.float32))).astype(h.dtype)
    y_a = o_a @ w_br_a
    y_b = mla_mix(cq, ckv, kr, pos, q_norm_g, w_q_up, kv_norm_g, w_kv_up) @ w_br_b
    g = jax.nn.sigmoid(gates.astype(jnp.float32))
    g_a, g_b = g[..., :D], g[..., D:]
    merged = (g_a * y_a.astype(jnp.float32) + g_b * y_b.astype(jnp.float32)).astype(h.dtype)
    return merged @ w_out

def grouped_moe(h, w_router, router_bias, w_gate, w_up, w_down):
    B, S, D = h.shape
    t = h.reshape(-1, D)
    scores = jax.nn.sigmoid((t @ w_router).astype(jnp.float32))
    biased = (scores + router_bias.astype(jnp.float32)).reshape(-1, N_GROUPS, EXPERTS_PER_GROUP)
    group_score = lax.top_k(biased, 2)[0].sum(-1)
    _, gidx = lax.top_k(group_score, TOPK_GROUPS)
    gmask = jax.nn.one_hot(gidx, N_GROUPS, dtype=jnp.float32).sum(-2) > 0
    masked = jnp.where(gmask[:, :, None], biased, -jnp.inf).reshape(-1, N_EXPERTS)
    _, eidx = lax.top_k(masked, TOP_K)
    sel = jnp.take_along_axis(scores, eidx, axis=-1)
    w = sel / sel.sum(-1, keepdims=True)
    combine = (jax.nn.one_hot(eidx, N_EXPERTS, dtype=jnp.float32) * w[..., None]).sum(-2)
    y = jnp.zeros(t.shape, jnp.float32)
    for e in range(N_EXPERTS):
        he = jax.nn.silu(t @ w_gate[e]) * (t @ w_up[e])
        y = y + combine[:, e:e + 1] * (he @ w_down[e]).astype(jnp.float32)
    return y.astype(h.dtype).reshape(B, S, D)

def second_inputs(seed: int = 0) -> dict:
    key = jax.random.key(seed)
    ks = jax.random.split(key, 24)
    f32 = jnp.float32
    D = D_MODEL

    def nrm(k, shape, scale):
        return jax.random.normal(k, shape, f32) * scale

    positions = (jax.random.randint(ks[2], (BATCH, 1), 0, MAX_OFFSET, dtype=jnp.int32)
                 + jnp.arange(SEQ, dtype=jnp.int32)[None, :]).astype(jnp.int32)
    return {
        "x": nrm(ks[0], (BATCH, SEQ, D), 1.0),
        "c": nrm(ks[1], (BATCH, D), 1.0),
        "positions": positions,
        "ada_w": nrm(ks[3], (DEPTH_2, D, 6 * D), 0.5 * D ** -0.5),
        "ada_b": nrm(ks[4], (DEPTH_2, 6 * D), 0.02),
        "norm1_g": 1.0 + nrm(ks[5], (DEPTH_2, D), 0.02),
        "w_in": nrm(ks[6], (DEPTH_2, D, IN_COLS), D ** -0.5),
        "hg_lb_logits": nrm(ks[7], (DEPTH_2, HG_HEADS * HG_DK), 1.0),
        "hg_norm_g": 1.0 + nrm(ks[8], (DEPTH_2, HG_WIDTH), 0.02),
        "q_norm_g": 1.0 + nrm(ks[9], (DEPTH_2, MLA_Q_LORA), 0.02),
        "w_q_up": nrm(ks[10], (DEPTH_2, MLA_Q_LORA, MLA_HEADS * MLA_DQK), MLA_Q_LORA ** -0.5),
        "kv_norm_g": 1.0 + nrm(ks[11], (DEPTH_2, MLA_KV_LORA), 0.02),
        "w_kv_up": nrm(ks[12], (DEPTH_2, MLA_KV_LORA, MLA_HEADS * (MLA_NOPE + MLA_V)), MLA_KV_LORA ** -0.5),
        "w_br_a": nrm(ks[13], (DEPTH_2, HG_WIDTH, D), HG_WIDTH ** -0.5),
        "w_br_b": nrm(ks[14], (DEPTH_2, MLA_WIDTH, D), MLA_WIDTH ** -0.5),
        "w_out": nrm(ks[15], (DEPTH_2, D, D), D ** -0.5),
        "norm2_g": 1.0 + nrm(ks[16], (DEPTH_2, D), 0.02),
        "w_router": nrm(ks[17], (D, N_EXPERTS), D ** -0.5),
        "router_bias": nrm(ks[18], (N_EXPERTS,), 0.01),
        "w_gate": nrm(ks[19], (DEPTH_2, N_EXPERTS, D, D_EXPERT), D ** -0.5),
        "w_up": nrm(ks[20], (DEPTH_2, N_EXPERTS, D, D_EXPERT), D ** -0.5),
        "w_down": nrm(ks[21], (DEPTH_2, N_EXPERTS, D_EXPERT, D), D_EXPERT ** -0.5),
        "final_g": 1.0 + nrm(ks[22], (D,), 0.02),
    }

def second_block(x, c, positions, ada_w, ada_b, norm1_g, w_in, hg_lb_logits, hg_norm_g,
              q_norm_g, w_q_up, kv_norm_g, w_kv_up, w_br_a, w_br_b, w_out, norm2_g,
              w_router, router_bias, w_gate, w_up, w_down, final_g):
    D = D_MODEL
    lb_soft = jax.nn.softmax(hg_lb_logits.astype(jnp.float32), axis=0)
    lb_all = jnp.cumsum(lb_soft, axis=0) - lb_soft[0:1]
    c_act = jax.nn.silu(c)
    for l in range(DEPTH_2):
        mod = c_act @ ada_w[l] + ada_b[l]
        sh1, sc1, g1 = mod[:, None, 0:D], mod[:, None, D:2 * D], mod[:, None, 2 * D:3 * D]
        sh2, sc2, g2 = mod[:, None, 3 * D:4 * D], mod[:, None, 4 * D:5 * D], mod[:, None, 5 * D:6 * D]
        h = rmsnorm(x, norm1_g[l]) * (1.0 + sc1) + sh1
        x = x + g1 * token_mix(h, positions, w_in[l], lb_all[l], hg_norm_g[l], q_norm_g[l], w_q_up[l],
                               kv_norm_g[l], w_kv_up[l], w_br_a[l], w_br_b[l], w_out[l])
        h = rmsnorm(x, norm2_g[l]) * (1.0 + sc2) + sh2
        x = x + g2 * grouped_moe(h, w_router, router_bias, w_gate[l], w_up[l], w_down[l])
    return rmsnorm(x, final_g)


def setup_inputs(seed=0):
    out = dict(first_inputs(seed))
    for name, value in second_inputs(seed + 1).items():
        if name != "x":
            out[name + "_2"] = value
    return out


def reference(
    x, mem, ffn1_norm, ffn1_w_in, ffn1_w_out, mix_norm, mem_norm, w_in, lru_conv_w, lru_conv_b,
    lru_a_w, lru_a_b, lru_x_w, lru_x_b, lru_lambda, moba_q_norm, moba_k_norm, mem_w_kv,
    mem_q_norm, mem_k_norm, w_out, ffn2_norm, ffn2_w_in, ffn2_w_out, c_2, positions_2, ada_w_2,
    ada_b_2, norm1_g_2, w_in_2, hg_lb_logits_2, hg_norm_g_2, q_norm_g_2, w_q_up_2, kv_norm_g_2,
    w_kv_up_2, w_br_a_2, w_br_b_2, w_out_2, norm2_g_2, w_router_2, router_bias_2, w_gate_2,
    w_up_2, w_down_2, final_g_2,
):
    x = first_block(
        x, mem, ffn1_norm, ffn1_w_in, ffn1_w_out, mix_norm, mem_norm, w_in, lru_conv_w,
        lru_conv_b, lru_a_w, lru_a_b, lru_x_w, lru_x_b, lru_lambda, moba_q_norm, moba_k_norm,
        mem_w_kv, mem_q_norm, mem_k_norm, w_out, ffn2_norm, ffn2_w_in, ffn2_w_out,
    )
    return second_block(
        x, c_2, positions_2, ada_w_2, ada_b_2, norm1_g_2, w_in_2, hg_lb_logits_2, hg_norm_g_2,
        q_norm_g_2, w_q_up_2, kv_norm_g_2, w_kv_up_2, w_br_a_2, w_br_b_2, w_out_2, norm2_g_2,
        w_router_2, router_bias_2, w_gate_2, w_up_2, w_down_2, final_g_2,
    )


_drawn_inputs = setup_inputs


def setup_inputs(seed=0):
    import zlib

    import numpy as np

    out = dict(_drawn_inputs(seed))
    spreads = {}
    factors = {'ffn1_norm': 3.167,
     'mix_norm': 4.784,
     'mem_norm': 8.0,
     'lru_a_b': 27.211,
     'lru_x_b': 21.348,
     'moba_q_norm': 6.528,
     'moba_k_norm': 4.124,
     'mem_q_norm': 5.165,
     'mem_k_norm': 8.0,
     'ffn2_norm': 3.191,
     'norm1_g_2': 4.068,
     'hg_lb_logits_2': 4.631,
     'hg_norm_g_2': 29.069,
     'q_norm_g_2': 21.704,
     'kv_norm_g_2': 19.268,
     'final_g_2': 8.724,
     'lru_conv_b': 3.359,
     'norm2_g_2': 8.0,
     'router_bias_2': 8.0}
    for name, (base, spread) in spreads.items():
        noise = np.random.default_rng([zlib.crc32(name.encode()), seed]).standard_normal(out[name].shape)
        drawn = base * np.exp(spread * noise) if base else spread * noise
        out[name] = __import__('jax').numpy.asarray(drawn.astype(out[name].dtype))
    for name, factor in factors.items():
        out[name] = (out[name] * factor).astype(out[name].dtype)
    return out
```

```python
from contextlib import ExitStack

import numpy as np
import concourse.bass as bass
from concourse import mybir

F32 = mybir.dt.float32
I32 = mybir.dt.int32
U8 = mybir.dt.uint8
ALU = mybir.AluOpType
ACT = mybir.ActivationFunctionType
AX = mybir.AxisListType

P = 128
SEQ = 256
T = SEQ // P
D = 1024
KC = D // P
EPS = 1e-6
HD = 64
LW = 512
LC = LW // P
LRU_C = 8.0
DFF = 2816
LAYERS = 2
HGH, DK = 4, 128
QL, KVL, ROPE, NOPE, MV = 384, 256, 32, 64, 64
MH = 8
DQK = NOPE + ROPE
NE, NG, EPG, DE = 16, 4, 4, 512
CHUNK = 64
FB = 256
RING = 6
TILE = 2048
LEVELS = [1, 2, 4, 8, 16, 32, 64, 128]
NEG = -1.0e30
MISC = QL + KVL + ROPE
ADA = 6 * D
ADA_SLABS = ADA // FB


def ffn_pos(n, kind, c):
    if kind == "down":
        return 3 * n - 1 if c == n - 1 else 3 * c + 4
    off = {"gate": 0, "up": 1}[kind]
    return off if c == 0 else 3 * c - 1 + off


def build(nc, a):
    ctx = ExitStack()
    with ctx:
        def sb(name, shape, dt=F32):
            return ctx.enter_context(nc.sbuf_tensor("sb_" + name, shape, dt))

        def sem(name):
            return ctx.enter_context(nc.semaphore(name))

        bank = [ctx.enter_context(nc.psum_tensor(f"bank{i}", [P, 512], F32)) for i in range(8)]

        x = sb("x", [P, T, D])
        hT = sb("hT", [P, KC, SEQ])
        xn = sb("xn", [P, T, D])
        ring = sb("ring", [P, RING, TILE])
        small_a = sb("small_a", [P, 2, 512])
        small_b = sb("small_b", [P, 2, 512])
        gbc = sb("gbc", [P, D])
        ident = sb("ident", [P, P])
        ones = sb("ones", [P, P])
        pcol = sb("pcol", [P, 2, P])
        abcol = sb("abcol", [P, LAYERS, 48])
        modc = sb("modc", [P, LAYERS, 48])
        scol = sb("scol", [P, LAYERS, 2, KC])
        csilu = sb("csilu", [P, KC])
        stat = sb("stat", [P, 8, 32])
        lbc = sb("lbc", [P, 8, HGH])
        lruc = sb("lruc", [P, 10, LC])
        level_mask = sb("level_mask", [P, 8, P])
        seg = sb("seg", [P, 8, 1028], U8)
        dist = sb("dist", [P, T, SEQ])
        mla_mask = sb("mla_mask", [P, T, SEQ])
        rope_t = sb("rope_t", [P, 12, T, 16])
        pos_i = sb("pos_i", [P, T], I32)
        rank = sb("rank", [P, NE])
        router = sb("router", [P, KC, NE])
        rbias = sb("rbias", [P, NE])
        combT = sb("combT", [NE, SEQ])
        arena = sb("arena", [P, 25600])

        def view(at, *shape):
            n = int(np.prod(shape))
            assert at + n <= 25600, (at, shape)
            v = arena[:, at:at + n]
            if len(shape) == 2:
                v = v.rearrange("p (a b) -> p a b", b=shape[1])
            if len(shape) == 3:
                v = v.rearrange("p (a b c) -> p a b c", b=shape[1], c=shape[2])
            if len(shape) == 4:
                v = v.rearrange("p (a b c d) -> p a b c d", b=shape[1], c=shape[2], d=shape[3])
            return v

        prow = view(12000, 2, P)
        abrow = view(12256, LAYERS, P)
        iot = view(12512, 3, P).bitcast(I32)
        ada_acc = view(0, ADA_SLABS, FB)
        ada_w = view(6144, 2, KC, FB)
        mixT = view(0, KC, SEQ)
        memx = view(19456, T, D)
        memT = view(21504, KC, SEQ)
        qk4 = view(6144, 4, 512)
        qkT = view(8192, 4, 2, SEQ)
        v2 = view(10240, 2, T, 256)
        att_p = view(11264, 16, SEQ)
        att_pT = view(15360, 8, T, SEQ)
        xl = view(19456, LC, SEQ + 4)
        xb = view(20496, LC, SEQ)
        lr = view(21520, LC, SEQ)
        li = view(22544, LC, SEQ)
        lt = view(2048, LC, SEQ)
        lt2 = view(3072, LC, SEQ)
        gel = view(5120, LC, SEQ)
        lru_w_all = view(24576, 2, LC, P)
        G = view(0, T, 2, D)
        hq = view(4096, HGH, SEQ)
        hk = view(5120, HGH, SEQ)
        hg = view(6144, HGH, SEQ)
        hf = view(7168, HGH, SEQ)
        scan_f = view(8192, HGH * SEQ)
        scan_b = view(9216, HGH * SEQ)
        hy = view(10240, HGH * SEQ)
        attT = view(11264, 3, HGH, P)
        prod = view(12800, T, HGH, P)
        mlp_p = view(4096, 16, SEQ)
        mlp_pT = view(8192, 8, T, SEQ)
        oaT = view(13312, HGH, SEQ)
        misc = view(14336, T, MISC)
        cT = view(15680, 5, SEQ)
        q96 = view(16960, T, MH, DQK)
        k96 = view(18496, T, MH, DQK)
        vm = view(20032, T, MH, MV)
        qT96 = view(21056, MH, SEQ)
        kT96 = view(23104, MH, SEQ)
        ymT = view(14336, 4, SEQ)
        merged = view(16960, T, D)
        diag = view(19008, KC, P)
        oa = view(8192, T, 512)
        oa_sq = view(9216, 1024)
        fin = view(21056, D)
        scr = small_b[:, :, :].rearrange("p a b -> p (a b)")
        hgate = xn[:, 0, :].rearrange("p (h s) -> p h s", h=HGH)
        vh = xn[:, 1, :].rearrange("p (t c) -> p t c", t=T)
        cb = view(0, NE, SEQ)
        sel = view(4096, NE, P)
        ep = view(6144, 2, 512)
        rt = view(7168, 16, T * NE)

        acc = bank[0:4]
        two = [b[:, :].rearrange("p (a c) -> p a c", a=2) for b in bank]

        rows, row_loads = {}, []

        def param(tile, name, ap, n):
            at = sum(v[2] for v in rows.values() if v[0] == tile)
            rows[name] = (tile, at, n)
            row_loads.append((tile, at, n, ap))

        def by_row(ap):
            return ap.rearrange("a (r c) -> (a r) c", c=P)

        param(0, "ffn1", by_row(a["ffn1_norm"]), 8)
        param(0, "mix", by_row(a["mix_norm"]), 8)
        param(0, "mem", by_row(a["mem_norm"]), 8)
        param(0, "ffn2", by_row(a["ffn2_norm"]), 8)
        param(0, "n1", by_row(a["norm1_g_2"]), 16)
        param(0, "n2", by_row(a["norm2_g_2"]), 16)
        param(0, "qn", by_row(a["q_norm_g_2"]), 6)
        param(0, "kvn", by_row(a["kv_norm_g_2"]), 4)
        param(0, "hgn", by_row(a["hg_norm_g_2"]), 8)
        param(0, "convw", a["lru_conv_w"].rearrange("a w (r c) -> (a w r) c", c=P), 16)
        param(0, "convb", by_row(a["lru_conv_b"]), 4)
        param(0, "ab", a["lru_a_b"].rearrange("a (r b) c -> (a r) (b c)", b=2), 4)
        param(0, "xb", a["lru_x_b"].rearrange("a (r b) c -> (a r) (b c)", b=2), 4)
        param(0, "lam", by_row(a["lru_lambda"]), 4)
        param(0, "lb", by_row(a["hg_lb_logits_2"]), 8)
        param(1, "c", by_row(a["c_2"]), 8)
        param(1, "heads", None, 4)
        row_loads.pop()
        heads_row = rows["heads"][1]
        HEAD_GAINS = ["moba_q_norm", "moba_k_norm", "mem_q_norm", "mem_k_norm"]
        N_ROW_DMA = len(row_loads) + 2 * len(HEAD_GAINS) + LAYERS

        def col(name, i=0, n=1):
            tile, at, _ = rows[name]
            return pcol[:, tile, at + i:at + i + n]

        stream, place, total = [], {}, 0

        def tile(name, src):
            nonlocal total
            stream.append((name, src))
            place[name] = total
            total += 1

        def swiglu_tiles(name, n, gate, up, down):
            nonlocal total
            stream.append((name, n, gate, up, down))
            place[name] = total
            total += 3 * n

        def cols(w, c0, n):
            return w.rearrange("(k p) n -> p k n", p=P)[:, :, bass.ds(c0, n)]

        def rws(w, r0, n):
            return w[bass.ds(r0, n * P), :].rearrange("(k p) n -> p k n", p=P)

        def dense(name, w_in, w_out):
            swiglu_tiles(name, DFF // FB,
                         lambda i, c: cols(w_in, i * (2 * FB) + c * FB, FB),
                         lambda i, c: cols(w_in, i * (2 * FB) + (DFF + c * FB), FB),
                         lambda i, c: rws(w_out, i * (2 * FB) + c * FB, FB // P))

        dense("ffn1", a["ffn1_w_in"][0], a["ffn1_w_out"][0])
        for n in range(2):
            tile(f"mem_kv{n}", cols(a["mem_w_kv"][0], n * FB, FB))
        for n in range(8):
            tile(f"w_in{n}", cols(a["w_in"][0], n * FB, FB))
        for n in range(4):
            tile(f"w_out{n}", rws(a["w_out"][0], n * FB, 2))
        dense("ffn2", a["ffn2_w_in"][0], a["ffn2_w_out"][0])
        for l in range(LAYERS):
            w2 = a["w_in_2"][l]
            for n in (0, 1, 6, 7, 2, 3, 4, 5):
                tile(f"proj{n}.{l}", cols(w2, n * FB, FB))
            for n in range(3):
                tile(f"misc{n}.{l}", cols(w2, 2048 + n * FB, min(FB, MISC - n * FB)))
            for n in range(2):
                tile(f"q_up{n}.{l}", cols(a["w_q_up_2"][l], n * QL, QL))
            tile(f"kv_up.{l}", cols(a["w_kv_up_2"][l], 0, 1024))
            for n in range(8):
                tile(f"gates{n}.{l}", cols(w2, 2048 + MISC + n * FB, FB))
            for n in range(2):
                tile(f"br_a{n}.{l}", rws(a["w_br_a_2"][l], n * FB, 2))
            for n in range(2):
                tile(f"br_b{n}.{l}", rws(a["w_br_b_2"][l], n * FB, 2))
            for n in range(4):
                tile(f"w_out{n}.{l}", rws(a["w_out_2"][l], n * FB, 2))
            wg, wu, wd = a["w_gate_2"][l], a["w_up_2"][l], a["w_down_2"][l]
            swiglu_tiles(f"moe.{l}", NE * DE // FB,
                         lambda i, c, w=wg: w.rearrange("e (k p) n -> p e k n", p=P)[:, i + c // 2, :, (c % 2) * FB:(c % 2 + 1) * FB],
                         lambda i, c, w=wu: w.rearrange("e (k p) n -> p e k n", p=P)[:, i + c // 2, :, (c % 2) * FB:(c % 2 + 1) * FB],
                         lambda i, c, w=wd: w.rearrange("e (k p) n -> p e k n", p=P)[:, i + c // 2, 2 * (c % 2):2 * (c % 2) + 2, :])

        class Signals(dict):
            def __missing__(self, name):
                self[name] = sem(name)
                return self[name]

        s = Signals()
        ring_full = [sem(f"ring_full{i}") for i in range(RING)]
        tiles_used = sem("tiles_used")
        block = ctx.enter_context(nc.Block())

        def slot_view(pos, kind):
            w = ring[:, pos % RING, :]
            if kind == 3 * QL:
                return w[:, 0:3 * QL].rearrange("p (k n) -> p k n", k=3)
            if kind == 1024:
                return w.rearrange("p (k n) -> p k n", k=2)
            return w[:, 0:KC * kind].rearrange("p (k n) -> p k n", k=KC)

        def loop_shape(n):
            j0 = 3 if n % 2 else 2
            return j0, (n - j0) // 2

        @block.sync
        def _(sp):
            sp.dma_start(x[:, :, :], a["x"][0].rearrange("(t p) d -> p t d", p=P)).then_inc(s["x_in"], 16)

            def load(pos, src, i=0):
                if not (isinstance(i, int) and pos < RING):
                    sp.wait_ge(tiles_used, RING * i + (pos - RING + 1))
                n, k = src.shape[2], src.shape[1]
                dst = ring[:, pos % RING, 0:n * k].rearrange("p (k n) -> p k n", k=k)
                sp.dma_start(dst, src).then_inc(ring_full[pos % RING], 16)

            for entry in stream:
                pos = place[entry[0]]
                if len(entry) == 2:
                    load(pos, entry[1])
                    continue
                _, n, gate, up, down = entry

                def step(i, c, first=False):
                    load(pos + ffn_pos(n, "gate", c), gate(i, c), i)
                    load(pos + ffn_pos(n, "up", c), up(i, c), i)
                    if not first:
                        load(pos + 3 * (c - 1) + 4, down(i, c - 1), i)

                j0, turns = loop_shape(n)
                step(0, 0, True)
                for c in range(1, j0):
                    step(0, c)
                with sp.Fori(0, turns) as i:
                    step(i, j0)
                    step(i, j0 + 1)
                load(pos + 3 * n - 1, down(turns - 1, j0 + 1))

            sp.wait_ge(s["out_ready"], 1)
            sp.dma_start(a["out"][0].rearrange("(t p) d -> p t d", p=P), xn[:, :, :]).then_inc(s["out_stored"], 16)
            sp.wait_ge(s["out_stored"], 16)

        @block.gpsimd
        def _(pool):
            done = [0]

            def link(ins):
                done[0] += 1
                ins.then_inc(s["pool_chain"], 1)
                pool.wait_ge(s["pool_chain"], done[0])

            pool.wait_ge(s["prow_zero"], 1)
            for tile_, at, n, ap in row_loads:
                pool.dma_start(prow[at:at + n, tile_, :], ap).then_inc(s["rows_in"], 16)
            for r, name in enumerate(HEAD_GAINS):
                for half in range(2):
                    pool.dma_start(prow[heads_row + r:heads_row + r + 1, 1, half * HD:(half + 1) * HD],
                                   a[name]).then_inc(s["rows_in"], 16)
            for l in range(LAYERS):
                pool.dma_start(abrow[0:48, l, :], a["ada_b_2"][l].rearrange("(r c) -> r c", c=P)).then_inc(s["rows_in"], 16)
            link(pool.memset(ident[:, :], 0.0))
            pool.affine_select(out=ident[:, :], in_=ident[:, :], compare_op=ALU.not_equal, fill=1.0,
                               base=0, pattern=[[-1, P]], channel_multiplier=1).then_inc(s["ident"], 1)
            pool.dma_start(pos_i[:, :], a["positions_2"].rearrange("a (t p) -> p (a t)", p=P),
                           allow_slow_non_contiguous=True).then_inc(s["pos_in"], 16)
            pool.iota(iot[:, 0, :], [[0, P]], base=0, channel_multiplier=1)
            pool.iota(iot[:, 1, :], [[1, P]], base=0, channel_multiplier=0)
            pool.iota(view(22000, 1028).bitcast(I32), [[1, 1028]], base=0, channel_multiplier=0)
            for t in range(T):
                ins = pool.iota(dist[:, t, :], [[-1, SEQ]], base=t * P, channel_multiplier=1,
                                allow_small_or_imprecise_dtypes=True)
            link(ins)
            for t in range(T):
                ins = pool.affine_select(out=dist[:, t, :], in_=dist[:, t, :], compare_op=ALU.is_ge, fill=-NEG,
                                         base=t * P, pattern=[[-1, SEQ]], channel_multiplier=1)
            ins.then_inc(s["patterns"], 1)
            link(pool.memset(mla_mask[:, :, :], 0.0))
            link(pool.memset(mla_mask[0:CHUNK, 0, CHUNK:SEQ], NEG))
            link(pool.memset(mla_mask[CHUNK:P, 0, P:SEQ], NEG))
            link(pool.memset(mla_mask[0:CHUNK, 1, P + CHUNK:SEQ], NEG))
            inv = np.float32(10000.0) ** (-np.arange(16, dtype=np.float32) / np.float32(16))
            for n in range(16):
                ins = pool.memset(rope_t[:, 0, 0, n:n + 1], float(inv[n]))
            ins.then_inc(s["inv_freq"], 1)
            pool.dma_start(router[:, :, :], a["w_router_2"].rearrange("(k p) e -> p k e", p=P)).then_inc(s["router_in"], 16)
            pool.dma_start(rbias[:, :], a["router_bias_2"].partition_broadcast(P)).then_inc(s["router_in"], 16)
            pool.wait_ge(s["lru_w_zero"], 1)
            for g, name in ((0, "lru_a_w"), (1, "lru_x_w")):
                for half in range(2):
                    w = lru_w_all[half * HD:(half + 1) * HD, g, :, half * HD:(half + 1) * HD]
                    pool.dma_start(w, a[name][0].rearrange("(c h) i j -> h i c j", h=2)[half]).then_inc(s["lru_w_in"], 16)

            pool.wait_ge(s["csilu"], 1)
            for l in range(LAYERS):
                if l:
                    pool.wait_ge(s["x"], 2)
                w = a["ada_w_2"][l].rearrange("(k p) n -> p k n", p=P)
                ada_base = l * ADA_SLABS

                def slab_load(n, b):
                    pool.dma_start(ada_w[:, b], w[:, :, bass.ds(n * FB, FB)]).then_inc(s[f"ada_in{b}"], 16)

                def slab(i, b, more):
                    n = 2 * i + b
                    pool.wait_ge(s[f"ada_in{b}"], 16 * i + 16 * (l * ADA_SLABS // 2 + 1))
                    base = 4 * (ada_base + b)
                    wv = ada_w[:, b]
                    c_b = csilu[:, :].unsqueeze(2).broadcast_to([P, KC, FB])
                    pool.tensor_tensor(wv, wv, c_b, ALU.mult).then_inc(s["ada_chain"], 1)
                    pool.wait_ge(s["ada_chain"], 8 * i + base + 1)
                    pool.tensor_tensor(wv[:, 0:4], wv[:, 0:4], wv[:, 4:8], ALU.add).then_inc(s["ada_chain"], 1)
                    pool.wait_ge(s["ada_chain"], 8 * i + base + 2)
                    pool.tensor_tensor(wv[:, 0:2], wv[:, 0:2], wv[:, 2:4], ALU.add).then_inc(s["ada_chain"], 1)
                    pool.wait_ge(s["ada_chain"], 8 * i + base + 3)
                    pool.tensor_tensor(ada_acc[:, bass.ds(n, 1), :], wv[:, 0:1], wv[:, 1:2], ALU.add).then_inc(s["ada_chain"], 1)
                    if more:
                        pool.wait_ge(s["ada_chain"], 8 * i + base + 4)
                        slab_load(n + 2, b)

                for b in range(2):
                    slab_load(b, b)
                with pool.Fori(0, ADA_SLABS // 2 - 1) as i:
                    slab(i, 0, True)
                    slab(i, 1, True)
                slab(ADA_SLABS // 2 - 1, 0, False)
                slab(ADA_SLABS // 2 - 1, 1, False)
            pool.wait_ge(s["cb_dve"], LAYERS)
            pool.dma_start(fin[:, :], a["final_g_2"].partition_broadcast(P)).then_inc(s["final_in"], 16)

        @block.scalar
        def _(act):
            A = act.activation

            def used(name):
                act.wait_ge(tiles_used, place[name] + 1)

            def root(run):
                act.wait_ge(s["ms"], run)
                A(stat[:, 2, :], stat[:, 1, :], ACT.Sqrt).then_inc(s["root"], 1)

            def turn(run, dst, scale, bias):
                act.wait_ge(s["xnT"], run)
                for k in range(KC // 2):
                    src = bank[4 + k // 2][:, (k % 2) * SEQ:(k % 2 + 1) * SEQ]
                    ins = A(dst[:, k, :], src, ACT.Identity, scale=scale(k), bias=bias(k) if bias else 0.0)
                ins.then_inc(s["hT_act"], 1)

            def swiglu(name, n, base):
                pos = place[name]

                def step(i, c, late=True):
                    j = 2 * i + c
                    p = c % 2
                    act.wait_ge(tiles_used, RING * i + (pos + (0 if c == 0 else 3 * c - 1) + 1))
                    if late:
                        act.wait_ge(s["hidden"], j + (base - 1))
                    A(small_a[:, p, :], bank[4 + 2 * p][:, :], ACT.Silu).then_inc(s["silu"], 1)

                j0, turns = loop_shape(n)
                for c in range(j0):
                    step(0, c, base + c >= 2)
                with act.Fori(0, turns) as i:
                    step(i, j0)
                    step(i, j0 + 1)

            def softmax_exp(event, run, src, dst, rows_, scale):
                act.wait_ge(s[event], run)
                for r in rows_:
                    ins = A(dst[:, r, :], src(r), ACT.Exp, bias=stat[:, 4, r:r + 1], scale=scale,
                            accum_out=stat[:, 5, r:r + 1])
                return ins

            def gain(name, off=0):
                return lambda k: col(name, off + k)

            act.dma_start(memx[:, :, :], a["mem"][0].rearrange("(t p) d -> p t d", p=P)).then_inc(s["mem_in"], 16)
            roots = iter(range(1, 100))
            root(next(roots))
            act.wait_ge(s["pcol"], 1)
            A(csilu[:, :], col("c", 0, KC), ACT.Silu).then_inc(s["csilu"], 1)
            act.wait_ge(s["small_in"], 1)
            A(lruc[:, 2, :], lruc[:, 1, :], ACT.Exp, scale=-1.0)
            A(lbc[:, 2, :], lbc[:, 0, :], ACT.Exp)
            A(lbc[:, 3, :], lbc[:, 1, :], ACT.Exp).then_inc(s["small_exp"], 1)
            act.wait_ge(s["angles"], 1)
            A(rope_t[:, 10], rope_t[:, 8], ACT.Sin)
            A(rope_t[:, 11], rope_t[:, 9], ACT.Sin).then_inc(s["sincos"], 1)
            turn(1, hT, gain("ffn1"), None)
            root(next(roots))
            n1 = DFF // FB
            swiglu("ffn1", n1, 0)

            turn(2, memT, gain("mem"), None)
            used("mem_kv1")
            A(v2[:, 1], two[1], ACT.Copy).then_inc(s["mem_v"], 1)
            root(next(roots))
            turn(3, hT, gain("mix"), None)
            act.wait_ge(s["xl_zero"], 1)
            for n in range(2):
                used(f"w_in{n}")
                ins = A(xl[:, 2 * n:2 * n + 2, 3:3 + SEQ], two[2 + n], ACT.Copy)
            ins.then_inc(s["xl"], 1)
            for n in range(2):
                used(f"w_in{2 + n}")
                ins = A(gel[:, 2 * n:2 * n + 2, :], two[4 + n], ACT.Gelu_apprx_tanh)
            ins.then_inc(s["gelu"], 1)
            used("w_in6")
            A(v2[:, 0], two[0], ACT.Copy).then_inc(s["moba_v"], 1)
            act.wait_ge(s["lru_gates"], 1)
            for c in range(LC):
                A(lr[:, c, :], bank[2 + c // 2][:, (c % 2) * SEQ:(c % 2 + 1) * SEQ], ACT.Sigmoid, bias=col("ab", c))
                ins = A(li[:, c, :], bank[4 + c // 2][:, (c % 2) * SEQ:(c % 2 + 1) * SEQ], ACT.Sigmoid, bias=col("xb", c))
            ins.then_inc(s["lru_ri"], 1)
            act.wait_ge(s["lru_ri"], 1)
            for c in range(LC):
                A(lt[:, c, :], lr[:, c, :], ACT.Tanh, scale=lruc[:, 9, c:c + 1])
            for c in range(LC):
                ins = A(lt2[:, c, :], lr[:, c, :], ACT.Exp, scale=lruc[:, 8, c:c + 1])
            ins.then_inc(s["lru_a"], 1)
            root(next(roots))
            act.wait_ge(s["lru_m2"], 1)
            A(lt[:, :, :], lt[:, :, :], ACT.Sqrt, scale=2.0).then_inc(s["lru_mult"], 1)
            act.wait_ge(s["qkT"], 1)
            for w in range(2):
                ins = A(qkT[:, w], two[w], ACT.Identity, scale=col("heads", w))
            ins.then_inc(s["qk_act"], 1)
            softmax_exp("moba_max", 1, lambda r: att_p[:, r, :], att_p, range(8), HD ** -0.5).then_inc(s["moba_exp"], 1)
            act.wait_ge(s["mem_max"], 1)
            for r in range(8, 16):
                h, t = (r - 8) // 2, r % 2
                ins = A(att_p[:, r, :], bank[2 * t + h % 2][:, (h // 2) * SEQ:(h // 2 + 1) * SEQ], ACT.Exp,
                        bias=stat[:, 4, r:r + 1], scale=HD ** -0.5, accum_out=stat[:, 5, r:r + 1])
            ins.then_inc(s["mem_exp"], 1)
            act.wait_ge(s["moba_pT"], 1)
            for h in range(4):
                ins = A(att_pT[:, h], two[4 + h], ACT.Copy)
            ins.then_inc(s["moba_pT_out"], 1)
            act.wait_ge(s["moba_pv"], 1)
            A(mixT[:, 4:6, :], two[4], ACT.Copy)
            act.wait_ge(s["mem_pv"], 1)
            A(mixT[:, 6:8, :], two[0], ACT.Copy).then_inc(s["mix_heads"], 1)

            root(next(roots))
            turn(4, hT, gain("ffn2"), None)
            swiglu("ffn2", n1, n1)

            for l in range(LAYERS):
                run = l + 1
                root(next(roots))
                turn(5 + 2 * l, hT, lambda k: scol[:, l, 0, k:k + 1], lambda k: modc[:, l, k:k + 1])
                for n in range(2):
                    used(f"proj{n}.{l}")
                    ins = A(hq[:, 2 * n:2 * n + 2, :], two[n], ACT.Silu)
                ins.then_inc(s["hq"], 1)
                for n in range(2):
                    used(f"proj{6 + n}.{l}")
                    ins = A(hgate[:, 2 * n:2 * n + 2, :], two[2 + n], ACT.Silu)
                ins.then_inc(s["hgate"], 1)
                for n in range(2):
                    used(f"proj{2 + n}.{l}")
                    ins = A(hf[:, 2 * n:2 * n + 2, :], two[4 + n], ACT.Sigmoid)
                ins.then_inc(s["hf"], 1)
                for n in range(3):
                    w = min(FB, MISC - n * FB)
                    used(f"misc{n}.{l}")
                    ins = A(misc[:, :, n * FB:n * FB + w], bank[n][:, 0:T * w].rearrange("p (t w) -> p t w", t=T), ACT.Copy)
                ins.then_inc(s["misc"], 1)
                act.wait_ge(s["hf_clamped"], run)
                A(hg[:, :, :], hg[:, :, :], ACT.Ln).then_inc(s["hg"], 1)
                root(next(roots))
                act.wait_ge(s["cT"], run)
                for k in range(5):
                    g_col = col("qn", 3 * l + k) if k < 3 else col("kvn", 2 * l + k - 3)
                    ins = A(cT[:, k, :], bank[k // 2][:, (k % 2) * SEQ:(k % 2 + 1) * SEQ], ACT.Identity, scale=g_col)
                ins.then_inc(s["cT_out"], 1)
                used(f"kv_up.{l}")
                for t in range(T):
                    for half in range(2):
                        src = bank[2 * t + half][:, :].rearrange("p (h c) -> p h c", h=4)
                        A(k96[:, t, 4 * half:4 * half + 4, 0:NOPE], src[:, :, 0:NOPE], ACT.Copy)
                        ins = A(vm[:, t, 4 * half:4 * half + 4, :], src[:, :, NOPE:], ACT.Copy)
                ins.then_inc(s["kv_out"], 1)
                for n, L in enumerate(LEVELS):
                    used(f"gates{n}.{l}")
                    ins = A(G[:, :, n // 4, (n % 4) * FB:(n % 4 + 1) * FB],
                            bank[n % 4][:, :].rearrange("p (t c) -> p t c", t=T), ACT.Tanh, scale=0.5)
                    ins.then_inc(s["gates"], 1)
                    act.wait_ge(s["scans"], 8 * l + n + 1)
                    if n:
                        act.wait_ge(s["hy"], 8 * l + n)
                    m = HGH * SEQ // (2 * L)
                    dst = hf[:, :, :].rearrange("p h s -> p (h s)").rearrange("p (m two c) -> p m two c", two=2, c=L)
                    sf = scan_f[:, :].rearrange("p (m two c) -> p m two c", two=2, c=L)
                    sb_ = scan_b[:, :].rearrange("p (m two c) -> p m two c", two=2, c=L)
                    A(dst[:, :, 1, :], sf[:, :, 1, :], ACT.Exp)
                    A(dst[:, :, 0, :], sb_[:, :, 0, :], ACT.Exp).then_inc(s["decay"], 1)
                root(next(roots))
                act.wait_ge(s["mla_qT"], run)
                for n in range(4):
                    ins = A(qT96[0:DQK, 2 * n:2 * n + 2, :], two[n][0:DQK], ACT.Copy)
                ins.then_inc(s["qT_out"], 1)
                for t in range(T):
                    act.wait_ge(s["mla_max"], T * l + t + 1)
                    for r in range(8 * t, 8 * t + 8):
                        ins = A(mlp_p[:, r, :], mlp_p[:, r, :], ACT.Exp, bias=stat[:, 4, r:r + 1],
                                scale=DQK ** -0.5, accum_out=stat[:, 5, r:r + 1])
                    ins.then_inc(s["mla_exp"], 1)
                act.wait_ge(s["mla_pT"], run)
                for h in range(4):
                    ins = A(mlp_pT[:, h], two[h], ACT.Copy)
                ins.then_inc(s["pT_act"], 1)
                act.wait_ge(s["mla_pv"], run)
                for n in range(2):
                    ins = A(ymT[:, 2 * n:2 * n + 2, :], two[n], ACT.Copy)
                ins.then_inc(s["ymT"], 1)
                act.wait_ge(s["mergedT"], run)
                for k in range(KC // 2):
                    ins = A(hT[:, k, :], bank[4 + k // 2][:, (k % 2) * SEQ:(k % 2 + 1) * SEQ], ACT.Copy)
                ins.then_inc(s["mT_act"], 1)
                root(next(roots))
                turn(6 + 2 * l, hT, lambda k: scol[:, l, 1, k:k + 1], lambda k: modc[:, l, 24 + k:25 + k])
                act.wait_ge(s["logits"], run)
                A(rt[:, 0, :], bank[0][:, 0:T * NE], ACT.Sigmoid).then_inc(s["scores"], 1)
                act.wait_ge(s["combine_bc"], run)
                for n in range(4):
                    ins = A(cb[:, 2 * n:2 * n + 2, :], two[n], ACT.Copy)
                ins.then_inc(s["cb_act"], 1)
                nm = NE * DE // FB
                swiglu(f"moe.{l}", nm, 2 * n1 + nm * l)
            root(next(roots))

        @block.tensor
        def _(pe):
            mm, tr = pe.matmul, pe.transpose

            def landed(pos, i=0):
                pe.wait_ge(ring_full[pos % RING], 16 * i + 16 * (pos // RING + 1))

            def turn(run):
                pe.wait_ge(s["xn"], run)
                for k in range(KC):
                    for t in range(T):
                        ins = tr(bank[4 + k // 2][:, (k % 2) * SEQ + t * P:(k % 2) * SEQ + (t + 1) * P],
                                 xn[:, t, k * P:(k + 1) * P], ident[:, :])
                ins.then_inc(s["xnT"], 1)

            def have_hT(run):
                pe.wait_ge(s["hT_act"], run)
                pe.wait_ge(s["hT_dve"], run)

            def by_feature(name, out):
                pos = place[name]
                landed(pos)
                w = slot_view(pos, FB)
                for j in range(2):
                    for k in range(KC):
                        ins = mm(out[:, j * SEQ:(j + 1) * SEQ], w[:, k, j * P:(j + 1) * P], hT[:, k, :],
                                 start=k == 0, stop=k == KC - 1)
                ins.then_inc(tiles_used, 1)

            def by_token(name, out, lhs=None, n=FB):
                lhs = hT if lhs is None else lhs
                pos = place[name]
                landed(pos)
                w = slot_view(pos, n)
                for t in range(T):
                    for k in range(KC):
                        ins = mm(out[:, t * n:(t + 1) * n], lhs[:, k, t * P:(t + 1) * P], w[:, k, :],
                                 start=k == 0, stop=k == KC - 1)
                ins.then_inc(tiles_used, 1)

            def rows_product(pos, lhs, out, start, stop, i=0):
                landed(pos, i)
                w = slot_view(pos, 1024)
                for kk in range(2):
                    for t in range(T):
                        for half in range(2):
                            ins = mm(out[2 * t + half][:, :], lhs[:, kk, t * P:(t + 1) * P],
                                     w[:, kk, half * 512:(half + 1) * 512],
                                     start=start and kk == 0, stop=stop and kk == 1)
                ins.then_inc(tiles_used, 1)

            def swiglu(name, n, base):
                pos = place[name]

                def first(i, c, late=True):
                    j, p = 2 * i + c, c % 2
                    if late:
                        pe.wait_ge(s["hidden"], j + (base - 1))
                    for b in range(2):
                        at = pos + (0 if c == 0 else 3 * c - 1) + b
                        landed(at, i)
                        w = slot_view(at, FB)
                        for jj in range(2):
                            for k in range(KC):
                                ins = mm(bank[4 + 2 * p + b][:, jj * SEQ:(jj + 1) * SEQ], w[:, k, jj * P:(jj + 1) * P],
                                         hT[:, k, :], start=k == 0, stop=k == KC - 1)
                        ins.then_inc(tiles_used, 1)

                def second(i, c, at, start=False, stop=False):
                    pe.wait_ge(s["hidden"], 2 * i + (c + base + 1))
                    h = small_b[:, c % 2, :].rearrange("p (k s) -> p k s", k=2)
                    rows_product(pos + at, h, acc, start, stop, i)

                j0, turns = loop_shape(n)
                first(0, 0, base >= 2)
                for c in range(1, j0):
                    first(0, c, base + c >= 2)
                    second(0, c - 1, 3 * (c - 1) + 4, start=c == 1)
                with pe.Fori(0, turns) as i:
                    for c in (j0, j0 + 1):
                        first(i, c)
                        second(i, c - 1, 3 * (c - 1) + 4)
                second(0, n - 1, 3 * n - 1, stop=True)

            def ada_columns(l):
                pe.wait_ge(s["ada_chain"], 4 * ADA_SLABS * (l + 1))
                for c in range(48):
                    ins = mm(bank[4][:, c:c + 1], ada_acc[:, c // 2, (c % 2) * P:(c % 2 + 1) * P], ones[:, 0:1],
                             start=True, stop=True)
                ins.then_inc(s["ada_sum"], 1)

            def gate_rows(run):
                pe.wait_ge(s["diag"], run)
                for half in range(2):
                    ins = mm(bank[4 + half][:, :], ones[:, :], diag[:, 4 * half:4 * half + 4, :], start=True, stop=True)
                ins.then_inc(s["gate_bc"], 1)

            pe.wait_ge(s["ident"], 1)
            pe.wait_ge(s["rows_in"], 16 * N_ROW_DMA)
            for t in range(2):
                tr(bank[0][:, t * P:(t + 1) * P], prow[:, t, :], ident[:, :])
            for l in range(LAYERS):
                ins = tr(bank[1][:, l * 48:(l + 1) * 48], abrow[0:48, l, :], ident[0:48, 0:48])
            ins.then_inc(s["prowT"], 1)
            turn(1)
            have_hT(1)
            pe.wait_ge(s["pcol"], 1)
            n1 = DFF // FB
            swiglu("ffn1", n1, 0)
            pe.wait_ge(s["ones"], 1)
            pe.wait_ge(s["x"], 1)
            ada_columns(0)
            pe.wait_ge(s["mod"], 1)
            turn(2)
            have_hT(2)
            by_token("mem_kv0", bank[0], memT)
            by_token("mem_kv1", bank[1], memT)
            turn(3)
            have_hT(3)
            by_feature("w_in0", bank[2])
            by_feature("w_in1", bank[3])
            by_feature("w_in2", bank[4])
            by_feature("w_in3", bank[5])
            by_token("w_in4", bank[6])
            by_token("w_in5", bank[7])
            pe.wait_ge(s["mem_k"], 1)
            by_token("w_in6", bank[0])
            pe.wait_ge(s["mem_v"], 1)
            by_token("w_in7", bank[1])
            pe.wait_ge(s["lru_w_in"], 16 * 4)
            pe.wait_ge(s["lru_xb"], 1)
            pe.wait_ge(s["xl"], 1)
            pe.wait_ge(s["gelu"], 1)
            for g in range(2):
                for c in range(LC):
                    ins = mm(bank[2 + 2 * g + c // 2][:, (c % 2) * SEQ:(c % 2 + 1) * SEQ], lru_w_all[:, g, c, :],
                             xb[:, c, :], start=True, stop=True)
            ins.then_inc(s["lru_gates"], 1)
            pe.wait_ge(s["qkn"], 1)
            pe.wait_ge(s["moba_v"], 1)
            pe.wait_ge(s["lru_ri"], 1)
            rows_ = xn[:, :, :].rearrange("p t d -> p (t d)")
            for w in range(4):
                for pair in range(2):
                    for t in range(T):
                        ins = tr(bank[w][:, pair * SEQ + t * P:pair * SEQ + (t + 1) * P],
                                 rows_[:, w * 512 + t * 256 + pair * P:w * 512 + t * 256 + (pair + 1) * P], ident[:, :])
            ins.then_inc(s["qkT"], 1)
            pe.wait_ge(s["qk_act"], 1)
            pe.wait_ge(s["qk_dve"], 1)
            for att in range(2):
                for t in range(T):
                    for par in range(2):
                        out = bank[4 - 4 * att + 2 * t + par]
                        for pair in range(2):
                            ins = mm(out[:, pair * SEQ:(pair + 1) * SEQ],
                                     qkT[par * HD:(par + 1) * HD, 2 * att, pair, t * P:(t + 1) * P],
                                     qkT[par * HD:(par + 1) * HD, 2 * att + 1, pair, :], start=True, stop=True)
                ins.then_inc(s["att_s"], 1)
            for att, name in ((0, "moba"), (1, "mem")):
                pe.wait_ge(s[name + "_p"], 1)
                for h in range(4):
                    for t in range(T):
                        for kb in range(T):
                            ins = tr(bank[4 - 4 * att + h][:, kb * SEQ + t * P:kb * SEQ + (t + 1) * P],
                                     att_p[:, att * 8 + 2 * h + t, kb * P:(kb + 1) * P], ident[:, :])
                ins.then_inc(s[name + "_pT"], 1)
            for att, name in ((0, "moba"), (1, "mem")):
                pe.wait_ge(s[name + "_pT_out"], 1)
                for h in range(4):
                    for kb in range(T):
                        o = (h % 2) * HD
                        ins = mm(bank[4 - 4 * att][o:o + HD, (h // 2) * SEQ:(h // 2 + 1) * SEQ],
                                 v2[:, att, kb, h * HD:(h + 1) * HD], att_pT[:, att * 4 + h, kb, :],
                                 start=kb == 0, stop=kb == T - 1)
                ins.then_inc(s[name + "_pv"], 1)
            pe.wait_ge(s["mix_heads"], 1)
            pe.wait_ge(s["mix_lru"], 1)
            for n in range(4):
                rows_product(place[f"w_out{n}"], mixT[:, 2 * n:2 * n + 2, :], acc, n == 0, n == 3)
            turn(4)
            have_hT(4)
            swiglu("ffn2", n1, n1)
            pe.wait_ge(s["x"], 3)
            ada_columns(1)
            pe.wait_ge(s["mod"], 2)

            for l in range(LAYERS):
                run = l + 1
                turn(5 + 2 * l)
                have_hT(5 + 2 * l)
                by_feature(f"proj0.{l}", bank[0])
                by_feature(f"proj1.{l}", bank[1])
                by_feature(f"proj6.{l}", bank[2])
                by_feature(f"proj7.{l}", bank[3])
                by_feature(f"proj2.{l}", bank[4])
                by_feature(f"proj3.{l}", bank[5])
                by_token(f"proj4.{l}", bank[6])
                by_token(f"proj5.{l}", bank[7])
                pe.wait_ge(s["hq"], run)
                by_token(f"misc0.{l}", bank[0])
                by_token(f"misc1.{l}", bank[1])
                pe.wait_ge(s["hgate"], run)
                by_token(f"misc2.{l}", bank[2], n=MISC - 2 * FB)
                pe.wait_ge(s["latents"], run)
                for k in range(5):
                    for t in range(T):
                        ins = tr(bank[k // 2][:, (k % 2) * SEQ + t * P:(k % 2) * SEQ + (t + 1) * P],
                                 misc[:, t, k * P:(k + 1) * P], ident[:, :])
                ins.then_inc(s["cT"], 1)
                pe.wait_ge(s["cT_out"], run)
                pe.wait_ge(s["hf"], run)
                pe.wait_ge(s["vh"], run)
                for n in range(2):
                    pos = place[f"q_up{n}.{l}"]
                    landed(pos)
                    w = slot_view(pos, 3 * QL)
                    for t in range(T):
                        for k in range(3):
                            ins = mm(bank[4 + 2 * n + t][:, 0:QL], cT[:, k, t * P:(t + 1) * P], w[:, k, :],
                                     start=k == 0, stop=k == 2)
                    ins.then_inc(tiles_used, 1)
                pos = place[f"kv_up.{l}"]
                rows_product(pos, cT[:, 3:5, :], bank[0:4], True, True)
                pe.wait_ge(s["kv_out"], run)
                pe.wait_ge(s["q_out"], run)
                for n in range(9):
                    if n < 8:
                        if n >= 4:
                            pe.wait_ge(s["gates"], 8 * l + n - 3)
                        by_token(f"gates{n}.{l}", bank[n % 4])
                    if n == 0:
                        pe.wait_ge(s["hk"], run)
                        pe.wait_ge(s["hq"], run)
                        for t in range(T):
                            for h in range(HGH):
                                ins = mm(bank[4 + t][:, h * P:(h + 1) * P], hk[:, h, t * P:(t + 1) * P],
                                         hq[:, h, t * P:(t + 1) * P], start=True, stop=True)
                        ins.then_inc(s["level"], 1)
                        continue
                    pe.wait_ge(s["hy"], 8 * l + n)
                    y = hy[:, :].rearrange("p (h s) -> p h s", h=HGH)
                    if n < 8:
                        if n >= 2:
                            pe.wait_ge(s["level_added"], 9 * l + n - 1)
                        for t in range(T):
                            for h in range(HGH):
                                ins = mm(bank[4 + 2 * (n % 2) + t][:, h * P:(h + 1) * P], y[:, h, t * P:(t + 1) * P],
                                         y[:, h, t * P:(t + 1) * P], start=True, stop=True)
                    else:
                        pe.wait_ge(s["level_added"], 9 * l + n - 1)
                        for h in range(HGH):
                            ins = mm(bank[4][:, h * P:(h + 1) * P], y[:, h, 0:P], y[:, h, P:SEQ], start=True, stop=True)
                    ins.then_inc(s["level"], 1)
                pe.wait_ge(s["level_added"], 9 * l + 9)
                vh_ = vh[:, :, :].rearrange("p t (h c) -> p t h c", h=HGH)
                for h in range(HGH):
                    mm(bank[6][:, h * P:(h + 1) * P], attT[:, 0, h, :], vh_[:, 0, h, :], start=True, stop=True)
                for h in range(HGH):
                    mm(bank[7][:, h * P:(h + 1) * P], attT[:, 1, h, :], vh_[:, 1, h, :], start=True, stop=False)
                    ins = mm(bank[7][:, h * P:(h + 1) * P], attT[:, 2, h, :], vh_[:, 0, h, :], start=False, stop=True)
                ins.then_inc(s["hg_o"], 1)
                pe.wait_ge(s["gates"], 8 * l + 8)
                pe.wait_ge(s["k_rope"], run)
                for src, b0, ev in ((q96, 0, "mla_qT"), (k96, 4, "mla_kT")):
                    if b0:
                        pe.wait_ge(s["oa_rows"], run)
                    for h in range(MH):
                        for t in range(T):
                            ins = tr(bank[b0 + h // 2][0:DQK, (h % 2) * SEQ + t * P:(h % 2) * SEQ + (t + 1) * P],
                                     src[:, t, h, :], ident[:, :])
                    ins.then_inc(s[ev], 1)
                pe.wait_ge(s["qT_out"], run)
                pe.wait_ge(s["kT_out"], run)
                for h in range(HGH):
                    for t in range(T):
                        ins = tr(bank[4 + h // 2][:, (h % 2) * SEQ + t * P:(h % 2) * SEQ + (t + 1) * P],
                                 oa[:, t, h * P:(h + 1) * P], ident[:, :])
                ins.then_inc(s["oaT"], 1)
                for t in range(T):
                    if t:
                        pe.wait_ge(s["mla_max"], T * l + t)
                    for h in range(MH):
                        ins = mm(bank[h // 2][:, (h % 2) * SEQ:(h % 2 + 1) * SEQ], qT96[0:DQK, h, t * P:(t + 1) * P],
                                 kT96[0:DQK, h, :], start=True, stop=True)
                    ins.then_inc(s["mla_s"], 1)
                pe.wait_ge(s["oaT_out"], run)
                pe.wait_ge(s["mla_p"], run)
                for h in range(MH):
                    for t in range(T):
                        for kb in range(T):
                            ins = tr(bank[h][:, kb * SEQ + t * P:kb * SEQ + (t + 1) * P],
                                     mlp_p[:, t * 8 + h, kb * P:(kb + 1) * P], ident[:, :])
                ins.then_inc(s["mla_pT"], 1)
                pe.wait_ge(s["pT_act"], run)
                pe.wait_ge(s["pT_dve"], run)
                for h in range(MH):
                    for kb in range(T):
                        o = (h % 2) * MV
                        ins = mm(bank[h // 4][o:o + MV, (h // 2 % 2) * SEQ:(h // 2 % 2 + 1) * SEQ],
                                 vm[:, kb, h, :], mlp_pT[:, h, kb, :], start=kb == 0, stop=kb == T - 1)
                ins.then_inc(s["mla_pv"], 1)
                for n in range(2):
                    rows_product(place[f"br_a{n}.{l}"], oaT[:, 2 * n:2 * n + 2, :], bank[4:8], n == 0, n == 1)
                pe.wait_ge(s["ymT"], run)
                for n in range(2):
                    rows_product(place[f"br_b{n}.{l}"], ymT[:, 2 * n:2 * n + 2, :], acc, n == 0, n == 1)
                pe.wait_ge(s["merged"], run)
                for k in range(KC):
                    for t in range(T):
                        ins = tr(bank[4 + k // 2][:, (k % 2) * SEQ + t * P:(k % 2) * SEQ + (t + 1) * P],
                                 merged[:, t, k * P:(k + 1) * P], ident[:, :])
                ins.then_inc(s["mergedT"], 1)
                pe.wait_ge(s["mT_act"], run)
                pe.wait_ge(s["mT_dve"], run)
                gate_rows(2 * l + 1)
                for n in range(4):
                    rows_product(place[f"w_out{n}.{l}"], hT[:, 2 * n:2 * n + 2, :], acc, n == 0, n == 3)

                turn(6 + 2 * l)
                have_hT(6 + 2 * l)
                gate_rows(2 * l + 2)
                pe.wait_ge(s["router_in"], 32)
                for t in range(T):
                    for k in range(KC):
                        ins = mm(bank[0][:, t * NE:(t + 1) * NE], hT[:, k, t * P:(t + 1) * P], router[:, k, :],
                                 start=k == 0, stop=k == KC - 1)
                ins.then_inc(s["logits"], 1)
                pe.wait_ge(s["combine"], run)
                for t in range(T):
                    ins = tr(bank[1][0:NE, t * P:(t + 1) * P], rt[:, 15, t * NE:(t + 1) * NE], ident[:, :])
                ins.then_inc(s["combineT"], 1)
                pe.wait_ge(s["combT"], run)
                pe.wait_ge(s["sel"], run)
                pe.wait_ge(s["gbc"], 2 * l + 2)
                for e in range(NE):
                    ins = mm(bank[e // 2][:, (e % 2) * SEQ:(e % 2 + 1) * SEQ], sel[0:NE, e, :], combT[:, :],
                             start=True, stop=True)
                ins.then_inc(s["combine_bc"], 1)
                pe.wait_ge(s["cb_act"], run)
                pe.wait_ge(s["cb_dve"], run)
                nm = NE * DE // FB
                swiglu(f"moe.{l}", nm, 2 * n1 + nm * l)

        @block.vector
        def _(v):
            done = [0]

            def link(ins):
                done[0] += 1
                ins.then_inc(s["dve_chain"], 1)
                v.wait_ge(s["dve_chain"], done[0])

            ts, tt, stt, cp = v.tensor_scalar, v.tensor_tensor, v.scalar_tensor_tensor, v.tensor_copy
            M, AD = ALU.mult, ALU.add

            def used(name):
                v.wait_ge(tiles_used, place[name] + 1)

            roots = [0]

            def inverse_root(n, width):
                roots[0] += 1
                ts(stat[:, 1, 0:n], stat[:, 0, 0:n], 1.0 / width, EPS, M, AD).then_inc(s["ms"], 1)
                v.wait_ge(s["root"], roots[0])
                link(v.reciprocal(stat[:, 3, 0:n], stat[:, 2, 0:n]))
                link(tt(stat[:, 6, 0:n], stat[:, 3, 0:n], stat[:, 3, 0:n], M))
                link(tt(stat[:, 6, 0:n], stat[:, 6, 0:n], stat[:, 1, 0:n], M))
                link(ts(stat[:, 6, 0:n], stat[:, 6, 0:n], -0.5, 1.5, M, AD))
                link(tt(stat[:, 3, 0:n], stat[:, 3, 0:n], stat[:, 6, 0:n], M))

            def normalise(src, dst):
                for t in range(T):
                    ins = v.tensor_tensor_reduce(dst[:, t, :], src[:, t, :], src[:, t, :], 1.0, 0.0, M, AD,
                                                 stat[:, 0, t:t + 1])
                link(ins)
                inverse_root(T, D)
                for t in range(T):
                    ins = ts(dst[:, t, :], src[:, t, :], stat[:, 3, t:t + 1], None, M)
                return ins

            def turn(run, dst, scale, bias):
                v.wait_ge(s["xnT"], run)
                for k in range(KC // 2, KC):
                    src = bank[4 + k // 2][:, (k % 2) * SEQ:(k % 2 + 1) * SEQ]
                    if bias:
                        ins = ts(dst[:, k, :], src, scale(k), bias(k), M, AD)
                    else:
                        ins = ts(dst[:, k, :], src, scale(k), None, M)
                ins.then_inc(s["hT_dve"], 1)

            def gain(name, off=0):
                return lambda k: col(name, off + k)

            def swiglu(name, n, base, weights=None):
                pos = place[name]

                def step(i, c, late=True):
                    j, p = 2 * i + c, c % 2
                    v.wait_ge(s["silu"], j + (base + 1))
                    v.wait_ge(tiles_used, RING * i + (pos + (0 if c == 0 else 3 * c - 1) + 2))
                    if late:
                        v.wait_ge(tiles_used, RING * i + (pos + 3 * (c - 2) + 4 + 1))
                    if weights is None:
                        tt(small_b[:, p, :], small_a[:, p, :], bank[5 + 2 * p][:, :], M).then_inc(s["hidden"], 1)
                    else:
                        tt(ep[:, p, :], small_a[:, p, :], bank[5 + 2 * p][:, :], M).then_inc(s["unweighted"], 1)
                        v.wait_ge(s["unweighted"], j + (weights + 1))
                        e = cb[:, bass.ds(i + c // 2, 1), :].broadcast_to([P, 2, SEQ])
                        tt(small_b[:, p, :].rearrange("p (k s) -> p k s", k=2),
                           ep[:, p, :].rearrange("p (k s) -> p k s", k=2), e, M).then_inc(s["hidden"], 1)

                j0, turns = loop_shape(n)
                for c in range(j0):
                    step(0, c, c >= 2)
                with v.Fori(0, turns) as i:
                    step(i, j0)
                    step(i, j0 + 1)
                v.wait_ge(tiles_used, pos + 3 * n)

            def add_to_x(scale):
                for t in range(T):
                    for half in range(2):
                        xs = x[:, t, half * 512:(half + 1) * 512]
                        ins = stt(xs, acc[2 * t + half][:, :], scale, xs, M, AD)
                ins.then_inc(s["x"], 1)

            def add_gated_to_x():
                for t in range(T):
                    for half in range(2):
                        ins = tt(xn[:, t, half * 512:(half + 1) * 512], acc[2 * t + half][:, :],
                                 gbc[:, half * 512:(half + 1) * 512], M)
                link(ins)
                tt(x[:, :, :], x[:, :, :], xn[:, :, :], AD).then_inc(s["x"], 1)

            def modulation(l):
                v.wait_ge(s["ada_sum"], l + 1)
                link(tt(modc[:, l, :], bank[4][:, 0:48], abcol[:, l, :], AD))
                stt(scol[:, l, 0, :], modc[:, l, 8:16], 1.0, col("n1", 8 * l, 8), AD, M)
                stt(scol[:, l, 1, :], modc[:, l, 32:40], 1.0, col("n2", 8 * l, 8), AD, M).then_inc(s["mod"], 1)
                v.wait_ge(s["mod"], l + 1)

            def gate_diag(l, c0):
                tt(diag[:, :, :], ident[:, :].unsqueeze(1).broadcast_to([P, KC, P]),
                   modc[:, l, c0:c0 + KC].unsqueeze(2).broadcast_to([P, KC, P]), M).then_inc(s["diag"], 1)

            def gate_copy(run, scale):
                v.wait_ge(s["gate_bc"], run)
                for half in range(2):
                    ins = ts(gbc[:, half * 512:(half + 1) * 512], bank[4 + half][:, :], scale, None, M)
                ins.then_inc(s["gbc"], 1)

            def negative_max(src, r0, n, scale):
                link(v.tensor_reduce(stat[:, 7, r0:r0 + n], src, AX.X, ALU.max))
                return ts(stat[:, 4, r0:r0 + n], stat[:, 7, r0:r0 + n], -scale, None, M)

            link(v.memset(stat[:, :, :], 1.0))
            v.memset(ones[:, :], 1.0).then_inc(s["ones"], 1)
            v.memset(prow[:, :, :], 0.0).then_inc(s["prow_zero"], 1)
            v.memset(lru_w_all[:, :, :, :], 0.0).then_inc(s["lru_w_zero"], 1)
            v.wait_ge(s["x_in"], 16)
            normalise(x, xn).then_inc(s["xn"], 1)
            v.wait_ge(s["prowT"], 1)
            cp(pcol[:, :, :].rearrange("p a b -> p (a b)"), bank[0][:, 0:2 * P])
            cp(abcol[:, :, :].rearrange("p a b -> p (a b)"), bank[1][:, 0:LAYERS * 48]).then_inc(s["pcol"], 1)
            v.wait_ge(s["pcol"], 1)
            l0, l1 = col("lb", 0, 4), col("lb", 4, 4)
            link(tt(lbc[:, 4, :], l0, l1, ALU.max))
            tt(lbc[:, 0, :], l0, lbc[:, 4, :], ALU.subtract)
            tt(lbc[:, 1, :], l1, lbc[:, 4, :], ALU.subtract)
            link(ts(lruc[:, 0, :], col("lam", 0, 4), -1.0, None, M))
            tt(lruc[:, 1, :], lruc[:, 0, :], col("lam", 0, 4), ALU.max).then_inc(s["small_in"], 1)
            v.wait_ge(s["inv_freq"], 1)
            v.wait_ge(s["pos_in"], 16)
            link(cp(stat[:, 7, 0:T], pos_i[:, :]))
            for t in range(T):
                ins = ts(rope_t[:, 1, t, :], rope_t[:, 0, 0, :], stat[:, 7, t:t + 1], None, M)
            link(ins)
            two_pi = 2 * np.pi
            c1 = 6.28125
            c2 = np.floor((two_pi - c1) * 2 ** 21) / 2 ** 21
            c3 = two_pi - c1 - c2
            for n, quarter in ((0, 0.25), (1, 0.0)):
                link(ts(rope_t[:, 2], rope_t[:, 1], 1 / two_pi, quarter, M, AD))
                link(cp(rope_t[:, 3].bitcast(I32), rope_t[:, 2]))
                link(cp(rope_t[:, 2], rope_t[:, 3].bitcast(I32)))
                link(stt(rope_t[:, 4], rope_t[:, 2], -c1, rope_t[:, 1], M, AD))
                link(stt(rope_t[:, 5], rope_t[:, 2], -c2, rope_t[:, 4], M, AD))
                link(stt(rope_t[:, 6], rope_t[:, 2], -c3, rope_t[:, 5], M, AD))
                link(ts(rope_t[:, 7], rope_t[:, 6], quarter * two_pi, 3.1415925, AD, ALU.min))
                link(ts(rope_t[:, 8 + n], rope_t[:, 7], -3.1415925, None, ALU.max))
            cp(stat[:, 6, 0:1], stat[:, 7, 0:1]).then_inc(s["angles"], 1)
            v.wait_ge(s["small_exp"], 1)
            link(tt(lbc[:, 4, :], lbc[:, 2, :], lbc[:, 3, :], AD))
            link(v.reciprocal(lbc[:, 4, :], lbc[:, 4, :]))
            tt(lbc[:, 2, :], lbc[:, 2, :], lbc[:, 4, :], M)
            link(tt(lbc[:, 3, :], lbc[:, 3, :], lbc[:, 4, :], M))
            link(tt(lbc[:, 5, :], lbc[:, 2, :], lbc[:, 3, :], AD))
            tt(lbc[:, 0, :], lbc[:, 2, :], lbc[:, 2, :], ALU.subtract)
            link(tt(lbc[:, 1, :], lbc[:, 5, :], lbc[:, 2, :], ALU.subtract))
            for l in range(LAYERS):
                link(ts(lbc[:, 6 + l, :], lbc[:, l, :], -1.0, 1.0, M, AD))
            link(ts(lruc[:, 3, :], lruc[:, 2, :], 2.0, None, AD))
            link(v.reciprocal(lruc[:, 3, :], lruc[:, 3, :]))
            link(tt(lruc[:, 3, :], lruc[:, 2, :], lruc[:, 3, :], M))
            link(tt(lruc[:, 4, :], lruc[:, 3, :], lruc[:, 3, :], M))
            link(ts(lruc[:, 5, :], lruc[:, 4, :], 1.0 / 21, None, M))
            for n in range(19, 2, -2):
                link(stt(lruc[:, 5, :], lruc[:, 5, :], 1.0 / n, lruc[:, 4, :], AD, M))
            link(stt(lruc[:, 6, :], lruc[:, 5, :], 1.0, lruc[:, 3, :], AD, M))
            link(ts(lruc[:, 7, :], lruc[:, 0, :], 0.0, None, ALU.max))
            link(stt(lruc[:, 5, :], lruc[:, 6, :], 2.0, lruc[:, 7, :], M, AD))
            ts(lruc[:, 8, :], lruc[:, 5, :], -LRU_C, None, M)
            link(ts(lruc[:, 9, :], lruc[:, 5, :], LRU_C, None, M))
            turn(1, hT, gain("ffn1"), None)
            v.wait_ge(s["patterns"], 1)
            v.wait_ge(s["ident"], 1)
            scale = DK ** -0.5
            ts(rank[:, :], iot[:, 1, 0:NE], -1.0, float(NE), M, AD)
            link(tt(iot[:, 2, :], iot[:, 0, :], iot[:, 1, :], ALU.bitwise_xor))
            link(tt(diag[:, 0, :], iot[:, 1, :], iot[:, 0, :], ALU.is_gt))
            for n, L in enumerate(LEVELS[:-1]):
                link(ts(diag[:, 1, :], iot[:, 2, :], float(L), scale, ALU.is_ge, M))
                link(stt(diag[:, 2, :], iot[:, 2, :], float(2 * L), diag[:, 1, :], ALU.is_lt, M))
                link(tt(level_mask[:, n, :], diag[:, 2, :], diag[:, 0, :], M))
            link(ts(level_mask[:, 7, :], ident[:, :], scale, None, M))
            idx, low = view(22000, 1028).bitcast(I32), view(23100, 1028).bitcast(I32)
            for n, L in enumerate(LEVELS):
                link(ts(low, idx, L - 1, None, ALU.bitwise_and))
                link(ts(seg[:, n, :], low, 0.0, None, ALU.is_gt))
            v.wait_ge(s["mem_in"], 16)
            v.wait_ge(s["xnT"], 1)
            normalise(memx, xn).then_inc(s["xn"], 1)

            n1 = DFF // FB
            swiglu("ffn1", n1, 0)
            add_to_x(0.5)
            v.wait_ge(s["x"], 1)
            modulation(0)
            turn(2, memT, gain("mem"), None)
            normalise(x, xn).then_inc(s["xn"], 1)
            used("mem_kv0")
            cp(qk4[:, 3, :], bank[0][:, :]).then_inc(s["mem_k"], 1)
            turn(3, hT, gain("mix"), None)
            used("mem_kv1")
            v.memset(xl[:, :, 0:3], 0.0).then_inc(s["xl_zero"], 1)
            v.wait_ge(s["xl"], 1)
            for j in range(4):
                for c in range(LC):
                    w = col("convw", 4 * j + c)
                    if j == 0:
                        ins = ts(xb[:, c, :], xl[:, c, 0:SEQ], w, col("convb", c), M, AD)
                    else:
                        ins = stt(xb[:, c, :], xl[:, c, j:j + SEQ], w, xb[:, c, :], M, AD)
                if j < 3:
                    link(ins)
            ins.then_inc(s["lru_xb"], 1)
            used("w_in4")
            cp(qk4[:, 0, :], bank[6][:, :])
            used("w_in5")
            cp(qk4[:, 1, :], bank[7][:, :])
            used("w_in7")
            link(cp(qk4[:, 2, :], bank[1][:, :]))
            rows_ = xn[:, :, :].rearrange("p t d -> p (t d)")
            qk_flat = qk4[:, :, :].rearrange("p w c -> p (w c)")
            link(tt(rows_, qk_flat, qk_flat, M))
            link(v.tensor_reduce(stat[:, 0, 0:32], rows_.rearrange("p (r c) -> p r c", c=HD), AX.X, AD))
            inverse_root(32, HD)
            tt(rows_.rearrange("p (r c) -> p r c", c=HD), qk_flat.rearrange("p (r c) -> p r c", c=HD),
               stat[:, 3, 0:32].unsqueeze(2).broadcast_to([P, 32, HD]), M).then_inc(s["qkn"], 1)
            v.wait_ge(s["lru_a"], 1)
            sc = small_a[:, :, :].rearrange("p a b -> p (a b)")
            lt_flat = lt[:, :, :].rearrange("p c s -> p (c s)")
            link(ts(sc, lt_flat, 1.0, None, AD))
            link(v.reciprocal(sc, sc))
            link(tt(sc, sc, lt_flat, M))
            ts(lt_flat, sc, 1.0e-30, None, ALU.max).then_inc(s["lru_m2"], 1)
            v.wait_ge(s["qkT"], 1)
            for w in range(2, 4):
                ins = ts(qkT[:, w].rearrange("p a b -> p (a b)"), bank[w][:, :], col("heads", w), None, M)
            ins.then_inc(s["qk_dve"], 1)
            v.wait_ge(s["att_s"], 1)
            for h in range(4):
                slope = 2.0 ** (-8.0 * (h + 1) / 4)
                for t in range(T):
                    ins = stt(att_p[:, 2 * h + t, :], dist[:, t, :], -slope / HD ** -0.5,
                              bank[4 + 2 * t + h % 2][:, (h // 2) * SEQ:(h // 2 + 1) * SEQ], M, AD)
            link(ins)
            negative_max(att_p[:, 0:8, :], 0, 8, HD ** -0.5).then_inc(s["moba_max"], 1)
            v.wait_ge(s["att_s"], 2)
            for t in range(T):
                for par in range(2):
                    for pair in range(2):
                        h = 2 * pair + par
                        ins = v.tensor_reduce(stat[:, 7, 8 + 2 * h + t:9 + 2 * h + t],
                                              bank[2 * t + par][:, pair * SEQ:(pair + 1) * SEQ], AX.X, ALU.max)
            link(ins)
            ts(stat[:, 4, 8:16], stat[:, 7, 8:16], -HD ** -0.5, None, M).then_inc(s["mem_max"], 1)
            v.wait_ge(s["lru_mult"], 1)
            v.memset(lt[:, :, 0:1], 1.0)
            v.memset(lt2[:, :, 0:1], 0.0)
            link(tt(li[:, :, :], li[:, :, :], xb[:, :, :], M))
            link(tt(li[:, :, :], li[:, :, :], lt[:, :, :], M))
            link(v.tensor_tensor_scan(lt_flat, lt2[:, :, :].rearrange("p c s -> p (c s)"),
                                      li[:, :, :].rearrange("p c s -> p (c s)"), 0.0, M, AD))
            tt(mixT[:, 0:4, :], lt[:, :, :], gel[:, :, :], M).then_inc(s["mix_lru"], 1)
            for att, name in ((0, "moba"), (1, "mem")):
                v.wait_ge(s[name + "_exp"], 1)
                link(v.reciprocal(stat[:, 6, 8 * att:8 * att + 8], stat[:, 5, 8 * att:8 * att + 8]))
                for r in range(8 * att, 8 * att + 8):
                    ins = ts(att_p[:, r, :], att_p[:, r, :], stat[:, 6, r:r + 1], None, M)
                ins.then_inc(s[name + "_p"], 1)
            v.wait_ge(s["mem_pT"], 1)
            for h in range(4):
                ins = cp(att_pT[:, 4 + h].rearrange("p a b -> p (a b)"), bank[h][:, :])
            ins.then_inc(s["mem_pT_out"], 1)
            used("w_out3")
            add_to_x(1.0)
            v.wait_ge(s["x"], 2)
            normalise(x, xn).then_inc(s["xn"], 1)
            turn(4, hT, gain("ffn2"), None)
            swiglu("ffn2", n1, n1)
            add_to_x(0.5)
            v.wait_ge(s["x"], 3)
            modulation(1)

            for l in range(LAYERS):
                run = l + 1
                normalise(x, xn).then_inc(s["xn"], 1)
                turn(5 + 2 * l, hT, lambda k: scol[:, l, 0, k:k + 1], lambda k: modc[:, l, k:k + 1])
                v.wait_ge(s["hf"], run)
                for h in range(HGH):
                    ins = ts(hf[:, h, :], hf[:, h, :], lbc[:, 6 + l, h:h + 1], lbc[:, l, h:h + 1], M, AD)
                link(ins)
                ts(hg[:, :, :], hf[:, :, :], 1.0e-19, None, ALU.max).then_inc(s["hf_clamped"], 1)
                ts(hk[:, :, :], hf[:, :, :], -1.0, 1.0, M, AD).then_inc(s["hk"], 1)
                for n in range(2):
                    used(f"proj{4 + n}.{l}")
                    ins = cp(vh[:, :, n * FB:(n + 1) * FB], bank[6 + n][:, :].rearrange("p (t c) -> p t c", t=T))
                ins.then_inc(s["vh"], 1)
                v.wait_ge(s["misc"], run)
                for t in range(T):
                    v.tensor_tensor_reduce(scr[:, 0:QL], misc[:, t, 0:QL], misc[:, t, 0:QL], 1.0, 0.0, M, AD,
                                           stat[:, 0, t:t + 1])
                    ins = v.tensor_tensor_reduce(scr[:, QL:QL + KVL], misc[:, t, QL:QL + KVL], misc[:, t, QL:QL + KVL],
                                                 1.0, 0.0, M, AD, stat[:, 0, 2 + t:3 + t])
                    link(ins)
                link(ts(stat[:, 0, 2:4], stat[:, 0, 2:4], QL / KVL, None, M))
                inverse_root(4, QL)
                for t in range(T):
                    ts(misc[:, t, 0:QL], misc[:, t, 0:QL], stat[:, 3, t:t + 1], None, M)
                    ins = ts(misc[:, t, QL:QL + KVL], misc[:, t, QL:QL + KVL], stat[:, 3, 2 + t:3 + t], None, M)
                ins.then_inc(s["latents"], 1)
                v.wait_ge(s["sincos"], 1)
                half = ROPE // 2
                cos, sin = rope_t[:, 10], rope_t[:, 11]
                k1, k2 = misc[:, :, QL + KVL:QL + KVL + half], misc[:, :, QL + KVL + half:MISC]
                tmp = [scr[:, 256 * n:256 * n + 256] for n in range(4)]
                small = [z[:, 0:T * half].rearrange("p (t c) -> p t c", t=T) for z in tmp]
                tt(small[0], k1, cos, M)
                tt(small[1], k2, sin, M)
                tt(small[2], k1, sin, M)
                link(tt(small[3], k2, cos, M))
                tt(small[0], small[0], small[1], ALU.subtract)
                link(tt(small[2], small[2], small[3], AD))
                for t in range(T):
                    cp(k96[:, t, :, NOPE:NOPE + half], small[0][:, t:t + 1, :].broadcast_to([P, MH, half]))
                    ins = cp(k96[:, t, :, NOPE + half:DQK], small[2][:, t:t + 1, :].broadcast_to([P, MH, half]))
                ins.then_inc(s["k_rope"], 1)
                v.wait_ge(s["k_rope"], run)
                for n in range(2):
                    used(f"q_up{n}.{l}")
                    for t in range(T):
                        ins = cp(q96[:, t, 4 * n:4 * n + 4, :].rearrange("p h c -> p (h c)"), bank[4 + 2 * n + t][:, 0:QL])
                link(ins)
                big = [z.rearrange("p (t h c) -> p t h c", t=T, h=MH) for z in tmp]
                for t in range(T):
                    q1, q2 = q96[:, t, :, NOPE:NOPE + half], q96[:, t, :, NOPE + half:DQK]
                    cb_ = cos[:, t:t + 1, :].broadcast_to([P, MH, half])
                    sb_ = sin[:, t:t + 1, :].broadcast_to([P, MH, half])
                    tt(big[0][:, t], q1, cb_, M)
                    tt(big[1][:, t], q2, sb_, M)
                    tt(big[2][:, t], q1, sb_, M)
                    ins = tt(big[3][:, t], q2, cb_, M)
                link(ins)
                for t in range(T):
                    tt(q96[:, t, :, NOPE:NOPE + half], big[0][:, t], big[1][:, t], ALU.subtract)
                    ins = tt(q96[:, t, :, NOPE + half:DQK], big[2][:, t], big[3][:, t], AD)
                ins.then_inc(s["q_out"], 1)
                v.wait_ge(s["hg"], run)
                v.wait_ge(s["hq"], run)
                g_flat = hg[:, :, :].rearrange("p h s -> p (h s)")
                N = HGH * SEQ

                def add_level(n, mask):
                    v.wait_ge(s["level"], 9 * l + n + 1)
                    m = level_mask[:, mask, :].unsqueeze(1).broadcast_to([P, HGH, P])
                    for t in range(T):
                        src = bank[4 + 2 * (n % 2) + t][:, :].rearrange("p (h c) -> p h c", h=HGH)
                        if n == 0:
                            ins = tt(attT[:, t], src, m, M)
                        else:
                            link(tt(prod[:, t], src, m, M))
                            ins = tt(attT[:, t], attT[:, t], prod[:, t], AD)
                    ins.then_inc(s["level_added"], 1)
                    v.wait_ge(s["level_added"], 9 * l + n + 1)

                for n, L in enumerate(LEVELS):
                    if n:
                        v.wait_ge(s["decay"], 8 * l + n)
                    v.tensor_tensor_scan(scan_f[:, :], seg[:, n, 0:N], g_flat, 0.0, M, AD)
                    v.tensor_tensor_scan(scan_b[:, N - 2::-1], g_flat[:, N - 1:0:-1], seg[:, n, N - 1:0:-1], 0.0, AD, M)\
                        .then_inc(s["scans"], 1)
                    if n:
                        v.wait_ge(s["level"], 9 * l + n + 1)
                        add_level(n, n - 1)
                    else:
                        add_level(0, 7)
                    v.wait_ge(s["decay"], 8 * l + n + 1)
                    by = lambda z: z.rearrange("p (m two c) -> p m two c", two=2, c=L)
                    dec = by(hf[:, :, :].rearrange("p h s -> p (h s)"))
                    y = by(hy[:, :])
                    tt(y[:, :, 1, :], dec[:, :, 1, :], by(hq[:, :, :].rearrange("p h s -> p (h s)"))[:, :, 1, :], M)
                    tt(y[:, :, 0, :], dec[:, :, 0, :], by(hk[:, :, :].rearrange("p h s -> p (h s)"))[:, :, 0, :], M)\
                        .then_inc(s["hy"], 1)
                v.wait_ge(s["level"], 9 * l + 9)
                ts(attT[:, 2], bank[4][:, :].rearrange("p (h c) -> p h c", h=HGH), scale, None, M)\
                    .then_inc(s["level_added"], 1)
                v.wait_ge(s["hg_o"], run)
                for t in range(T):
                    ins = cp(oa[:, t, :], bank[6 + t][:, :])
                link(ins)
                sq = oa_sq[:, :]
                oa_flat = oa[:, :, :].rearrange("p t c -> p (t c)")
                link(tt(sq, oa_flat, oa_flat, M))
                link(v.tensor_reduce(stat[:, 0, 0:8], sq.rearrange("p (r c) -> p r c", c=P), AX.X, AD))
                inverse_root(8, DK)
                tt(oa_flat.rearrange("p (r c) -> p r c", c=P), oa_flat.rearrange("p (r c) -> p r c", c=P),
                   stat[:, 3, 0:8].unsqueeze(2).broadcast_to([P, 8, P]), M).then_inc(s["oa_rows"], 1)
                v.wait_ge(s["mla_kT"], run)
                for n in range(4):
                    ins = cp(kT96[0:DQK, 2 * n:2 * n + 2, :].rearrange("p h s -> p (h s)"), bank[4 + n][0:DQK, :])
                ins.then_inc(s["kT_out"], 1)
                v.wait_ge(s["hgate"], run)
                v.wait_ge(s["oaT"], run)
                for h in range(HGH):
                    ins = stt(oaT[:, h, :], bank[4 + h // 2][:, (h % 2) * SEQ:(h % 2 + 1) * SEQ], col("hgn", 4 * l + h),
                              hgate[:, h, :], M, M)
                ins.then_inc(s["oaT_out"], 1)
                for t in range(T):
                    v.wait_ge(s["mla_s"], T * l + t + 1)
                    for n in range(4):
                        ins = tt(mlp_p[:, 8 * t + 2 * n:8 * t + 2 * n + 2, :],
                                 bank[n][:, :].rearrange("p (h c) -> p h c", h=2),
                                 mla_mask[:, t:t + 1, :].broadcast_to([P, 2, SEQ]), AD)
                    link(ins)
                    negative_max(mlp_p[:, 8 * t:8 * t + 8, :], 8 * t, 8, DQK ** -0.5).then_inc(s["mla_max"], 1)
                v.wait_ge(s["mla_exp"], T * (l + 1))
                link(v.reciprocal(stat[:, 6, 0:16], stat[:, 5, 0:16]))
                for r in range(16):
                    ins = ts(mlp_p[:, r, :], mlp_p[:, r, :], stat[:, 6, r:r + 1], None, M)
                ins.then_inc(s["mla_p"], 1)
                v.wait_ge(s["mla_pT"], run)
                for h in range(4, MH):
                    ins = cp(mlp_pT[:, h].rearrange("p a b -> p (a b)"), bank[h][:, :])
                ins.then_inc(s["pT_dve"], 1)
                used(f"br_a1.{l}")
                for t in range(T):
                    for half_ in range(2):
                        c = slice(half_ * 512, half_ * 512 + 512)
                        ins = stt(merged[:, t, c], G[:, t, 0, c], 1.0, bank[4 + 2 * t + half_][:, :], AD, M)
                link(ins)
                used(f"br_b1.{l}")
                for t in range(T):
                    for half_ in range(2):
                        c = slice(half_ * 512, half_ * 512 + 512)
                        ins = stt(xn[:, t, c], G[:, t, 1, c], 1.0, acc[2 * t + half_][:, :], AD, M)
                link(ins)
                tt(merged[:, :, :], merged[:, :, :], xn[:, :, :], AD).then_inc(s["merged"], 1)
                gate_diag(l, 16)
                v.wait_ge(s["mergedT"], run)
                for k in range(KC // 2, KC):
                    ins = cp(hT[:, k, :], bank[4 + k // 2][:, (k % 2) * SEQ:(k % 2 + 1) * SEQ])
                ins.then_inc(s["mT_dve"], 1)
                gate_copy(2 * l + 1, 0.5)
                used(f"w_out3.{l}")
                v.wait_ge(s["gbc"], 2 * l + 1)
                add_gated_to_x()
                v.wait_ge(s["x"], 4 + 2 * l)

                normalise(x, xn).then_inc(s["xn"], 1)
                gate_diag(l, 40)
                cp(sel[0:NE, :, :], ident[0:NE, 0:NE].unsqueeze(2).broadcast_to([NE, NE, P])).then_inc(s["sel"], 1)
                turn(6 + 2 * l, hT, lambda k: scol[:, l, 1, k:k + 1], lambda k: modc[:, l, 24 + k:25 + k])
                gate_copy(2 * l + 2, 1.0)
                v.wait_ge(s["scores"], run)

                def r(n):
                    return rt[:, n, :].rearrange("p (t e) -> p t e", t=T)

                def rg(n):
                    return rt[:, n, :].rearrange("p (g e) -> p g e", e=EPG)

                link(tt(r(1), r(0), rbias[:, :].unsqueeze(1).broadcast_to([P, T, NE]), AD))
                b_ = rg(1)
                p6 = rt[:, 2:4, :].rearrange("p a b -> p (a b)")[:, 0:6 * T * NG].rearrange("p (g k) -> p g k", k=6)
                tt(p6[:, :, 0:2], b_[:, :, 0:2], b_[:, :, 2:4], AD)
                tt(p6[:, :, 2:3], b_[:, :, 0:1], b_[:, :, 1:2], AD)
                tt(p6[:, :, 3:4], b_[:, :, 2:3], b_[:, :, 3:4], AD)
                tt(p6[:, :, 4:5], b_[:, :, 0:1], b_[:, :, 3:4], AD)
                link(tt(p6[:, :, 5:6], b_[:, :, 1:2], b_[:, :, 2:3], AD))
                gs = rt[:, 4, 0:T * NG].rearrange("p (t g) -> p t g", t=T)
                link(v.tensor_reduce(rt[:, 4, 0:T * NG], p6, AX.X, ALU.max))

                def first_best(scores_, n, rank, mx, out_, eq):
                    link(v.tensor_reduce(mx, scores_, AX.X, ALU.max))
                    link(tt(eq, scores_, mx.unsqueeze(2).broadcast_to([P, T, n]), ALU.is_equal))
                    link(tt(eq, eq, rank.unsqueeze(1).broadcast_to([P, T, n]), M))
                    link(v.tensor_reduce(mx, eq, AX.X, ALU.max))
                    link(tt(out_, eq, mx.unsqueeze(2).broadcast_to([P, T, n]), ALU.is_equal))

                mx = rt[:, 6, 0:T]
                gsel = rt[:, 7, 0:T * NG].rearrange("p (t g) -> p t g", t=T)
                first_best(gs, NG, rank[:, 0:NG], mx, gsel, rt[:, 8, 0:T * NG].rearrange("p (t g) -> p t g", t=T))
                gm = rt[:, 7, 0:T * NG].unsqueeze(2).broadcast_to([P, T * NG, EPG])
                link(tt(rg(9), rg(1), gm, M))
                link(ts(rt[:, 7, 0:T * NG], rt[:, 7, 0:T * NG], -1.0, -NEG, AD, M))
                link(tt(rg(9), rg(9), gm, AD))
                first_best(r(9), NE, rank[:, :], mx, r(10), r(11))
                link(stt(r(12), r(10), 2 * NEG, r(9), M, AD))
                first_best(r(12), NE, rank[:, :], mx, r(13), r(11))
                link(tt(r(13), r(13), r(10), AD))
                link(tt(r(13), r(13), r(0), M))
                link(v.tensor_reduce(mx, r(13), AX.X, AD))
                link(v.reciprocal(mx, mx))
                tt(r(15), r(13), mx.unsqueeze(2).broadcast_to([P, T, NE]), M).then_inc(s["combine"], 1)
                v.wait_ge(s["combineT"], run)
                cp(combT[:, :], bank[1][0:NE, 0:SEQ]).then_inc(s["combT"], 1)
                v.wait_ge(s["combine_bc"], run)
                for n in range(4, 8):
                    ins = cp(cb[:, 2 * n:2 * n + 2, :].rearrange("p a b -> p (a b)"), bank[n][:, :])
                ins.then_inc(s["cb_dve"], 1)
                v.wait_ge(s["cb_dve"], run)
                v.wait_ge(s["cb_act"], run)
                nm = NE * DE // FB
                swiglu(f"moe.{l}", nm, 2 * n1 + nm * l, nm * l)
                add_gated_to_x()
                v.wait_ge(s["x"], 5 + 2 * l)
            link(normalise(x, xn))
            v.wait_ge(s["final_in"], 16)
            tt(xn[:, :, :], xn[:, :, :], fin[:, :].unsqueeze(1).broadcast_to([P, T, D]), M).then_inc(s["out_ready"], 1)


_INS = ["x", "mem", "ffn1_norm", "ffn1_w_in", "ffn1_w_out", "mix_norm", "mem_norm", "w_in", "lru_conv_w", "lru_conv_b",
        "lru_a_w", "lru_a_b", "lru_x_w", "lru_x_b", "lru_lambda", "moba_q_norm", "moba_k_norm", "mem_w_kv",
        "mem_q_norm", "mem_k_norm", "w_out", "ffn2_norm", "ffn2_w_in", "ffn2_w_out", "c_2", "positions_2", "ada_w_2",
        "ada_b_2", "norm1_g_2", "w_in_2", "hg_lb_logits_2", "hg_norm_g_2", "q_norm_g_2", "w_q_up_2", "kv_norm_g_2",
        "w_kv_up_2", "w_br_a_2", "w_br_b_2", "w_out_2", "norm2_g_2", "w_router_2", "router_bias_2", "w_gate_2",
        "w_up_2", "w_down_2", "final_g_2"]


def kernel(**inputs):
    import concourse.bacc as _bacc
    from concourse.bass_utils import run_bass_kernel_spmd as _run

    nc = _bacc.Bacc("TRN2", target_bir_lowering=False, num_devices=1)
    arrays, args = {}, {}
    for name in _INS:
        v = np.ascontiguousarray(inputs[name])
        arrays[f"in_{name}"] = v
        args[name] = nc.dram_tensor(f"in_{name}", v.shape, mybir.dt.from_np(v.dtype), kind="ExternalInput").ap()
    args["out"] = nc.dram_tensor("out_x", (1, SEQ, D), F32, kind="ExternalOutput").ap()
    build(nc, args)
    return _run(nc, [arrays], core_ids=[0]).results[0]["out_x"]
```

```python
from contextlib import ExitStack

import numpy as np
import concourse.bass as bass
from concourse import mybir

F32 = mybir.dt.float32
F32R = mybir.dt.float32r
I32 = mybir.dt.int32
U8 = mybir.dt.uint8
ALU = mybir.AluOpType
ACT = mybir.ActivationFunctionType
AX = mybir.AxisListType

P = 128
SEQ = 256
T = SEQ // P
D = 1024
KC = D // P
EPS = 1e-6
HD = 64
LW = 512
LC = LW // P
LRU_C = 8.0
DFF = 2816
LAYERS = 2
HGH, DK = 4, 128
QL, KVL, ROPE, NOPE, MV = 384, 256, 32, 64, 64
MH = 8
DQK = NOPE + ROPE
NE, NG, EPG, DE = 16, 4, 4, 512
CHUNK = 64
FB = 256
RING = 6
TILE = 2048
LEVELS = [1, 2, 4, 8, 16, 32, 64, 128]
NEG = -1.0e30
MISC = QL + KVL + ROPE
ADA = 6 * D
ADA_SLABS = ADA // FB


def ffn_pos(n, kind, c):
    if kind == "down":
        return 3 * n - 1 if c == n - 1 else 3 * c + 4
    off = {"gate": 0, "up": 1}[kind]
    return off if c == 0 else 3 * c - 1 + off


def build(nc, a):
    ctx = ExitStack()
    with ctx:
        def sb(name, shape, dt=F32):
            return ctx.enter_context(nc.sbuf_tensor("sb_" + name, shape, dt))

        def sem(name):
            return ctx.enter_context(nc.semaphore(name))

        bank = [ctx.enter_context(nc.psum_tensor(f"bank{i}", [P, 512], F32)) for i in range(8)]

        x = sb("x", [P, T, D])
        hT = sb("hT", [P, KC, SEQ])
        xn = sb("xn", [P, T, D])
        ring = sb("ring", [P, RING, TILE])
        small_a = sb("small_a", [P, 2, 512])
        small_b = sb("small_b", [P, 2, 512])
        gbc = sb("gbc", [P, D])
        ident = sb("ident", [P, P])
        ones = sb("ones", [P, P])
        pcol = sb("pcol", [P, 2, P])
        abcol = sb("abcol", [P, LAYERS, 48])
        modc = sb("modc", [P, LAYERS, 48])
        scol = sb("scol", [P, LAYERS, 2, KC])
        csilu = sb("csilu", [P, KC])
        stat = sb("stat", [P, 8, 32])
        lbc = sb("lbc", [P, 8, HGH])
        lruc = sb("lruc", [P, 10, LC])
        level_mask = sb("level_mask", [P, 8, P])
        seg = sb("seg", [P, 8, 1028], U8)
        dist = sb("dist", [P, T, SEQ])
        mla_mask = sb("mla_mask", [P, T, SEQ])
        rope_t = sb("rope_t", [P, 12, T, 16])
        pos_i = sb("pos_i", [P, T], I32)
        rank = sb("rank", [P, NE])
        router = sb("router", [P, KC, NE])
        rbias = sb("rbias", [P, NE])
        combT = sb("combT", [NE, SEQ])
        overflow = sb("overflow", [P, 8], I32)
        w_next = sb("w_next", [P, 8])
        w_slot = sb("w_slot", [P, 8])
        slot_col = sb("slot_col", [P, 8])
        arena_at = nc.sbuf_base
        arena = sb("arena", [P, 25600])

        def view(at, *shape):
            n = int(np.prod(shape))
            assert at + n <= 25600, (at, shape)
            v = arena[:, at:at + n]
            if len(shape) == 2:
                v = v.rearrange("p (a b) -> p a b", b=shape[1])
            if len(shape) == 3:
                v = v.rearrange("p (a b c) -> p a b c", b=shape[1], c=shape[2])
            if len(shape) == 4:
                v = v.rearrange("p (a b c d) -> p a b c d", b=shape[1], c=shape[2], d=shape[3])
            return v

        prow = view(12000, 2, P)
        abrow = view(12256, LAYERS, P)
        iot = view(12512, 3, P).bitcast(I32)
        ada_acc = view(0, ADA_SLABS, FB)
        ada_w = view(6144, 2, KC, FB)
        mixT = view(0, KC, SEQ)
        memx = view(19456, T, D)
        memT = view(21504, KC, SEQ)
        qk4 = view(6144, 4, 512)
        qkT = view(8192, 4, 2, SEQ)
        v2 = view(10240, 2, T, 256)
        att_p = view(11264, 16, SEQ)
        att_pT = view(15360, 8, T, SEQ)
        xl = view(19456, LC, SEQ + 4)
        xb = view(20496, LC, SEQ)
        lr = view(21520, LC, SEQ)
        li = view(22544, LC, SEQ)
        lt = view(2048, LC, SEQ)
        lt2 = view(3072, LC, SEQ)
        gel = view(5120, LC, SEQ)
        lru_w_all = view(24576, 2, LC, P)
        G = view(0, T, 2, D)
        hq = view(4096, HGH, SEQ)
        hk = view(5120, HGH, SEQ)
        hg = view(6144, HGH, SEQ)
        hf = view(7168, HGH, SEQ)
        scan_f = view(8192, HGH * SEQ)
        scan_b = view(9216, HGH * SEQ)
        hy = view(10240, HGH * SEQ)
        attT = view(11264, 3, HGH, P)
        prod = view(12800, T, HGH, P)
        mlp_p = view(4096, 16, SEQ)
        mlp_pT = view(8192, 8, T, SEQ)
        oaT = view(13312, HGH, SEQ)
        misc = view(14336, T, MISC)
        cT = view(15680, 5, SEQ)
        q96 = view(16960, T, MH, DQK)
        k96 = view(18496, T, MH, DQK)
        vm = view(20032, T, MH, MV)
        qT96 = view(21056, MH, SEQ)
        kT96 = view(23104, MH, SEQ)
        ymT = view(14336, 4, SEQ)
        merged = view(16960, T, D)
        diag = view(19008, KC, P)
        oa = view(8192, T, 512)
        oa_sq = view(9216, 1024)
        fin = view(24576, D)
        scr = small_b[:, :, :].rearrange("p a b -> p (a b)")
        hgate = xn[:, 0, :].rearrange("p (h s) -> p h s", h=HGH)
        vh = xn[:, 1, :].rearrange("p (t c) -> p t c", t=T)
        cb = view(0, NE, SEQ)
        sel = view(4096, NE, P)
        ep = view(6144, 2, 512)
        rt = view(7168, 16, T * NE)
        def rounded(name, at, *shape):
            assert at + int(np.prod(shape)) <= 25600
            return nc.alloc_sbuf_tensor_at("sb_" + name, [P, *shape], F32R, offset=arena_at + 4 * at)

        xn_parts = rounded("xn_parts", 8192, 2, T, D)
        pos_bc = view(12288, NE, SEQ)
        pick = rounded("pick", 16384, T, 2, P)
        put = rounded("put", 16896, 2, SEQ)
        ye_parts = rounded("ye_parts", 17408, 2, D)
        before = view(22400, P)
        slot_row = view(22528, P)
        sel_r = rounded("sel_r", 20032, NE, P)
        posT = rounded("posT", 22080, SEQ)
        slot_no = view(22336, T * NE)

        acc = bank[0:4]
        two = [b[:, :].rearrange("p (a c) -> p a c", a=2) for b in bank]

        rows, row_loads = {}, []

        def param(tile, name, ap, n):
            at = sum(v[2] for v in rows.values() if v[0] == tile)
            rows[name] = (tile, at, n)
            row_loads.append((tile, at, n, ap))

        def by_row(ap):
            return ap.rearrange("a (r c) -> (a r) c", c=P)

        param(0, "ffn1", by_row(a["ffn1_norm"]), 8)
        param(0, "mix", by_row(a["mix_norm"]), 8)
        param(0, "mem", by_row(a["mem_norm"]), 8)
        param(0, "ffn2", by_row(a["ffn2_norm"]), 8)
        param(0, "n1", by_row(a["norm1_g_2"]), 16)
        param(0, "n2", by_row(a["norm2_g_2"]), 16)
        param(0, "qn", by_row(a["q_norm_g_2"]), 6)
        param(0, "kvn", by_row(a["kv_norm_g_2"]), 4)
        param(0, "hgn", by_row(a["hg_norm_g_2"]), 8)
        param(0, "convw", a["lru_conv_w"].rearrange("a w (r c) -> (a w r) c", c=P), 16)
        param(0, "convb", by_row(a["lru_conv_b"]), 4)
        param(0, "ab", a["lru_a_b"].rearrange("a (r b) c -> (a r) (b c)", b=2), 4)
        param(0, "xb", a["lru_x_b"].rearrange("a (r b) c -> (a r) (b c)", b=2), 4)
        param(0, "lam", by_row(a["lru_lambda"]), 4)
        param(0, "lb", by_row(a["hg_lb_logits_2"]), 8)
        param(1, "c", by_row(a["c_2"]), 8)
        param(1, "heads", None, 4)
        row_loads.pop()
        heads_row = rows["heads"][1]
        HEAD_GAINS = ["moba_q_norm", "moba_k_norm", "mem_q_norm", "mem_k_norm"]
        N_ROW_DMA = len(row_loads) + 2 * len(HEAD_GAINS) + LAYERS

        def col(name, i=0, n=1):
            tile, at, _ = rows[name]
            return pcol[:, tile, at + i:at + i + n]

        stream, place, total = [], {}, 0

        def tile(name, src):
            nonlocal total
            stream.append((name, src))
            place[name] = total
            total += 1

        def swiglu_tiles(name, n, gate, up, down):
            nonlocal total
            stream.append((name, n, gate, up, down))
            place[name] = total
            total += 3 * n

        def cols(w, c0, n):
            return w.rearrange("(k p) n -> p k n", p=P)[:, :, bass.ds(c0, n)]

        def rws(w, r0, n):
            return w[bass.ds(r0, n * P), :].rearrange("(k p) n -> p k n", p=P)

        def dense(name, w_in, w_out):
            swiglu_tiles(name, DFF // FB,
                         lambda i, c: cols(w_in, i * (2 * FB) + c * FB, FB),
                         lambda i, c: cols(w_in, i * (2 * FB) + (DFF + c * FB), FB),
                         lambda i, c: rws(w_out, i * (2 * FB) + c * FB, FB // P))

        dense("ffn1", a["ffn1_w_in"][0], a["ffn1_w_out"][0])
        for n in range(2):
            tile(f"mem_kv{n}", cols(a["mem_w_kv"][0], n * FB, FB))
        for n in range(8):
            tile(f"w_in{n}", cols(a["w_in"][0], n * FB, FB))
        for n in range(4):
            tile(f"w_out{n}", rws(a["w_out"][0], n * FB, 2))
        dense("ffn2", a["ffn2_w_in"][0], a["ffn2_w_out"][0])
        for l in range(LAYERS):
            w2 = a["w_in_2"][l]
            for n in (0, 1, 6, 7, 2, 3, 4, 5):
                tile(f"proj{n}.{l}", cols(w2, n * FB, FB))
            for n in range(3):
                tile(f"misc{n}.{l}", cols(w2, 2048 + n * FB, min(FB, MISC - n * FB)))
            for n in range(2):
                tile(f"q_up{n}.{l}", cols(a["w_q_up_2"][l], n * QL, QL))
            tile(f"kv_up.{l}", cols(a["w_kv_up_2"][l], 0, 1024))
            for n in range(8):
                tile(f"gates{n}.{l}", cols(w2, 2048 + MISC + n * FB, FB))
            for n in range(2):
                tile(f"br_a{n}.{l}", rws(a["w_br_a_2"][l], n * FB, 2))
            for n in range(2):
                tile(f"br_b{n}.{l}", rws(a["w_br_b_2"][l], n * FB, 2))
            for n in range(4):
                tile(f"w_out{n}.{l}", rws(a["w_out_2"][l], n * FB, 2))
            wg, wu, wd = a["w_gate_2"][l], a["w_up_2"][l], a["w_down_2"][l]
            swiglu_tiles(f"moe.{l}", NE * DE // FB,
                         lambda i, c, w=wg: w.rearrange("e (k p) n -> p e k n", p=P)[:, i + c // 2, :, (c % 2) * FB:(c % 2 + 1) * FB],
                         lambda i, c, w=wu: w.rearrange("e (k p) n -> p e k n", p=P)[:, i + c // 2, :, (c % 2) * FB:(c % 2 + 1) * FB],
                         lambda i, c, w=wd: w.rearrange("e (k p) n -> p e k n", p=P)[:, i + c // 2, 2 * (c % 2):2 * (c % 2) + 2, :])

        class Signals(dict):
            def __missing__(self, name):
                self[name] = sem(name)
                return self[name]

        s = Signals()
        ring_full = [sem(f"ring_full{i}") for i in range(RING)]
        tiles_used = sem("tiles_used")
        block = ctx.enter_context(nc.Block())

        def slot_view(pos, kind):
            w = ring[:, pos % RING, :]
            if kind == 3 * QL:
                return w[:, 0:3 * QL].rearrange("p (k n) -> p k n", k=3)
            if kind == 1024:
                return w.rearrange("p (k n) -> p k n", k=2)
            return w[:, 0:KC * kind].rearrange("p (k n) -> p k n", k=KC)

        SLOT_COUNTS = dict(
            act=(("xg_act", NE), ("pos_out", NE // 2), ("ye_hi", NE)),
            pe=(("pos_turned", 1), ("gathered", 2 * NE), ("weights", NE // 2), ("pos_bc", NE // 2), ("scattered", NE)),
            v=(("pick", NE // 2), ("posT", 1), ("xg_dve", NE), ("w_next", NE // 2), ("w_slot", NE // 2),
               ("put", NE), ("ye_lo", NE)))

        def expert_pos(kind, j):
            return ffn_pos(2 * NE, kind, j)

        def loop_shape(n):
            j0 = 3 if n % 2 else 2
            return j0, (n - j0) // 2

        @block.sync
        def _(sp):
            sp.dma_start(x[:, :, :], a["x"][0].rearrange("(t p) d -> p t d", p=P)).then_inc(s["x_in"], 16)

            def load(pos, src, i=0):
                if not (isinstance(i, int) and pos < RING):
                    sp.wait_ge(tiles_used, RING * i + (pos - RING + 1))
                n, k = src.shape[2], src.shape[1]
                dst = ring[:, pos % RING, 0:n * k].rearrange("p (k n) -> p k n", k=k)
                sp.dma_start(dst, src).then_inc(ring_full[pos % RING], 16)

            for entry in stream:
                pos = place[entry[0]]
                if len(entry) == 2:
                    load(pos, entry[1])
                    continue
                _, n, gate, up, down = entry

                def step(i, c, first=False):
                    load(pos + ffn_pos(n, "gate", c), gate(i, c), i)
                    load(pos + ffn_pos(n, "up", c), up(i, c), i)
                    if not first:
                        load(pos + 3 * (c - 1) + 4, down(i, c - 1), i)

                j0, turns = loop_shape(n)
                step(0, 0, True)
                for c in range(1, j0):
                    step(0, c)
                with sp.Fori(0, turns) as i:
                    step(i, j0)
                    step(i, j0 + 1)
                load(pos + 3 * n - 1, down(turns - 1, j0 + 1))

            sp.wait_ge(s["out_ready"], 1)
            sp.dma_start(a["out"][0].rearrange("(t p) d -> p t d", p=P), xn[:, :, :]).then_inc(s["out_stored"], 16)
            sp.wait_ge(s["out_stored"], 16)

        @block.gpsimd
        def _(pool):
            done = [0]

            def link(ins):
                done[0] += 1
                ins.then_inc(s["pool_chain"], 1)
                pool.wait_ge(s["pool_chain"], done[0])

            pool.wait_ge(s["prow_zero"], 1)
            for tile_, at, n, ap in row_loads:
                pool.dma_start(prow[at:at + n, tile_, :], ap).then_inc(s["rows_in"], 16)
            for r, name in enumerate(HEAD_GAINS):
                for half in range(2):
                    pool.dma_start(prow[heads_row + r:heads_row + r + 1, 1, half * HD:(half + 1) * HD],
                                   a[name]).then_inc(s["rows_in"], 16)
            for l in range(LAYERS):
                pool.dma_start(abrow[0:48, l, :], a["ada_b_2"][l].rearrange("(r c) -> r c", c=P)).then_inc(s["rows_in"], 16)
            link(pool.memset(ident[:, :], 0.0))
            pool.affine_select(out=ident[:, :], in_=ident[:, :], compare_op=ALU.not_equal, fill=1.0,
                               base=0, pattern=[[-1, P]], channel_multiplier=1).then_inc(s["ident"], 1)
            pool.dma_start(pos_i[:, :], a["positions_2"].rearrange("a (t p) -> p (a t)", p=P),
                           allow_slow_non_contiguous=True).then_inc(s["pos_in"], 16)
            pool.iota(iot[:, 0, :], [[0, P]], base=0, channel_multiplier=1)
            pool.iota(iot[:, 1, :], [[1, P]], base=0, channel_multiplier=0)
            pool.iota(view(22000, 1028).bitcast(I32), [[1, 1028]], base=0, channel_multiplier=0)
            for t in range(T):
                ins = pool.iota(dist[:, t, :], [[-1, SEQ]], base=t * P, channel_multiplier=1,
                                allow_small_or_imprecise_dtypes=True)
            link(ins)
            for t in range(T):
                ins = pool.affine_select(out=dist[:, t, :], in_=dist[:, t, :], compare_op=ALU.is_ge, fill=-NEG,
                                         base=t * P, pattern=[[-1, SEQ]], channel_multiplier=1)
            ins.then_inc(s["patterns"], 1)
            link(pool.memset(mla_mask[:, :, :], 0.0))
            link(pool.memset(mla_mask[0:CHUNK, 0, CHUNK:SEQ], NEG))
            link(pool.memset(mla_mask[CHUNK:P, 0, P:SEQ], NEG))
            link(pool.memset(mla_mask[0:CHUNK, 1, P + CHUNK:SEQ], NEG))
            inv = np.float32(10000.0) ** (-np.arange(16, dtype=np.float32) / np.float32(16))
            for n in range(16):
                ins = pool.memset(rope_t[:, 0, 0, n:n + 1], float(inv[n]))
            ins.then_inc(s["inv_freq"], 1)
            pool.dma_start(router[:, :, :], a["w_router_2"].rearrange("(k p) e -> p k e", p=P)).then_inc(s["router_in"], 16)
            pool.dma_start(rbias[:, :], a["router_bias_2"].partition_broadcast(P)).then_inc(s["router_in"], 16)
            pool.wait_ge(s["lru_w_zero"], 1)
            for g, name in ((0, "lru_a_w"), (1, "lru_x_w")):
                for half in range(2):
                    w = lru_w_all[half * HD:(half + 1) * HD, g, :, half * HD:(half + 1) * HD]
                    pool.dma_start(w, a[name][0].rearrange("(c h) i j -> h i c j", h=2)[half]).then_inc(s["lru_w_in"], 16)

            pool.wait_ge(s["csilu"], 1)
            for l in range(LAYERS):
                if l:
                    pool.wait_ge(s["x"], 2)
                w = a["ada_w_2"][l].rearrange("(k p) n -> p k n", p=P)
                ada_base = l * ADA_SLABS

                def slab_load(n, b):
                    pool.dma_start(ada_w[:, b], w[:, :, bass.ds(n * FB, FB)]).then_inc(s[f"ada_in{b}"], 16)

                def slab(i, b, more):
                    n = 2 * i + b
                    pool.wait_ge(s[f"ada_in{b}"], 16 * i + 16 * (l * ADA_SLABS // 2 + 1))
                    base = 4 * (ada_base + b)
                    wv = ada_w[:, b]
                    c_b = csilu[:, :].unsqueeze(2).broadcast_to([P, KC, FB])
                    pool.tensor_tensor(wv, wv, c_b, ALU.mult).then_inc(s["ada_chain"], 1)
                    pool.wait_ge(s["ada_chain"], 8 * i + base + 1)
                    pool.tensor_tensor(wv[:, 0:4], wv[:, 0:4], wv[:, 4:8], ALU.add).then_inc(s["ada_chain"], 1)
                    pool.wait_ge(s["ada_chain"], 8 * i + base + 2)
                    pool.tensor_tensor(wv[:, 0:2], wv[:, 0:2], wv[:, 2:4], ALU.add).then_inc(s["ada_chain"], 1)
                    pool.wait_ge(s["ada_chain"], 8 * i + base + 3)
                    pool.tensor_tensor(ada_acc[:, bass.ds(n, 1), :], wv[:, 0:1], wv[:, 1:2], ALU.add).then_inc(s["ada_chain"], 1)
                    if more:
                        pool.wait_ge(s["ada_chain"], 8 * i + base + 4)
                        slab_load(n + 2, b)

                for b in range(2):
                    slab_load(b, b)
                with pool.Fori(0, ADA_SLABS // 2 - 1) as i:
                    slab(i, 0, True)
                    slab(i, 1, True)
                slab(ADA_SLABS // 2 - 1, 0, False)
                slab(ADA_SLABS // 2 - 1, 1, False)
            for l in range(LAYERS):
                pool.wait_ge(s["x"], 4 + 2 * l)
                pool.iota(slot_row, [[1, P]], base=0, channel_multiplier=0, allow_small_or_imprecise_dtypes=True)
                pool.iota(slot_col[:, 0:1], [[0, 1]], base=0, channel_multiplier=1, allow_small_or_imprecise_dtypes=True)
                link(pool.memset(before, 1.0))
                pool.affine_select(out=before, in_=before, compare_op=ALU.is_ge, fill=0.0, base=-1,
                                   pattern=[[1, P]], channel_multiplier=-1).then_inc(s["slot_patterns"], 1)
                pool.wait_ge(s["xn_hi"], l + 1)
                pool.tensor_tensor(xn_parts[:, 1], xn[:, :, :], xn_parts[:, 0].bitcast(F32), ALU.subtract)\
                    .then_inc(s["xn_lo"], 1)
            pool.dma_start(fin[:, :], a["final_g_2"].partition_broadcast(P)).then_inc(s["final_in"], 16)

        @block.scalar
        def _(act):
            A = act.activation

            def used(name):
                act.wait_ge(tiles_used, place[name] + 1)

            def root(run):
                act.wait_ge(s["ms"], run)
                A(stat[:, 2, :], stat[:, 1, :], ACT.Sqrt).then_inc(s["root"], 1)

            def turn(run, dst, scale, bias):
                act.wait_ge(s["xnT"], run)
                for k in range(KC // 2):
                    src = bank[4 + k // 2][:, (k % 2) * SEQ:(k % 2 + 1) * SEQ]
                    ins = A(dst[:, k, :], src, ACT.Identity, scale=scale(k), bias=bias(k) if bias else 0.0)
                ins.then_inc(s["hT_act"], 1)

            def swiglu(name, n, base):
                pos = place[name]

                def step(i, c, late=True):
                    j = 2 * i + c
                    p = c % 2
                    act.wait_ge(tiles_used, RING * i + (pos + (0 if c == 0 else 3 * c - 1) + 1))
                    if late:
                        act.wait_ge(s["hidden"], j + (base - 1))
                    A(small_a[:, p, :], bank[4 + 2 * p][:, :], ACT.Silu).then_inc(s["silu"], 1)

                j0, turns = loop_shape(n)
                for c in range(j0):
                    step(0, c, base + c >= 2)
                with act.Fori(0, turns) as i:
                    step(i, j0)
                    step(i, j0 + 1)

            def sparse(l):
                pos0 = place[f"moe.{l}"]
                base = 2 * (DFF // FB) + 2 * NE * l

                def step(i, c):
                    p = c % 2
                    act.wait_ge(tiles_used, 2 * RING * i + (pos0 + expert_pos("up", c) + 1))
                    if c >= 2:
                        act.wait_ge(s["hidden"], 4 * i + (base + c - 1))
                    A(small_a[:, p, 0:2 * P], bank[4 + p][:, 0:2 * P], ACT.Silu).then_inc(s["silu"], 1)

                def gathered(i, g):
                    for r in (0, 2):
                        act.wait_ge(s["gathered"], 4 * i + (32 * l + 4 * g + r + 1))
                        for k in (2 * r, 2 * r + 1):
                            ins = A(hT[:, k, :], bank[6][:, (k % 2) * SEQ:(k % 2 + 1) * SEQ], ACT.Identity,
                                    scale=scol[:, l, 1, k:k + 1], bias=modc[:, l, 24 + k:25 + k])
                        ins.then_inc(s["xg_act"], 1)

                def ye(i, e):
                    act.wait_ge(tiles_used, 2 * RING * i + (pos0 + expert_pos("down", 2 * e + 1) + 1))
                    act.wait_ge(s["w_slot"], i + (8 * l + e // 2 + 1))
                    if e:
                        act.wait_ge(s["scattered"], 2 * i + (16 * l + e))
                    for half in range(2):
                        ins = A(ye_parts[:, 0, half * 512:(half + 1) * 512], bank[6 + half][:, :], ACT.Copy,
                                scale=w_slot[:, e % 2:e % 2 + 1])
                    ins.then_inc(s["ye_hi"], 1)

                def pos_copies(b):
                    for n in range(4):
                        act.wait_ge(s["pos_bc"], 8 * l + 4 * b + n + 1)
                        A(pos_bc[:, 8 * b + 2 * n:8 * b + 2 * n + 2, :], two[n], ACT.Copy).then_inc(s["pos_out"], 1)

                def pair(i, g, start=False, last=False):
                    step(i, 4 * g)
                    if not start:
                        ye(i, 2 * g - 1)
                    step(i, 4 * g + 1)
                    if start:
                        pos_copies(1)
                    step(i, 4 * g + 2)
                    ye(i, 2 * g)
                    step(i, 4 * g + 3)
                    if not last:
                        gathered(i, g + 1)

                gathered(0, 0)
                pos_copies(0)
                pair(0, 0, start=True)
                with act.Fori(0, NE // 2 - 2) as i:
                    pair(i, 1)
                pair(0, NE // 2 - 1, last=True)
                ye(0, NE - 1)

            def softmax_exp(event, run, src, dst, rows_, scale):
                act.wait_ge(s[event], run)
                for r in rows_:
                    ins = A(dst[:, r, :], src(r), ACT.Exp, bias=stat[:, 4, r:r + 1], scale=scale,
                            accum_out=stat[:, 5, r:r + 1])
                return ins

            def gain(name, off=0):
                return lambda k: col(name, off + k)

            act.dma_start(memx[:, :, :], a["mem"][0].rearrange("(t p) d -> p t d", p=P)).then_inc(s["mem_in"], 16)
            roots = iter(range(1, 100))
            root(next(roots))
            act.wait_ge(s["pcol"], 1)
            A(csilu[:, :], col("c", 0, KC), ACT.Silu).then_inc(s["csilu"], 1)
            act.wait_ge(s["small_in"], 1)
            A(lruc[:, 2, :], lruc[:, 1, :], ACT.Exp, scale=-1.0)
            A(lbc[:, 2, :], lbc[:, 0, :], ACT.Exp)
            A(lbc[:, 3, :], lbc[:, 1, :], ACT.Exp).then_inc(s["small_exp"], 1)
            act.wait_ge(s["angles"], 1)
            A(rope_t[:, 10], rope_t[:, 8], ACT.Sin)
            A(rope_t[:, 11], rope_t[:, 9], ACT.Sin).then_inc(s["sincos"], 1)
            turn(1, hT, gain("ffn1"), None)
            root(next(roots))
            n1 = DFF // FB
            swiglu("ffn1", n1, 0)

            turn(2, memT, gain("mem"), None)
            used("mem_kv1")
            A(v2[:, 1], two[1], ACT.Copy).then_inc(s["mem_v"], 1)
            root(next(roots))
            turn(3, hT, gain("mix"), None)
            act.wait_ge(s["xl_zero"], 1)
            for n in range(2):
                used(f"w_in{n}")
                ins = A(xl[:, 2 * n:2 * n + 2, 3:3 + SEQ], two[2 + n], ACT.Copy)
            ins.then_inc(s["xl"], 1)
            for n in range(2):
                used(f"w_in{2 + n}")
                ins = A(gel[:, 2 * n:2 * n + 2, :], two[4 + n], ACT.Gelu_apprx_tanh)
            ins.then_inc(s["gelu"], 1)
            used("w_in6")
            A(v2[:, 0], two[0], ACT.Copy).then_inc(s["moba_v"], 1)
            act.wait_ge(s["lru_gates"], 1)
            for c in range(LC):
                A(lr[:, c, :], bank[2 + c // 2][:, (c % 2) * SEQ:(c % 2 + 1) * SEQ], ACT.Sigmoid, bias=col("ab", c))
                ins = A(li[:, c, :], bank[4 + c // 2][:, (c % 2) * SEQ:(c % 2 + 1) * SEQ], ACT.Sigmoid, bias=col("xb", c))
            ins.then_inc(s["lru_ri"], 1)
            act.wait_ge(s["lru_ri"], 1)
            for c in range(LC):
                A(lt[:, c, :], lr[:, c, :], ACT.Tanh, scale=lruc[:, 9, c:c + 1])
            for c in range(LC):
                ins = A(lt2[:, c, :], lr[:, c, :], ACT.Exp, scale=lruc[:, 8, c:c + 1])
            ins.then_inc(s["lru_a"], 1)
            root(next(roots))
            act.wait_ge(s["lru_m2"], 1)
            A(lt[:, :, :], lt[:, :, :], ACT.Sqrt, scale=2.0).then_inc(s["lru_mult"], 1)
            act.wait_ge(s["qkT"], 1)
            for w in range(2):
                ins = A(qkT[:, w], two[w], ACT.Identity, scale=col("heads", w))
            ins.then_inc(s["qk_act"], 1)
            softmax_exp("att_max", 1, lambda r: att_p[:, r, :], att_p, range(8), HD ** -0.5).then_inc(s["att_exp"], 1)
            act.wait_ge(s["att_max"], 2)
            for r in range(8, 16):
                h, t = (r - 8) // 2, r % 2
                ins = A(att_p[:, r, :], bank[2 * t + h % 2][:, (h // 2) * SEQ:(h // 2 + 1) * SEQ], ACT.Exp,
                        bias=stat[:, 4, r:r + 1], scale=HD ** -0.5, accum_out=stat[:, 5, r:r + 1])
            ins.then_inc(s["att_exp"], 1)
            act.wait_ge(s["att_pT"], 1)
            for h in range(4):
                ins = A(att_pT[:, h], two[4 + h], ACT.Copy)
            ins.then_inc(s["moba_pT_out"], 1)
            act.wait_ge(s["att_pv"], 1)
            A(mixT[:, 4:6, :], two[4], ACT.Copy)
            act.wait_ge(s["att_pv"], 2)
            A(mixT[:, 6:8, :], two[0], ACT.Copy).then_inc(s["mix_heads"], 1)

            root(next(roots))
            turn(4, hT, gain("ffn2"), None)
            swiglu("ffn2", n1, n1)

            for l in range(LAYERS):
                run = l + 1
                root(next(roots))
                turn(5 + 2 * l, hT, lambda k: scol[:, l, 0, k:k + 1], lambda k: modc[:, l, k:k + 1])
                for n in range(2):
                    used(f"proj{n}.{l}")
                    ins = A(hq[:, 2 * n:2 * n + 2, :], two[n], ACT.Silu)
                ins.then_inc(s["hq"], 1)
                for n in range(2):
                    used(f"proj{6 + n}.{l}")
                    ins = A(hgate[:, 2 * n:2 * n + 2, :], two[2 + n], ACT.Silu)
                ins.then_inc(s["hgate"], 1)
                for n in range(2):
                    used(f"proj{2 + n}.{l}")
                    ins = A(hf[:, 2 * n:2 * n + 2, :], two[4 + n], ACT.Sigmoid)
                ins.then_inc(s["hf"], 1)
                for n in range(3):
                    w = min(FB, MISC - n * FB)
                    used(f"misc{n}.{l}")
                    ins = A(misc[:, :, n * FB:n * FB + w], bank[n][:, 0:T * w].rearrange("p (t w) -> p t w", t=T), ACT.Copy)
                ins.then_inc(s["misc"], 1)
                act.wait_ge(s["hf_clamped"], run)
                A(hg[:, :, :], hg[:, :, :], ACT.Ln).then_inc(s["hg"], 1)
                root(next(roots))
                act.wait_ge(s["cT"], run)
                for k in range(5):
                    g_col = col("qn", 3 * l + k) if k < 3 else col("kvn", 2 * l + k - 3)
                    ins = A(cT[:, k, :], bank[k // 2][:, (k % 2) * SEQ:(k % 2 + 1) * SEQ], ACT.Identity, scale=g_col)
                ins.then_inc(s["cT_out"], 1)
                used(f"kv_up.{l}")
                for t in range(T):
                    for half in range(2):
                        src = bank[2 * t + half][:, :].rearrange("p (h c) -> p h c", h=4)
                        A(k96[:, t, 4 * half:4 * half + 4, 0:NOPE], src[:, :, 0:NOPE], ACT.Copy)
                        ins = A(vm[:, t, 4 * half:4 * half + 4, :], src[:, :, NOPE:], ACT.Copy)
                ins.then_inc(s["kv_out"], 1)
                for n, L in enumerate(LEVELS):
                    used(f"gates{n}.{l}")
                    ins = A(G[:, :, n // 4, (n % 4) * FB:(n % 4 + 1) * FB],
                            bank[n % 4][:, :].rearrange("p (t c) -> p t c", t=T), ACT.Tanh, scale=0.5)
                    ins.then_inc(s["gates"], 1)
                    act.wait_ge(s["scans"], 8 * l + n + 1)
                    if n:
                        act.wait_ge(s["hy"], 8 * l + n)
                    m = HGH * SEQ // (2 * L)
                    dst = hf[:, :, :].rearrange("p h s -> p (h s)").rearrange("p (m two c) -> p m two c", two=2, c=L)
                    sf = scan_f[:, :].rearrange("p (m two c) -> p m two c", two=2, c=L)
                    sb_ = scan_b[:, :].rearrange("p (m two c) -> p m two c", two=2, c=L)
                    A(dst[:, :, 1, :], sf[:, :, 1, :], ACT.Exp)
                    A(dst[:, :, 0, :], sb_[:, :, 0, :], ACT.Exp).then_inc(s["decay"], 1)
                root(next(roots))
                act.wait_ge(s["mla_qT"], run)
                for n in range(4):
                    ins = A(qT96[0:DQK, 2 * n:2 * n + 2, :], two[n][0:DQK], ACT.Copy)
                ins.then_inc(s["qT_out"], 1)
                for t in range(T):
                    act.wait_ge(s["mla_max"], T * l + t + 1)
                    for r in range(8 * t, 8 * t + 8):
                        ins = A(mlp_p[:, r, :], mlp_p[:, r, :], ACT.Exp, bias=stat[:, 4, r:r + 1],
                                scale=DQK ** -0.5, accum_out=stat[:, 5, r:r + 1])
                    ins.then_inc(s["mla_exp"], 1)
                act.wait_ge(s["mla_pT"], run)
                for h in range(4):
                    ins = A(mlp_pT[:, h], two[h], ACT.Copy)
                ins.then_inc(s["pT_act"], 1)
                act.wait_ge(s["mla_pv"], run)
                for n in range(2):
                    ins = A(ymT[:, 2 * n:2 * n + 2, :], two[n], ACT.Copy)
                ins.then_inc(s["ymT"], 1)
                act.wait_ge(s["mergedT"], run)
                for k in range(KC // 2):
                    ins = A(hT[:, k, :], bank[4 + k // 2][:, (k % 2) * SEQ:(k % 2 + 1) * SEQ], ACT.Copy)
                ins.then_inc(s["mT_act"], 1)
                root(next(roots))
                turn(6 + 2 * l, hT, lambda k: scol[:, l, 1, k:k + 1], lambda k: modc[:, l, 24 + k:25 + k])
                act.wait_ge(s["logits"], run)
                A(rt[:, 0, :], bank[0][:, 0:T * NE], ACT.Sigmoid).then_inc(s["scores"], 1)
                A(xn_parts[:, 0], xn[:, :, :], ACT.Copy).then_inc(s["xn_hi"], 1)
                act.wait_ge(s["overflow"], run)
                full = act.value_load(overflow[0:1, 0:1], min_val=0, max_val=1)
                base = 2 * n1 + 2 * NE * l
                with act.If(full):
                    act.wait_ge(s[f"combine_bc.{l}"], 1)
                    for n in range(4):
                        ins = A(cb[:, 2 * n:2 * n + 2, :], two[n], ACT.Copy)
                    ins.then_inc(s[f"cb_act.{l}"], 1)
                    swiglu(f"moe.{l}", 2 * NE, base)
                    if l < LAYERS - 1:
                        for name, n in SLOT_COUNTS["act"]:
                            act.sem_inc(s[name], n)
                with act.Else():
                    sparse(l)
            root(next(roots))

        @block.tensor
        def _(pe):
            mm, tr = pe.matmul, pe.transpose

            def landed(pos, i=0):
                pe.wait_ge(ring_full[pos % RING], 16 * i + 16 * (pos // RING + 1))

            def turn(run):
                pe.wait_ge(s["xn"], run)
                for k in range(KC):
                    for t in range(T):
                        ins = tr(bank[4 + k // 2][:, (k % 2) * SEQ + t * P:(k % 2) * SEQ + (t + 1) * P],
                                 xn[:, t, k * P:(k + 1) * P], ident[:, :])
                ins.then_inc(s["xnT"], 1)

            def have_hT(run):
                pe.wait_ge(s["hT_act"], run)
                pe.wait_ge(s["hT_dve"], run)

            def by_feature(name, out):
                pos = place[name]
                landed(pos)
                w = slot_view(pos, FB)
                for j in range(2):
                    for k in range(KC):
                        ins = mm(out[:, j * SEQ:(j + 1) * SEQ], w[:, k, j * P:(j + 1) * P], hT[:, k, :],
                                 start=k == 0, stop=k == KC - 1)
                ins.then_inc(tiles_used, 1)

            def by_token(name, out, lhs=None, n=FB):
                lhs = hT if lhs is None else lhs
                pos = place[name]
                landed(pos)
                w = slot_view(pos, n)
                for t in range(T):
                    for k in range(KC):
                        ins = mm(out[:, t * n:(t + 1) * n], lhs[:, k, t * P:(t + 1) * P], w[:, k, :],
                                 start=k == 0, stop=k == KC - 1)
                ins.then_inc(tiles_used, 1)

            def rows_product(pos, lhs, out, start, stop, i=0):
                landed(pos, i)
                w = slot_view(pos, 1024)
                for kk in range(2):
                    for t in range(T):
                        for half in range(2):
                            ins = mm(out[2 * t + half][:, :], lhs[:, kk, t * P:(t + 1) * P],
                                     w[:, kk, half * 512:(half + 1) * 512],
                                     start=start and kk == 0, stop=stop and kk == 1)
                ins.then_inc(tiles_used, 1)

            def swiglu(name, n, base):
                pos = place[name]

                def first(i, c, late=True):
                    j, p = 2 * i + c, c % 2
                    if late:
                        pe.wait_ge(s["hidden"], j + (base - 1))
                    for b in range(2):
                        at = pos + (0 if c == 0 else 3 * c - 1) + b
                        landed(at, i)
                        w = slot_view(at, FB)
                        for jj in range(2):
                            for k in range(KC):
                                ins = mm(bank[4 + 2 * p + b][:, jj * SEQ:(jj + 1) * SEQ], w[:, k, jj * P:(jj + 1) * P],
                                         hT[:, k, :], start=k == 0, stop=k == KC - 1)
                        ins.then_inc(tiles_used, 1)

                def second(i, c, at, start=False, stop=False):
                    pe.wait_ge(s["hidden"], 2 * i + (c + base + 1))
                    h = small_b[:, c % 2, :].rearrange("p (k s) -> p k s", k=2)
                    rows_product(pos + at, h, acc, start, stop, i)

                j0, turns = loop_shape(n)
                first(0, 0, base >= 2)
                for c in range(1, j0):
                    first(0, c, base + c >= 2)
                    second(0, c - 1, 3 * (c - 1) + 4, start=c == 1)
                with pe.Fori(0, turns) as i:
                    for c in (j0, j0 + 1):
                        first(i, c)
                        second(i, c - 1, 3 * (c - 1) + 4)
                second(0, n - 1, 3 * n - 1, stop=True)

            def sparse(l):
                pos0 = place[f"moe.{l}"]
                base = 2 * (DFF // FB) + 2 * NE * l
                comb = rt[:, 15, :].rearrange("p (t e) -> p t e", t=T)

                def first(i, c):
                    p = c % 2
                    if c % 4 == 0:
                        pe.wait_ge(s["xg_act"], 2 * i + (16 * l + c // 2 + 2))
                        pe.wait_ge(s["xg_dve"], 2 * i + (16 * l + c // 2 + 2))
                    if c >= 2:
                        pe.wait_ge(s["hidden"], 4 * i + (base + c - 1))
                    xg = hT[:, :, (c % 4 // 2) * P:(c % 4 // 2 + 1) * P]
                    for b, kind in enumerate(("gate", "up")):
                        at = pos0 + expert_pos(kind, c)
                        landed(at, 2 * i)
                        w = slot_view(at, FB)
                        for jj in range(2):
                            for k in range(KC):
                                ins = mm(bank[4 + p][:, (2 * b + jj) * P:(2 * b + jj + 1) * P], w[:, k, jj * P:(jj + 1) * P],
                                         xg[:, k, :], start=k == 0, stop=k == KC - 1)
                        ins.then_inc(tiles_used, 1)

                def second(i, c):
                    if c % 2 == 0 and c:
                        pe.wait_ge(s["ye_hi"], 2 * i + (16 * l + c // 2))
                        pe.wait_ge(s["ye_lo"], 2 * i + (16 * l + c // 2))
                    pe.wait_ge(s["hidden"], 4 * i + (base + c + 1))
                    at = pos0 + expert_pos("down", c)
                    landed(at, 2 * i)
                    w = slot_view(at, 1024)
                    for kk in range(2):
                        for half in range(2):
                            ins = mm(bank[6 + half][:, :], small_b[:, c % 2, kk * P:(kk + 1) * P],
                                     w[:, kk, half * 512:(half + 1) * 512],
                                     start=c % 2 == 0 and kk == 0, stop=c % 2 == 1 and kk == 1)
                    ins.then_inc(tiles_used, 1)

                def gather(i, g):
                    pe.wait_ge(s["pick"], i + (8 * l + g + 1))
                    if g:
                        pe.wait_ge(s["ye_hi"], 2 * i + (16 * l + 2 * g - 1))
                        pe.wait_ge(s["ye_lo"], 2 * i + (16 * l + 2 * g - 1))
                    for r in range(4):
                        if r >= 2:
                            pe.wait_ge(s["xg_dve" if r % 2 else "xg_act"], 2 * i + (16 * l + 2 * g + 1))
                        for kk in range(2):
                            k = 2 * r + kk
                            for n, (hl, t) in enumerate(((0, 0), (0, 1), (1, 0), (1, 1))):
                                ins = mm(bank[6 + r % 2][:, kk * SEQ:(kk + 1) * SEQ],
                                         xn_parts[:, hl, t, k * P:(k + 1) * P],
                                         pick[:, t].rearrange("p e s -> p (e s)"), start=n == 0, stop=n == 3)
                        ins.then_inc(s["gathered"], 1)
                    pe.wait_ge(s["xg_act"], 2 * i + (16 * l + 2 * g + 2))
                    for ee in range(2):
                        for t in range(T):
                            ins = mm(bank[6][:, ee:ee + 1], pick[:, t, ee, :].bitcast(F32),
                                     comb[:, t, bass.ds(2 * i + (2 * g + ee), 1)], start=t == 0, stop=t == T - 1)
                    ins.then_inc(s["weights"], 1)

                def gather_read(i, g):
                    pe.wait_ge(s["xg_dve"], 2 * i + (16 * l + 2 * g + 2))
                    pe.wait_ge(s["w_next"], i + (8 * l + g + 1))

                def scatter(i, e):
                    pe.wait_ge(s["put"], 2 * i + (16 * l + e + 1))
                    pe.wait_ge(s["ye_hi"], 2 * i + (16 * l + e + 1))
                    pe.wait_ge(s["ye_lo"], 2 * i + (16 * l + e + 1))
                    for hl in range(2):
                        for t in range(T):
                            for half in range(2):
                                ins = mm(acc[2 * t + half][:, :], put[:, e % 2, t * P:(t + 1) * P],
                                         ye_parts[:, hl, half * 512:(half + 1) * 512],
                                         start=e == 0 and hl == 0, stop=e == NE - 1 and hl == 1)
                    ins.then_inc(s["scattered"], 1)

                def spread(b):
                    for n in range(4):
                        if b:
                            pe.wait_ge(s["pos_out"], 8 * l + n + 1)
                        for ee in range(2):
                            ins = mm(bank[n][:, ee * SEQ:(ee + 1) * SEQ], sel_r[0:NE, 8 * b + 2 * n + ee, :], posT[0:NE, :],
                                     start=True, stop=True)
                        ins.then_inc(s["pos_bc"], 1)

                def pair(i, g, start=False, last=False):
                    first(i, 4 * g)
                    if not start:
                        second(i, 4 * g - 1)
                    first(i, 4 * g + 1)
                    if start:
                        spread(1)
                        gather_read(i, 0)
                    else:
                        scatter(i, 2 * g - 1)
                    second(i, 4 * g)
                    first(i, 4 * g + 2)
                    second(i, 4 * g + 1)
                    first(i, 4 * g + 3)
                    if not last:
                        gather(i, g + 1)
                    if start:
                        pe.wait_ge(s["pos_out"], 8 * l + 8)
                    scatter(i, 2 * g)
                    if not last:
                        gather_read(i, g + 1)
                    second(i, 4 * g + 2)

                pe.wait_ge(s["pos"], l + 1)
                for t in range(T):
                    ins = tr(bank[2][0:NE, t * P:(t + 1) * P], slot_no[:, t * NE:(t + 1) * NE], ident[:, :])
                ins.then_inc(s["pos_turned"], 1)
                pe.wait_ge(s["xn_hi"], l + 1)
                pe.wait_ge(s["xn_lo"], l + 1)
                gather(0, 0)
                pe.wait_ge(s["posT"], l + 1)
                spread(0)
                pair(0, 0, start=True)
                with pe.Fori(0, NE // 2 - 2) as i:
                    pair(i, 1)
                pair(0, NE // 2 - 1, last=True)
                second(0, 2 * NE - 1)
                scatter(0, NE - 1)

            def ada_columns(l):
                pe.wait_ge(s["ada_chain"], 4 * ADA_SLABS * (l + 1))
                for c in range(48):
                    ins = mm(bank[4][:, c:c + 1], ada_acc[:, c // 2, (c % 2) * P:(c % 2 + 1) * P], ones[:, 0:1],
                             start=True, stop=True)
                ins.then_inc(s["ada_sum"], 1)

            def gate_rows(run):
                pe.wait_ge(s["diag"], run)
                for half in range(2):
                    ins = mm(bank[4 + half][:, :], ones[:, :], diag[:, 4 * half:4 * half + 4, :], start=True, stop=True)
                ins.then_inc(s["gate_bc"], 1)

            pe.wait_ge(s["ident"], 1)
            pe.wait_ge(s["rows_in"], 16 * N_ROW_DMA)
            for t in range(2):
                tr(bank[0][:, t * P:(t + 1) * P], prow[:, t, :], ident[:, :])
            for l in range(LAYERS):
                ins = tr(bank[1][:, l * 48:(l + 1) * 48], abrow[0:48, l, :], ident[0:48, 0:48])
            ins.then_inc(s["prowT"], 1)
            turn(1)
            have_hT(1)
            pe.wait_ge(s["pcol"], 1)
            n1 = DFF // FB
            swiglu("ffn1", n1, 0)
            pe.wait_ge(s["ones"], 1)
            pe.wait_ge(s["x"], 1)
            ada_columns(0)
            pe.wait_ge(s["mod"], 1)
            turn(2)
            have_hT(2)
            by_token("mem_kv0", bank[0], memT)
            by_token("mem_kv1", bank[1], memT)
            turn(3)
            have_hT(3)
            by_feature("w_in0", bank[2])
            by_feature("w_in1", bank[3])
            by_feature("w_in2", bank[4])
            by_feature("w_in3", bank[5])
            by_token("w_in4", bank[6])
            by_token("w_in5", bank[7])
            pe.wait_ge(s["mem_k"], 1)
            by_token("w_in6", bank[0])
            pe.wait_ge(s["mem_v"], 1)
            by_token("w_in7", bank[1])
            pe.wait_ge(s["lru_w_in"], 16 * 4)
            pe.wait_ge(s["lru_xb"], 1)
            pe.wait_ge(s["xl"], 1)
            pe.wait_ge(s["gelu"], 1)
            for g in range(2):
                for c in range(LC):
                    ins = mm(bank[2 + 2 * g + c // 2][:, (c % 2) * SEQ:(c % 2 + 1) * SEQ], lru_w_all[:, g, c, :],
                             xb[:, c, :], start=True, stop=True)
            ins.then_inc(s["lru_gates"], 1)
            pe.wait_ge(s["qkn"], 1)
            pe.wait_ge(s["moba_v"], 1)
            pe.wait_ge(s["lru_ri"], 1)
            rows_ = xn[:, :, :].rearrange("p t d -> p (t d)")
            for w in range(4):
                for pair in range(2):
                    for t in range(T):
                        ins = tr(bank[w][:, pair * SEQ + t * P:pair * SEQ + (t + 1) * P],
                                 rows_[:, w * 512 + t * 256 + pair * P:w * 512 + t * 256 + (pair + 1) * P], ident[:, :])
            ins.then_inc(s["qkT"], 1)
            pe.wait_ge(s["qk_act"], 1)
            pe.wait_ge(s["qk_dve"], 1)
            for att in range(2):
                for t in range(T):
                    for par in range(2):
                        out = bank[4 - 4 * att + 2 * t + par]
                        for pair in range(2):
                            ins = mm(out[:, pair * SEQ:(pair + 1) * SEQ],
                                     qkT[par * HD:(par + 1) * HD, 2 * att, pair, t * P:(t + 1) * P],
                                     qkT[par * HD:(par + 1) * HD, 2 * att + 1, pair, :], start=True, stop=True)
                ins.then_inc(s["att_s"], 1)
            for att in range(2):
                pe.wait_ge(s["att_p"], att + 1)
                for h in range(4):
                    for t in range(T):
                        for kb in range(T):
                            ins = tr(bank[4 - 4 * att + h][:, kb * SEQ + t * P:kb * SEQ + (t + 1) * P],
                                     att_p[:, att * 8 + 2 * h + t, kb * P:(kb + 1) * P], ident[:, :])
                ins.then_inc(s["att_pT"], 1)
            for att, name in ((0, "moba"), (1, "mem")):
                pe.wait_ge(s[name + "_pT_out"], 1)
                for h in range(4):
                    for kb in range(T):
                        o = (h % 2) * HD
                        ins = mm(bank[4 - 4 * att][o:o + HD, (h // 2) * SEQ:(h // 2 + 1) * SEQ],
                                 v2[:, att, kb, h * HD:(h + 1) * HD], att_pT[:, att * 4 + h, kb, :],
                                 start=kb == 0, stop=kb == T - 1)
                ins.then_inc(s["att_pv"], 1)
            pe.wait_ge(s["mix_heads"], 1)
            pe.wait_ge(s["mix_lru"], 1)
            for n in range(4):
                rows_product(place[f"w_out{n}"], mixT[:, 2 * n:2 * n + 2, :], acc, n == 0, n == 3)
            turn(4)
            have_hT(4)
            swiglu("ffn2", n1, n1)
            pe.wait_ge(s["x"], 3)
            ada_columns(1)
            pe.wait_ge(s["mod"], 2)

            for l in range(LAYERS):
                run = l + 1
                turn(5 + 2 * l)
                have_hT(5 + 2 * l)
                by_feature(f"proj0.{l}", bank[0])
                by_feature(f"proj1.{l}", bank[1])
                by_feature(f"proj6.{l}", bank[2])
                by_feature(f"proj7.{l}", bank[3])
                by_feature(f"proj2.{l}", bank[4])
                by_feature(f"proj3.{l}", bank[5])
                by_token(f"proj4.{l}", bank[6])
                by_token(f"proj5.{l}", bank[7])
                pe.wait_ge(s["hq"], run)
                by_token(f"misc0.{l}", bank[0])
                by_token(f"misc1.{l}", bank[1])
                pe.wait_ge(s["hgate"], run)
                by_token(f"misc2.{l}", bank[2], n=MISC - 2 * FB)
                pe.wait_ge(s["latents"], run)
                for k in range(5):
                    for t in range(T):
                        ins = tr(bank[k // 2][:, (k % 2) * SEQ + t * P:(k % 2) * SEQ + (t + 1) * P],
                                 misc[:, t, k * P:(k + 1) * P], ident[:, :])
                ins.then_inc(s["cT"], 1)
                pe.wait_ge(s["cT_out"], run)
                pe.wait_ge(s["hf"], run)
                pe.wait_ge(s["vh"], run)
                for n in range(2):
                    pos = place[f"q_up{n}.{l}"]
                    landed(pos)
                    w = slot_view(pos, 3 * QL)
                    for t in range(T):
                        for k in range(3):
                            ins = mm(bank[4 + 2 * n + t][:, 0:QL], cT[:, k, t * P:(t + 1) * P], w[:, k, :],
                                     start=k == 0, stop=k == 2)
                    ins.then_inc(tiles_used, 1)
                pos = place[f"kv_up.{l}"]
                rows_product(pos, cT[:, 3:5, :], bank[0:4], True, True)
                pe.wait_ge(s["kv_out"], run)
                pe.wait_ge(s["q_out"], run)
                for n in range(9):
                    if n < 8:
                        if n >= 4:
                            pe.wait_ge(s["gates"], 8 * l + n - 3)
                        by_token(f"gates{n}.{l}", bank[n % 4])
                    if n == 0:
                        pe.wait_ge(s["hk"], run)
                        pe.wait_ge(s["hq"], run)
                        for t in range(T):
                            for h in range(HGH):
                                ins = mm(bank[4 + t][:, h * P:(h + 1) * P], hk[:, h, t * P:(t + 1) * P],
                                         hq[:, h, t * P:(t + 1) * P], start=True, stop=True)
                        ins.then_inc(s["level"], 1)
                        continue
                    pe.wait_ge(s["hy"], 8 * l + n)
                    y = hy[:, :].rearrange("p (h s) -> p h s", h=HGH)
                    if n < 8:
                        if n >= 2:
                            pe.wait_ge(s["level_added"], 9 * l + n - 1)
                        for t in range(T):
                            for h in range(HGH):
                                ins = mm(bank[4 + 2 * (n % 2) + t][:, h * P:(h + 1) * P], y[:, h, t * P:(t + 1) * P],
                                         y[:, h, t * P:(t + 1) * P], start=True, stop=True)
                    else:
                        pe.wait_ge(s["level_added"], 9 * l + n - 1)
                        for h in range(HGH):
                            ins = mm(bank[4][:, h * P:(h + 1) * P], y[:, h, 0:P], y[:, h, P:SEQ], start=True, stop=True)
                    ins.then_inc(s["level"], 1)
                pe.wait_ge(s["level_added"], 9 * l + 9)
                vh_ = vh[:, :, :].rearrange("p t (h c) -> p t h c", h=HGH)
                for h in range(HGH):
                    mm(bank[6][:, h * P:(h + 1) * P], attT[:, 0, h, :], vh_[:, 0, h, :], start=True, stop=True)
                for h in range(HGH):
                    mm(bank[7][:, h * P:(h + 1) * P], attT[:, 1, h, :], vh_[:, 1, h, :], start=True, stop=False)
                    ins = mm(bank[7][:, h * P:(h + 1) * P], attT[:, 2, h, :], vh_[:, 0, h, :], start=False, stop=True)
                ins.then_inc(s["hg_o"], 1)
                pe.wait_ge(s["gates"], 8 * l + 8)
                pe.wait_ge(s["k_rope"], run)
                for src, b0, ev in ((q96, 0, "mla_qT"), (k96, 4, "mla_kT")):
                    if b0:
                        pe.wait_ge(s["oa_rows"], run)
                    for h in range(MH):
                        for t in range(T):
                            ins = tr(bank[b0 + h // 2][0:DQK, (h % 2) * SEQ + t * P:(h % 2) * SEQ + (t + 1) * P],
                                     src[:, t, h, :], ident[:, :])
                    ins.then_inc(s[ev], 1)
                pe.wait_ge(s["qT_out"], run)
                pe.wait_ge(s["kT_out"], run)
                for h in range(HGH):
                    for t in range(T):
                        ins = tr(bank[4 + h // 2][:, (h % 2) * SEQ + t * P:(h % 2) * SEQ + (t + 1) * P],
                                 oa[:, t, h * P:(h + 1) * P], ident[:, :])
                ins.then_inc(s["oaT"], 1)
                for t in range(T):
                    if t:
                        pe.wait_ge(s["mla_max"], T * l + t)
                    for h in range(MH):
                        ins = mm(bank[h // 2][:, (h % 2) * SEQ:(h % 2 + 1) * SEQ], qT96[0:DQK, h, t * P:(t + 1) * P],
                                 kT96[0:DQK, h, :], start=True, stop=True)
                    ins.then_inc(s["mla_s"], 1)
                pe.wait_ge(s["oaT_out"], run)
                pe.wait_ge(s["mla_p"], run)
                for h in range(MH):
                    for t in range(T):
                        for kb in range(T):
                            ins = tr(bank[h][:, kb * SEQ + t * P:kb * SEQ + (t + 1) * P],
                                     mlp_p[:, t * 8 + h, kb * P:(kb + 1) * P], ident[:, :])
                ins.then_inc(s["mla_pT"], 1)
                pe.wait_ge(s["pT_act"], run)
                pe.wait_ge(s["pT_dve"], run)
                for h in range(MH):
                    for kb in range(T):
                        o = (h % 2) * MV
                        ins = mm(bank[h // 4][o:o + MV, (h // 2 % 2) * SEQ:(h // 2 % 2 + 1) * SEQ],
                                 vm[:, kb, h, :], mlp_pT[:, h, kb, :], start=kb == 0, stop=kb == T - 1)
                ins.then_inc(s["mla_pv"], 1)
                for n in range(2):
                    rows_product(place[f"br_a{n}.{l}"], oaT[:, 2 * n:2 * n + 2, :], bank[4:8], n == 0, n == 1)
                pe.wait_ge(s["ymT"], run)
                for n in range(2):
                    rows_product(place[f"br_b{n}.{l}"], ymT[:, 2 * n:2 * n + 2, :], acc, n == 0, n == 1)
                pe.wait_ge(s["merged"], run)
                for k in range(KC):
                    for t in range(T):
                        ins = tr(bank[4 + k // 2][:, (k % 2) * SEQ + t * P:(k % 2) * SEQ + (t + 1) * P],
                                 merged[:, t, k * P:(k + 1) * P], ident[:, :])
                ins.then_inc(s["mergedT"], 1)
                pe.wait_ge(s["mT_act"], run)
                pe.wait_ge(s["mT_dve"], run)
                gate_rows(2 * l + 1)
                for n in range(4):
                    rows_product(place[f"w_out{n}.{l}"], hT[:, 2 * n:2 * n + 2, :], acc, n == 0, n == 3)

                turn(6 + 2 * l)
                have_hT(6 + 2 * l)
                gate_rows(2 * l + 2)
                pe.wait_ge(s["router_in"], 32)
                for t in range(T):
                    for k in range(KC):
                        ins = mm(bank[0][:, t * NE:(t + 1) * NE], hT[:, k, t * P:(t + 1) * P], router[:, k, :],
                                 start=k == 0, stop=k == KC - 1)
                ins.then_inc(s["logits"], 1)
                pe.wait_ge(s["member"], run)
                pe.wait_ge(s["slot_patterns"], run)
                member = rt[:, 14, :]
                mm(bank[1][:, 0:NE], before, member[:, 0:NE], start=True, stop=True)
                mm(bank[1][:, NE:2 * NE], before, member[:, NE:2 * NE], start=True, stop=False)
                mm(bank[1][:, NE:2 * NE], ones[:, :], member[:, 0:NE], start=False, stop=True)
                mm(bank[1][:, 2 * NE:3 * NE], ones[:, :], member[:, 0:NE], start=True, stop=False)
                mm(bank[1][:, 2 * NE:3 * NE], ones[:, :], member[:, NE:2 * NE], start=False, stop=True)\
                    .then_inc(s["counts"], 1)
                pe.wait_ge(s["overflow"], run)
                pe.wait_ge(s["combine"], run)
                pe.wait_ge(s["gbc"], 2 * l + 2)
                full = pe.value_load(overflow[0:1, 0:1], min_val=0, max_val=1)
                base = 2 * n1 + 2 * NE * l
                with pe.If(full):
                    for t in range(T):
                        ins = tr(bank[1][0:NE, t * P:(t + 1) * P], rt[:, 15, t * NE:(t + 1) * NE], ident[:, :])
                    ins.then_inc(s[f"combineT.{l}"], 1)
                    pe.wait_ge(s[f"combT.{l}"], 1)
                    for e in range(NE):
                        ins = mm(bank[e // 2][:, (e % 2) * SEQ:(e % 2 + 1) * SEQ], sel[0:NE, e, :], combT[:, :],
                                 start=True, stop=True)
                    ins.then_inc(s[f"combine_bc.{l}"], 1)
                    pe.wait_ge(s[f"cb_act.{l}"], 1)
                    pe.wait_ge(s[f"cb_dve.{l}"], 1)
                    swiglu(f"moe.{l}", 2 * NE, base)
                    if l < LAYERS - 1:
                        for name, n in SLOT_COUNTS["pe"]:
                            pe.sem_inc(s[name], n)
                with pe.Else():
                    sparse(l)

        @block.vector
        def _(v):
            done = [0]

            def link(ins):
                done[0] += 1
                ins.then_inc(s["dve_chain"], 1)
                v.wait_ge(s["dve_chain"], done[0])

            ts, tt, stt, cp = v.tensor_scalar, v.tensor_tensor, v.scalar_tensor_tensor, v.tensor_copy
            M, AD = ALU.mult, ALU.add

            def used(name):
                v.wait_ge(tiles_used, place[name] + 1)

            roots = [0]

            def inverse_root(n, width):
                roots[0] += 1
                ts(stat[:, 1, 0:n], stat[:, 0, 0:n], 1.0 / width, EPS, M, AD).then_inc(s["ms"], 1)
                v.wait_ge(s["root"], roots[0])
                link(v.reciprocal(stat[:, 3, 0:n], stat[:, 2, 0:n]))
                link(tt(stat[:, 6, 0:n], stat[:, 3, 0:n], stat[:, 3, 0:n], M))
                link(tt(stat[:, 6, 0:n], stat[:, 6, 0:n], stat[:, 1, 0:n], M))
                link(ts(stat[:, 6, 0:n], stat[:, 6, 0:n], -0.5, 1.5, M, AD))
                link(tt(stat[:, 3, 0:n], stat[:, 3, 0:n], stat[:, 6, 0:n], M))

            def normalise(src, dst):
                for t in range(T):
                    ins = v.tensor_tensor_reduce(dst[:, t, :], src[:, t, :], src[:, t, :], 1.0, 0.0, M, AD,
                                                 stat[:, 0, t:t + 1])
                link(ins)
                inverse_root(T, D)
                for t in range(T):
                    ins = ts(dst[:, t, :], src[:, t, :], stat[:, 3, t:t + 1], None, M)
                return ins

            def turn(run, dst, scale, bias):
                v.wait_ge(s["xnT"], run)
                for k in range(KC // 2, KC):
                    src = bank[4 + k // 2][:, (k % 2) * SEQ:(k % 2 + 1) * SEQ]
                    if bias:
                        ins = ts(dst[:, k, :], src, scale(k), bias(k), M, AD)
                    else:
                        ins = ts(dst[:, k, :], src, scale(k), None, M)
                ins.then_inc(s["hT_dve"], 1)

            def gain(name, off=0):
                return lambda k: col(name, off + k)

            def swiglu(name, n, base, weighted=""):
                pos = place[name]

                def step(i, c, late=True):
                    j, p = 2 * i + c, c % 2
                    v.wait_ge(s["silu"], j + (base + 1))
                    v.wait_ge(tiles_used, RING * i + (pos + (0 if c == 0 else 3 * c - 1) + 2))
                    if late:
                        v.wait_ge(tiles_used, RING * i + (pos + 3 * (c - 2) + 4 + 1))
                    if not weighted:
                        tt(small_b[:, p, :], small_a[:, p, :], bank[5 + 2 * p][:, :], M).then_inc(s["hidden"], 1)
                    else:
                        tt(ep[:, p, :], small_a[:, p, :], bank[5 + 2 * p][:, :], M).then_inc(s["unweighted" + weighted], 1)
                        v.wait_ge(s["unweighted" + weighted], j + 1)
                        e = cb[:, bass.ds(i + c // 2, 1), :].broadcast_to([P, 2, SEQ])
                        tt(small_b[:, p, :].rearrange("p (k s) -> p k s", k=2),
                           ep[:, p, :].rearrange("p (k s) -> p k s", k=2), e, M).then_inc(s["hidden"], 1)

                j0, turns = loop_shape(n)
                for c in range(j0):
                    step(0, c, c >= 2)
                with v.Fori(0, turns) as i:
                    step(i, j0)
                    step(i, j0 + 1)
                v.wait_ge(tiles_used, pos + 3 * n)

            def sparse(l):
                pos0 = place[f"moe.{l}"]
                base = 2 * (DFF // FB) + 2 * NE * l
                slots = slot_no.rearrange("p (t e) -> p t e", t=T)

                def step(i, c):
                    p = c % 2
                    v.wait_ge(s["silu"], 4 * i + (base + c + 1))
                    if c >= 2:
                        v.wait_ge(tiles_used, 2 * RING * i + (pos0 + expert_pos("down", c - 2) + 1))
                    tt(small_b[:, p, 0:2 * P], small_a[:, p, 0:2 * P], bank[4 + p][:, 2 * P:4 * P], M)\
                        .then_inc(s["hidden"], 1)

                def picks(i, g):
                    if g:
                        v.wait_ge(s["weights"], i + (8 * l + g))
                    for t in range(T):
                        ins = tt(pick[:, t], slot_row.unsqueeze(1).broadcast_to([P, 2, P]),
                                 slots[:, t, bass.ds(2 * i + 2 * g, 2)].unsqueeze(2).broadcast_to([P, 2, P]), ALU.is_equal)
                    ins.then_inc(s["pick"], 1)

                def puts(i, e):
                    if e < 2:
                        v.wait_ge(s["pos_out"], 8 * l + 8)
                    else:
                        v.wait_ge(s["scattered"], 2 * i + (16 * l + e - 1))
                    ts(put[:, e % 2, :], pos_bc[:, bass.ds(2 * i + e, 1), :], slot_col[:, 0:1], None, ALU.is_equal)\
                        .then_inc(s["put"], 1)

                def gathered(i, g):
                    for r in (1, 3):
                        v.wait_ge(s["gathered"], 4 * i + (32 * l + 4 * g + r + 1))
                        for k in (2 * r, 2 * r + 1):
                            ins = ts(hT[:, k, :], bank[7][:, (k % 2) * SEQ:(k % 2 + 1) * SEQ], scol[:, l, 1, k:k + 1],
                                     modc[:, l, 24 + k:25 + k], M, AD)
                        ins.then_inc(s["xg_dve"], 1)
                    v.wait_ge(s["weights"], i + (8 * l + g + 1))
                    if g:
                        v.wait_ge(s["w_slot"], i + (8 * l + g))
                    cp(w_next[:, 0:2], bank[6][:, 0:2]).then_inc(s["w_next"], 1)

                def ye(i, e):
                    v.wait_ge(s["ye_hi"], 2 * i + (16 * l + e + 1))
                    if e:
                        v.wait_ge(s["scattered"], 2 * i + (16 * l + e))
                    for half in range(2):
                        c = slice(half * 512, (half + 1) * 512)
                        ins = stt(ye_parts[:, 1, c], bank[6 + half][:, :], w_slot[:, e % 2:e % 2 + 1],
                                  ye_parts[:, 0, c].bitcast(F32), M, ALU.subtract)
                    ins.then_inc(s["ye_lo"], 1)

                def weights(i, g):
                    v.wait_ge(s["w_next"], i + (8 * l + g + 1))
                    if g:
                        v.wait_ge(s["ye_lo"], 2 * i + (16 * l + 2 * g))
                    cp(w_slot[:, 0:2], w_next[:, 0:2]).then_inc(s["w_slot"], 1)
                    v.wait_ge(s["w_slot"], i + (8 * l + g + 1))

                def pair(i, g, start=False, last=False):
                    step(i, 4 * g)
                    if not start:
                        ye(i, 2 * g - 1)
                    weights(i, g)
                    step(i, 4 * g + 1)
                    if not last:
                        picks(i, g + 1)
                    puts(i, 2 * g)
                    step(i, 4 * g + 2)
                    puts(i, 2 * g + 1)
                    ye(i, 2 * g)
                    step(i, 4 * g + 3)
                    if not last:
                        gathered(i, g + 1)

                picks(0, 0)
                v.wait_ge(s["pos_turned"], l + 1)
                v.wait_ge(s["sel"], l + 1)
                cp(posT[0:NE, :], bank[2][0:NE, 0:SEQ]).then_inc(s["posT"], 1)
                gathered(0, 0)
                pair(0, 0, start=True)
                with v.Fori(0, NE // 2 - 2) as i:
                    pair(i, 1)
                pair(0, NE // 2 - 1, last=True)
                ye(0, NE - 1)
                v.wait_ge(s["scattered"], 16 * l + NE)

            def add_to_x(scale):
                for t in range(T):
                    for half in range(2):
                        xs = x[:, t, half * 512:(half + 1) * 512]
                        ins = stt(xs, acc[2 * t + half][:, :], scale, xs, M, AD)
                ins.then_inc(s["x"], 1)

            def add_gated_to_x():
                for t in range(T):
                    for half in range(2):
                        ins = tt(xn[:, t, half * 512:(half + 1) * 512], acc[2 * t + half][:, :],
                                 gbc[:, half * 512:(half + 1) * 512], M)
                link(ins)
                tt(x[:, :, :], x[:, :, :], xn[:, :, :], AD).then_inc(s["x"], 1)

            def modulation(l):
                v.wait_ge(s["ada_sum"], l + 1)
                link(tt(modc[:, l, :], bank[4][:, 0:48], abcol[:, l, :], AD))
                stt(scol[:, l, 0, :], modc[:, l, 8:16], 1.0, col("n1", 8 * l, 8), AD, M)
                stt(scol[:, l, 1, :], modc[:, l, 32:40], 1.0, col("n2", 8 * l, 8), AD, M).then_inc(s["mod"], 1)
                v.wait_ge(s["mod"], l + 1)

            def gate_diag(l, c0):
                tt(diag[:, :, :], ident[:, :].unsqueeze(1).broadcast_to([P, KC, P]),
                   modc[:, l, c0:c0 + KC].unsqueeze(2).broadcast_to([P, KC, P]), M).then_inc(s["diag"], 1)

            def gate_copy(run, scale):
                v.wait_ge(s["gate_bc"], run)
                for half in range(2):
                    ins = ts(gbc[:, half * 512:(half + 1) * 512], bank[4 + half][:, :], scale, None, M)
                ins.then_inc(s["gbc"], 1)

            def negative_max(src, r0, n, scale):
                link(v.tensor_reduce(stat[:, 7, r0:r0 + n], src, AX.X, ALU.max))
                return ts(stat[:, 4, r0:r0 + n], stat[:, 7, r0:r0 + n], -scale, None, M)

            link(v.memset(stat[:, :, :], 1.0))
            v.memset(ones[:, :], 1.0).then_inc(s["ones"], 1)
            v.memset(prow[:, :, :], 0.0).then_inc(s["prow_zero"], 1)
            v.memset(lru_w_all[:, :, :, :], 0.0).then_inc(s["lru_w_zero"], 1)
            v.wait_ge(s["x_in"], 16)
            normalise(x, xn).then_inc(s["xn"], 1)
            v.wait_ge(s["prowT"], 1)
            cp(pcol[:, :, :].rearrange("p a b -> p (a b)"), bank[0][:, 0:2 * P])
            cp(abcol[:, :, :].rearrange("p a b -> p (a b)"), bank[1][:, 0:LAYERS * 48]).then_inc(s["pcol"], 1)
            v.wait_ge(s["pcol"], 1)
            l0, l1 = col("lb", 0, 4), col("lb", 4, 4)
            link(tt(lbc[:, 4, :], l0, l1, ALU.max))
            tt(lbc[:, 0, :], l0, lbc[:, 4, :], ALU.subtract)
            tt(lbc[:, 1, :], l1, lbc[:, 4, :], ALU.subtract)
            link(ts(lruc[:, 0, :], col("lam", 0, 4), -1.0, None, M))
            tt(lruc[:, 1, :], lruc[:, 0, :], col("lam", 0, 4), ALU.max).then_inc(s["small_in"], 1)
            v.wait_ge(s["inv_freq"], 1)
            v.wait_ge(s["pos_in"], 16)
            link(cp(stat[:, 7, 0:T], pos_i[:, :]))
            for t in range(T):
                ins = ts(rope_t[:, 1, t, :], rope_t[:, 0, 0, :], stat[:, 7, t:t + 1], None, M)
            link(ins)
            two_pi = 2 * np.pi
            c1 = 6.28125
            c2 = np.floor((two_pi - c1) * 2 ** 21) / 2 ** 21
            c3 = two_pi - c1 - c2
            for n, quarter in ((0, 0.25), (1, 0.0)):
                link(ts(rope_t[:, 2], rope_t[:, 1], 1 / two_pi, quarter, M, AD))
                link(cp(rope_t[:, 3].bitcast(I32), rope_t[:, 2]))
                link(cp(rope_t[:, 2], rope_t[:, 3].bitcast(I32)))
                link(stt(rope_t[:, 4], rope_t[:, 2], -c1, rope_t[:, 1], M, AD))
                link(stt(rope_t[:, 5], rope_t[:, 2], -c2, rope_t[:, 4], M, AD))
                link(stt(rope_t[:, 6], rope_t[:, 2], -c3, rope_t[:, 5], M, AD))
                link(ts(rope_t[:, 7], rope_t[:, 6], quarter * two_pi, 3.1415925, AD, ALU.min))
                link(ts(rope_t[:, 8 + n], rope_t[:, 7], -3.1415925, None, ALU.max))
            cp(stat[:, 6, 0:1], stat[:, 7, 0:1]).then_inc(s["angles"], 1)
            v.wait_ge(s["small_exp"], 1)
            link(tt(lbc[:, 4, :], lbc[:, 2, :], lbc[:, 3, :], AD))
            link(v.reciprocal(lbc[:, 4, :], lbc[:, 4, :]))
            tt(lbc[:, 2, :], lbc[:, 2, :], lbc[:, 4, :], M)
            link(tt(lbc[:, 3, :], lbc[:, 3, :], lbc[:, 4, :], M))
            link(tt(lbc[:, 5, :], lbc[:, 2, :], lbc[:, 3, :], AD))
            tt(lbc[:, 0, :], lbc[:, 2, :], lbc[:, 2, :], ALU.subtract)
            link(tt(lbc[:, 1, :], lbc[:, 5, :], lbc[:, 2, :], ALU.subtract))
            for l in range(LAYERS):
                link(ts(lbc[:, 6 + l, :], lbc[:, l, :], -1.0, 1.0, M, AD))
            link(ts(lruc[:, 3, :], lruc[:, 2, :], 2.0, None, AD))
            link(v.reciprocal(lruc[:, 3, :], lruc[:, 3, :]))
            link(tt(lruc[:, 3, :], lruc[:, 2, :], lruc[:, 3, :], M))
            link(tt(lruc[:, 4, :], lruc[:, 3, :], lruc[:, 3, :], M))
            link(ts(lruc[:, 5, :], lruc[:, 4, :], 1.0 / 21, None, M))
            for n in range(19, 2, -2):
                link(stt(lruc[:, 5, :], lruc[:, 5, :], 1.0 / n, lruc[:, 4, :], AD, M))
            link(stt(lruc[:, 6, :], lruc[:, 5, :], 1.0, lruc[:, 3, :], AD, M))
            link(ts(lruc[:, 7, :], lruc[:, 0, :], 0.0, None, ALU.max))
            link(stt(lruc[:, 5, :], lruc[:, 6, :], 2.0, lruc[:, 7, :], M, AD))
            ts(lruc[:, 8, :], lruc[:, 5, :], -LRU_C, None, M)
            link(ts(lruc[:, 9, :], lruc[:, 5, :], LRU_C, None, M))
            turn(1, hT, gain("ffn1"), None)
            v.wait_ge(s["patterns"], 1)
            v.wait_ge(s["ident"], 1)
            scale = DK ** -0.5
            ts(rank[:, :], iot[:, 1, 0:NE], -1.0, float(NE), M, AD)
            link(tt(iot[:, 2, :], iot[:, 0, :], iot[:, 1, :], ALU.bitwise_xor))
            link(tt(diag[:, 0, :], iot[:, 1, :], iot[:, 0, :], ALU.is_gt))
            for n, L in enumerate(LEVELS[:-1]):
                link(ts(diag[:, 1, :], iot[:, 2, :], float(L), scale, ALU.is_ge, M))
                link(stt(diag[:, 2, :], iot[:, 2, :], float(2 * L), diag[:, 1, :], ALU.is_lt, M))
                link(tt(level_mask[:, n, :], diag[:, 2, :], diag[:, 0, :], M))
            link(ts(level_mask[:, 7, :], ident[:, :], scale, None, M))
            idx, low = view(22000, 1028).bitcast(I32), view(23100, 1028).bitcast(I32)
            for n, L in enumerate(LEVELS):
                link(ts(low, idx, L - 1, None, ALU.bitwise_and))
                link(ts(seg[:, n, :], low, 0.0, None, ALU.is_gt))
            v.wait_ge(s["mem_in"], 16)
            v.wait_ge(s["xnT"], 1)
            normalise(memx, xn).then_inc(s["xn"], 1)

            n1 = DFF // FB
            swiglu("ffn1", n1, 0)
            add_to_x(0.5)
            v.wait_ge(s["x"], 1)
            modulation(0)
            turn(2, memT, gain("mem"), None)
            normalise(x, xn).then_inc(s["xn"], 1)
            used("mem_kv0")
            cp(qk4[:, 3, :], bank[0][:, :]).then_inc(s["mem_k"], 1)
            turn(3, hT, gain("mix"), None)
            used("mem_kv1")
            v.memset(xl[:, :, 0:3], 0.0).then_inc(s["xl_zero"], 1)
            v.wait_ge(s["xl"], 1)
            for j in range(4):
                for c in range(LC):
                    w = col("convw", 4 * j + c)
                    if j == 0:
                        ins = ts(xb[:, c, :], xl[:, c, 0:SEQ], w, col("convb", c), M, AD)
                    else:
                        ins = stt(xb[:, c, :], xl[:, c, j:j + SEQ], w, xb[:, c, :], M, AD)
                if j < 3:
                    link(ins)
            ins.then_inc(s["lru_xb"], 1)
            used("w_in4")
            cp(qk4[:, 0, :], bank[6][:, :])
            used("w_in5")
            cp(qk4[:, 1, :], bank[7][:, :])
            used("w_in7")
            link(cp(qk4[:, 2, :], bank[1][:, :]))
            rows_ = xn[:, :, :].rearrange("p t d -> p (t d)")
            qk_flat = qk4[:, :, :].rearrange("p w c -> p (w c)")
            link(tt(rows_, qk_flat, qk_flat, M))
            link(v.tensor_reduce(stat[:, 0, 0:32], rows_.rearrange("p (r c) -> p r c", c=HD), AX.X, AD))
            inverse_root(32, HD)
            tt(rows_.rearrange("p (r c) -> p r c", c=HD), qk_flat.rearrange("p (r c) -> p r c", c=HD),
               stat[:, 3, 0:32].unsqueeze(2).broadcast_to([P, 32, HD]), M).then_inc(s["qkn"], 1)
            v.wait_ge(s["lru_a"], 1)
            sc = small_a[:, :, :].rearrange("p a b -> p (a b)")
            lt_flat = lt[:, :, :].rearrange("p c s -> p (c s)")
            link(ts(sc, lt_flat, 1.0, None, AD))
            link(v.reciprocal(sc, sc))
            link(tt(sc, sc, lt_flat, M))
            ts(lt_flat, sc, 1.0e-30, None, ALU.max).then_inc(s["lru_m2"], 1)
            v.wait_ge(s["qkT"], 1)
            for w in range(2, 4):
                ins = ts(qkT[:, w].rearrange("p a b -> p (a b)"), bank[w][:, :], col("heads", w), None, M)
            ins.then_inc(s["qk_dve"], 1)
            v.wait_ge(s["att_s"], 1)
            for h in range(4):
                slope = 2.0 ** (-8.0 * (h + 1) / 4)
                for t in range(T):
                    ins = stt(att_p[:, 2 * h + t, :], dist[:, t, :], -slope / HD ** -0.5,
                              bank[4 + 2 * t + h % 2][:, (h // 2) * SEQ:(h // 2 + 1) * SEQ], M, AD)
            link(ins)
            negative_max(att_p[:, 0:8, :], 0, 8, HD ** -0.5).then_inc(s["att_max"], 1)
            v.wait_ge(s["att_s"], 2)
            for t in range(T):
                for par in range(2):
                    for pair in range(2):
                        h = 2 * pair + par
                        ins = v.tensor_reduce(stat[:, 7, 8 + 2 * h + t:9 + 2 * h + t],
                                              bank[2 * t + par][:, pair * SEQ:(pair + 1) * SEQ], AX.X, ALU.max)
            link(ins)
            ts(stat[:, 4, 8:16], stat[:, 7, 8:16], -HD ** -0.5, None, M).then_inc(s["att_max"], 1)
            v.wait_ge(s["lru_mult"], 1)
            v.memset(lt[:, :, 0:1], 1.0)
            v.memset(lt2[:, :, 0:1], 0.0)
            link(tt(li[:, :, :], li[:, :, :], xb[:, :, :], M))
            link(tt(li[:, :, :], li[:, :, :], lt[:, :, :], M))
            link(v.tensor_tensor_scan(lt_flat, lt2[:, :, :].rearrange("p c s -> p (c s)"),
                                      li[:, :, :].rearrange("p c s -> p (c s)"), 0.0, M, AD))
            tt(mixT[:, 0:4, :], lt[:, :, :], gel[:, :, :], M).then_inc(s["mix_lru"], 1)
            for att in range(2):
                v.wait_ge(s["att_exp"], att + 1)
                link(v.reciprocal(stat[:, 6, 8 * att:8 * att + 8], stat[:, 5, 8 * att:8 * att + 8]))
                for r in range(8 * att, 8 * att + 8):
                    ins = ts(att_p[:, r, :], att_p[:, r, :], stat[:, 6, r:r + 1], None, M)
                ins.then_inc(s["att_p"], 1)
            v.wait_ge(s["att_pT"], 2)
            for h in range(4):
                ins = cp(att_pT[:, 4 + h].rearrange("p a b -> p (a b)"), bank[h][:, :])
            ins.then_inc(s["mem_pT_out"], 1)
            used("w_out3")
            add_to_x(1.0)
            v.wait_ge(s["x"], 2)
            normalise(x, xn).then_inc(s["xn"], 1)
            turn(4, hT, gain("ffn2"), None)
            swiglu("ffn2", n1, n1)
            add_to_x(0.5)
            v.wait_ge(s["x"], 3)
            modulation(1)

            for l in range(LAYERS):
                run = l + 1
                normalise(x, xn).then_inc(s["xn"], 1)
                turn(5 + 2 * l, hT, lambda k: scol[:, l, 0, k:k + 1], lambda k: modc[:, l, k:k + 1])
                v.wait_ge(s["hf"], run)
                for h in range(HGH):
                    ins = ts(hf[:, h, :], hf[:, h, :], lbc[:, 6 + l, h:h + 1], lbc[:, l, h:h + 1], M, AD)
                link(ins)
                ts(hg[:, :, :], hf[:, :, :], 1.0e-19, None, ALU.max).then_inc(s["hf_clamped"], 1)
                ts(hk[:, :, :], hf[:, :, :], -1.0, 1.0, M, AD).then_inc(s["hk"], 1)
                for n in range(2):
                    used(f"proj{4 + n}.{l}")
                    ins = cp(vh[:, :, n * FB:(n + 1) * FB], bank[6 + n][:, :].rearrange("p (t c) -> p t c", t=T))
                ins.then_inc(s["vh"], 1)
                v.wait_ge(s["misc"], run)
                for t in range(T):
                    v.tensor_tensor_reduce(scr[:, 0:QL], misc[:, t, 0:QL], misc[:, t, 0:QL], 1.0, 0.0, M, AD,
                                           stat[:, 0, t:t + 1])
                    ins = v.tensor_tensor_reduce(scr[:, QL:QL + KVL], misc[:, t, QL:QL + KVL], misc[:, t, QL:QL + KVL],
                                                 1.0, 0.0, M, AD, stat[:, 0, 2 + t:3 + t])
                    link(ins)
                link(ts(stat[:, 0, 2:4], stat[:, 0, 2:4], QL / KVL, None, M))
                inverse_root(4, QL)
                for t in range(T):
                    ts(misc[:, t, 0:QL], misc[:, t, 0:QL], stat[:, 3, t:t + 1], None, M)
                    ins = ts(misc[:, t, QL:QL + KVL], misc[:, t, QL:QL + KVL], stat[:, 3, 2 + t:3 + t], None, M)
                ins.then_inc(s["latents"], 1)
                v.wait_ge(s["sincos"], 1)
                half = ROPE // 2
                cos, sin = rope_t[:, 10], rope_t[:, 11]
                k1, k2 = misc[:, :, QL + KVL:QL + KVL + half], misc[:, :, QL + KVL + half:MISC]
                tmp = [scr[:, 256 * n:256 * n + 256] for n in range(4)]
                small = [z[:, 0:T * half].rearrange("p (t c) -> p t c", t=T) for z in tmp]
                tt(small[0], k1, cos, M)
                tt(small[1], k2, sin, M)
                tt(small[2], k1, sin, M)
                link(tt(small[3], k2, cos, M))
                tt(small[0], small[0], small[1], ALU.subtract)
                link(tt(small[2], small[2], small[3], AD))
                for t in range(T):
                    cp(k96[:, t, :, NOPE:NOPE + half], small[0][:, t:t + 1, :].broadcast_to([P, MH, half]))
                    ins = cp(k96[:, t, :, NOPE + half:DQK], small[2][:, t:t + 1, :].broadcast_to([P, MH, half]))
                ins.then_inc(s["k_rope"], 1)
                v.wait_ge(s["k_rope"], run)
                for n in range(2):
                    used(f"q_up{n}.{l}")
                    for t in range(T):
                        ins = cp(q96[:, t, 4 * n:4 * n + 4, :].rearrange("p h c -> p (h c)"), bank[4 + 2 * n + t][:, 0:QL])
                link(ins)
                big = [z.rearrange("p (t h c) -> p t h c", t=T, h=MH) for z in tmp]
                for t in range(T):
                    q1, q2 = q96[:, t, :, NOPE:NOPE + half], q96[:, t, :, NOPE + half:DQK]
                    cb_ = cos[:, t:t + 1, :].broadcast_to([P, MH, half])
                    sb_ = sin[:, t:t + 1, :].broadcast_to([P, MH, half])
                    tt(big[0][:, t], q1, cb_, M)
                    tt(big[1][:, t], q2, sb_, M)
                    tt(big[2][:, t], q1, sb_, M)
                    ins = tt(big[3][:, t], q2, cb_, M)
                link(ins)
                for t in range(T):
                    tt(q96[:, t, :, NOPE:NOPE + half], big[0][:, t], big[1][:, t], ALU.subtract)
                    ins = tt(q96[:, t, :, NOPE + half:DQK], big[2][:, t], big[3][:, t], AD)
                ins.then_inc(s["q_out"], 1)
                v.wait_ge(s["hg"], run)
                v.wait_ge(s["hq"], run)
                g_flat = hg[:, :, :].rearrange("p h s -> p (h s)")
                N = HGH * SEQ

                def add_level(n, mask):
                    v.wait_ge(s["level"], 9 * l + n + 1)
                    m = level_mask[:, mask, :].unsqueeze(1).broadcast_to([P, HGH, P])
                    for t in range(T):
                        src = bank[4 + 2 * (n % 2) + t][:, :].rearrange("p (h c) -> p h c", h=HGH)
                        if n == 0:
                            ins = tt(attT[:, t], src, m, M)
                        else:
                            link(tt(prod[:, t], src, m, M))
                            ins = tt(attT[:, t], attT[:, t], prod[:, t], AD)
                    ins.then_inc(s["level_added"], 1)
                    v.wait_ge(s["level_added"], 9 * l + n + 1)

                for n, L in enumerate(LEVELS):
                    if n:
                        v.wait_ge(s["decay"], 8 * l + n)
                    v.tensor_tensor_scan(scan_f[:, :], seg[:, n, 0:N], g_flat, 0.0, M, AD)
                    v.tensor_tensor_scan(scan_b[:, N - 2::-1], g_flat[:, N - 1:0:-1], seg[:, n, N - 1:0:-1], 0.0, AD, M)\
                        .then_inc(s["scans"], 1)
                    if n:
                        v.wait_ge(s["level"], 9 * l + n + 1)
                        add_level(n, n - 1)
                    else:
                        add_level(0, 7)
                    v.wait_ge(s["decay"], 8 * l + n + 1)
                    by = lambda z: z.rearrange("p (m two c) -> p m two c", two=2, c=L)
                    dec = by(hf[:, :, :].rearrange("p h s -> p (h s)"))
                    y = by(hy[:, :])
                    tt(y[:, :, 1, :], dec[:, :, 1, :], by(hq[:, :, :].rearrange("p h s -> p (h s)"))[:, :, 1, :], M)
                    tt(y[:, :, 0, :], dec[:, :, 0, :], by(hk[:, :, :].rearrange("p h s -> p (h s)"))[:, :, 0, :], M)\
                        .then_inc(s["hy"], 1)
                v.wait_ge(s["level"], 9 * l + 9)
                ts(attT[:, 2], bank[4][:, :].rearrange("p (h c) -> p h c", h=HGH), scale, None, M)\
                    .then_inc(s["level_added"], 1)
                v.wait_ge(s["hg_o"], run)
                for t in range(T):
                    ins = cp(oa[:, t, :], bank[6 + t][:, :])
                link(ins)
                sq = oa_sq[:, :]
                oa_flat = oa[:, :, :].rearrange("p t c -> p (t c)")
                link(tt(sq, oa_flat, oa_flat, M))
                link(v.tensor_reduce(stat[:, 0, 0:8], sq.rearrange("p (r c) -> p r c", c=P), AX.X, AD))
                inverse_root(8, DK)
                tt(oa_flat.rearrange("p (r c) -> p r c", c=P), oa_flat.rearrange("p (r c) -> p r c", c=P),
                   stat[:, 3, 0:8].unsqueeze(2).broadcast_to([P, 8, P]), M).then_inc(s["oa_rows"], 1)
                v.wait_ge(s["mla_kT"], run)
                for n in range(4):
                    ins = cp(kT96[0:DQK, 2 * n:2 * n + 2, :].rearrange("p h s -> p (h s)"), bank[4 + n][0:DQK, :])
                ins.then_inc(s["kT_out"], 1)
                v.wait_ge(s["hgate"], run)
                v.wait_ge(s["oaT"], run)
                for h in range(HGH):
                    ins = stt(oaT[:, h, :], bank[4 + h // 2][:, (h % 2) * SEQ:(h % 2 + 1) * SEQ], col("hgn", 4 * l + h),
                              hgate[:, h, :], M, M)
                ins.then_inc(s["oaT_out"], 1)
                for t in range(T):
                    v.wait_ge(s["mla_s"], T * l + t + 1)
                    for n in range(4):
                        ins = tt(mlp_p[:, 8 * t + 2 * n:8 * t + 2 * n + 2, :],
                                 bank[n][:, :].rearrange("p (h c) -> p h c", h=2),
                                 mla_mask[:, t:t + 1, :].broadcast_to([P, 2, SEQ]), AD)
                    link(ins)
                    negative_max(mlp_p[:, 8 * t:8 * t + 8, :], 8 * t, 8, DQK ** -0.5).then_inc(s["mla_max"], 1)
                v.wait_ge(s["mla_exp"], T * (l + 1))
                link(v.reciprocal(stat[:, 6, 0:16], stat[:, 5, 0:16]))
                for r in range(16):
                    ins = ts(mlp_p[:, r, :], mlp_p[:, r, :], stat[:, 6, r:r + 1], None, M)
                ins.then_inc(s["mla_p"], 1)
                v.wait_ge(s["mla_pT"], run)
                for h in range(4, MH):
                    ins = cp(mlp_pT[:, h].rearrange("p a b -> p (a b)"), bank[h][:, :])
                ins.then_inc(s["pT_dve"], 1)
                used(f"br_a1.{l}")
                for t in range(T):
                    for half_ in range(2):
                        c = slice(half_ * 512, half_ * 512 + 512)
                        ins = stt(merged[:, t, c], G[:, t, 0, c], 1.0, bank[4 + 2 * t + half_][:, :], AD, M)
                link(ins)
                used(f"br_b1.{l}")
                for t in range(T):
                    for half_ in range(2):
                        c = slice(half_ * 512, half_ * 512 + 512)
                        ins = stt(xn[:, t, c], G[:, t, 1, c], 1.0, acc[2 * t + half_][:, :], AD, M)
                link(ins)
                tt(merged[:, :, :], merged[:, :, :], xn[:, :, :], AD).then_inc(s["merged"], 1)
                gate_diag(l, 16)
                v.wait_ge(s["mergedT"], run)
                for k in range(KC // 2, KC):
                    ins = cp(hT[:, k, :], bank[4 + k // 2][:, (k % 2) * SEQ:(k % 2 + 1) * SEQ])
                ins.then_inc(s["mT_dve"], 1)
                gate_copy(2 * l + 1, 0.5)
                used(f"w_out3.{l}")
                v.wait_ge(s["gbc"], 2 * l + 1)
                add_gated_to_x()
                v.wait_ge(s["x"], 4 + 2 * l)

                normalise(x, xn).then_inc(s["xn"], 1)
                gate_diag(l, 40)
                cp(sel_r[0:NE, :, :], ident[0:NE, 0:NE].unsqueeze(2).broadcast_to([NE, NE, P])).then_inc(s["sel"], 1)
                turn(6 + 2 * l, hT, lambda k: scol[:, l, 1, k:k + 1], lambda k: modc[:, l, 24 + k:25 + k])
                gate_copy(2 * l + 2, 1.0)
                v.wait_ge(s["scores"], run)
                v.wait_ge(s["slot_patterns"], run)

                def r(n):
                    return rt[:, n, :].rearrange("p (t e) -> p t e", t=T)

                def rg(n):
                    return rt[:, n, :].rearrange("p (g e) -> p g e", e=EPG)

                link(tt(r(1), r(0), rbias[:, :].unsqueeze(1).broadcast_to([P, T, NE]), AD))
                b_ = rg(1)
                p6 = rt[:, 2:4, :].rearrange("p a b -> p (a b)")[:, 0:6 * T * NG].rearrange("p (g k) -> p g k", k=6)
                tt(p6[:, :, 0:2], b_[:, :, 0:2], b_[:, :, 2:4], AD)
                tt(p6[:, :, 2:3], b_[:, :, 0:1], b_[:, :, 1:2], AD)
                tt(p6[:, :, 3:4], b_[:, :, 2:3], b_[:, :, 3:4], AD)
                tt(p6[:, :, 4:5], b_[:, :, 0:1], b_[:, :, 3:4], AD)
                link(tt(p6[:, :, 5:6], b_[:, :, 1:2], b_[:, :, 2:3], AD))
                gs = rt[:, 4, 0:T * NG].rearrange("p (t g) -> p t g", t=T)
                link(v.tensor_reduce(rt[:, 4, 0:T * NG], p6, AX.X, ALU.max))

                def first_best(scores_, n, rank, mx, out_, eq):
                    link(v.tensor_reduce(mx, scores_, AX.X, ALU.max))
                    link(tt(eq, scores_, mx.unsqueeze(2).broadcast_to([P, T, n]), ALU.is_equal))
                    link(tt(eq, eq, rank.unsqueeze(1).broadcast_to([P, T, n]), M))
                    link(v.tensor_reduce(mx, eq, AX.X, ALU.max))
                    link(tt(out_, eq, mx.unsqueeze(2).broadcast_to([P, T, n]), ALU.is_equal))

                mx = rt[:, 6, 0:T]
                gsel = rt[:, 7, 0:T * NG].rearrange("p (t g) -> p t g", t=T)
                first_best(gs, NG, rank[:, 0:NG], mx, gsel, rt[:, 8, 0:T * NG].rearrange("p (t g) -> p t g", t=T))
                gm = rt[:, 7, 0:T * NG].unsqueeze(2).broadcast_to([P, T * NG, EPG])
                link(tt(rg(9), rg(1), gm, M))
                link(ts(rt[:, 7, 0:T * NG], rt[:, 7, 0:T * NG], -1.0, -NEG, AD, M))
                link(tt(rg(9), rg(9), gm, AD))
                first_best(r(9), NE, rank[:, :], mx, r(10), r(11))
                link(stt(r(12), r(10), 2 * NEG, r(9), M, AD))
                first_best(r(12), NE, rank[:, :], mx, r(13), r(11))
                tt(r(14), r(13), r(10), AD).then_inc(s["member"], 1)
                v.wait_ge(s["member"], run)
                link(tt(r(13), r(14), r(0), M))
                link(v.tensor_reduce(mx, r(13), AX.X, AD))
                link(v.reciprocal(mx, mx))
                tt(r(15), r(13), mx.unsqueeze(2).broadcast_to([P, T, NE]), M).then_inc(s["combine"], 1)
                v.wait_ge(s["counts"], run)
                link(v.tensor_reduce(rt[:, 5, 0:1], bank[1][:, 2 * NE:3 * NE], AX.X, ALU.max))
                ts(overflow[:, 0:1], rt[:, 5, 0:1], float(P), None, ALU.is_gt).then_inc(s["overflow"], 1)
                v.wait_ge(s["overflow"], run)
                link(stt(slot_no, bank[1][:, 0:2 * NE], 1.0, rt[:, 14, :], AD, M))
                ts(slot_no, slot_no, -1.0, None, AD).then_inc(s["pos"], 1)
                v.wait_ge(s["pos"], run)
                full = v.value_load(overflow[0:1, 0:1], min_val=0, max_val=1)
                base = 2 * n1 + 2 * NE * l
                with v.If(full):
                    cp(sel[0:NE, :, :], ident[0:NE, 0:NE].unsqueeze(2).broadcast_to([NE, NE, P]))
                    v.wait_ge(s[f"combineT.{l}"], 1)
                    cp(combT[:, :], bank[1][0:NE, 0:SEQ]).then_inc(s[f"combT.{l}"], 1)
                    v.wait_ge(s[f"combine_bc.{l}"], 1)
                    for n in range(4, 8):
                        ins = cp(cb[:, 2 * n:2 * n + 2, :].rearrange("p a b -> p (a b)"), bank[n][:, :])
                    ins.then_inc(s[f"cb_dve.{l}"], 1)
                    v.wait_ge(s[f"cb_dve.{l}"], 1)
                    v.wait_ge(s[f"cb_act.{l}"], 1)
                    swiglu(f"moe.{l}", 2 * NE, base, f".{l}")
                    if l < LAYERS - 1:
                        for name, n in SLOT_COUNTS["v"]:
                            v.sem_inc(s[name], n)
                with v.Else():
                    sparse(l)
                add_gated_to_x()
                v.wait_ge(s["x"], 5 + 2 * l)
            link(normalise(x, xn))
            v.wait_ge(s["final_in"], 16)
            tt(xn[:, :, :], xn[:, :, :], fin[:, :].unsqueeze(1).broadcast_to([P, T, D]), M).then_inc(s["out_ready"], 1)


_INS = ["x", "mem", "ffn1_norm", "ffn1_w_in", "ffn1_w_out", "mix_norm", "mem_norm", "w_in", "lru_conv_w", "lru_conv_b",
        "lru_a_w", "lru_a_b", "lru_x_w", "lru_x_b", "lru_lambda", "moba_q_norm", "moba_k_norm", "mem_w_kv",
        "mem_q_norm", "mem_k_norm", "w_out", "ffn2_norm", "ffn2_w_in", "ffn2_w_out", "c_2", "positions_2", "ada_w_2",
        "ada_b_2", "norm1_g_2", "w_in_2", "hg_lb_logits_2", "hg_norm_g_2", "q_norm_g_2", "w_q_up_2", "kv_norm_g_2",
        "w_kv_up_2", "w_br_a_2", "w_br_b_2", "w_out_2", "norm2_g_2", "w_router_2", "router_bias_2", "w_gate_2",
        "w_up_2", "w_down_2", "final_g_2"]


def kernel(**inputs):
    import concourse.bacc as _bacc
    from concourse.bass_utils import run_bass_kernel_spmd as _run

    nc = _bacc.Bacc("TRN2", target_bir_lowering=False, num_devices=1)
    arrays, args = {}, {}
    for name in _INS:
        v = np.ascontiguousarray(inputs[name])
        arrays[f"in_{name}"] = v
        args[name] = nc.dram_tensor(f"in_{name}", v.shape, mybir.dt.from_np(v.dtype), kind="ExternalInput").ap()
    args["out"] = nc.dram_tensor("out_x", (1, SEQ, D), F32, kind="ExternalOutput").ap()
    build(nc, args)
    return _run(nc, [arrays], core_ids=[0]).results[0]["out_x"]
```

```python
from contextlib import ExitStack

import numpy as np
import concourse.bass as bass
from concourse import mybir

F32 = mybir.dt.float32
F32R = mybir.dt.float32r
I32 = mybir.dt.int32
U8 = mybir.dt.uint8
ALU = mybir.AluOpType
ACT = mybir.ActivationFunctionType
AX = mybir.AxisListType

P = 128
SEQ = 256
T = SEQ // P
D = 1024
KC = D // P
EPS = 1e-6
HD = 64
LW = 512
LC = LW // P
LRU_C = 8.0
DFF = 2816
LAYERS = 2
HGH, DK = 4, 128
QL, KVL, ROPE, NOPE, MV = 384, 256, 32, 64, 64
MH = 8
DQK = NOPE + ROPE
NE, NG, EPG, DE = 16, 4, 4, 512
CHUNK = 64
FB = 256
RING = 6
TILE = 2048
LEVELS = [1, 2, 4, 8, 16, 32, 64, 128]
NEG = -1.0e30
MISC = QL + KVL + ROPE
ADA = 6 * D
ADA_SLABS = ADA // FB


def ffn_pos(n, kind, c):
    if kind == "down":
        return 3 * n - 1 if c == n - 1 else 3 * c + 4
    off = {"gate": 0, "up": 1}[kind]
    return off if c == 0 else 3 * c - 1 + off


def build(nc, a):
    ctx = ExitStack()
    with ctx:
        def sb(name, shape, dt=F32):
            return ctx.enter_context(nc.sbuf_tensor("sb_" + name, shape, dt))

        def sem(name):
            return ctx.enter_context(nc.semaphore(name))

        bank = [ctx.enter_context(nc.psum_tensor(f"bank{i}", [P, 512], F32)) for i in range(8)]

        x = sb("x", [P, T, D])
        hT_at = nc.sbuf_base
        hT = sb("hT", [P, KC, SEQ])
        xn = sb("xn", [P, T, D])
        ring_at = nc.sbuf_base
        ring = sb("ring", [P, RING, TILE])
        small_a = sb("small_a", [P, 2, 512])
        small_b_at = nc.sbuf_base
        small_b = sb("small_b", [P, 2, 512])
        gbc = sb("gbc", [P, D])
        ident = sb("ident", [P, P])
        ones = sb("ones", [P, P])
        pcol = sb("pcol", [P, 2, P])
        abcol = sb("abcol", [P, LAYERS, 48])
        modc = sb("modc", [P, LAYERS, 48])
        scol = sb("scol", [P, LAYERS, 2, KC])
        csilu = sb("csilu", [P, KC])
        stat = sb("stat", [P, 8, 32])
        lbc = sb("lbc", [P, 8, HGH])
        lruc = sb("lruc", [P, 10, LC])
        level_mask = sb("level_mask", [P, 8, P])
        seg = sb("seg", [P, 8, 1028], U8)
        dist = sb("dist", [P, T, SEQ])
        mla_mask = sb("mla_mask", [P, T, SEQ])
        rope_t = sb("rope_t", [P, 12, T, 16])
        pos_i = sb("pos_i", [P, T], I32)
        rank = sb("rank", [P, NE])
        router = sb("router", [P, KC, NE])
        rbias = sb("rbias", [P, NE])
        combT = sb("combT", [NE, SEQ])
        overflow = sb("overflow", [P, 8], I32)
        by_slot = sb("by_slot", [P, 8])
        w_next = by_slot[:, 0:2]
        w_slot = by_slot[:, 2:4]
        slot_col = by_slot[:, 4:5]
        row_pick = sb("row_pick", [P, 96])
        arena_at = nc.sbuf_base
        arena = sb("arena", [P, 25600])

        def view(at, *shape):
            n = int(np.prod(shape))
            assert at + n <= 25600, (at, shape)
            v = arena[:, at:at + n]
            if len(shape) == 2:
                v = v.rearrange("p (a b) -> p a b", b=shape[1])
            if len(shape) == 3:
                v = v.rearrange("p (a b c) -> p a b c", b=shape[1], c=shape[2])
            if len(shape) == 4:
                v = v.rearrange("p (a b c d) -> p a b c d", b=shape[1], c=shape[2], d=shape[3])
            return v

        def rounded(name, at, *shape):
            assert at + int(np.prod(shape)) <= 25600
            return nc.alloc_sbuf_tensor_at("sb_" + name, [P, *shape], F32R, offset=arena_at + 4 * at)

        def over(name, at, *shape):
            return nc.alloc_sbuf_tensor_at("sb_" + name, [P, *shape], F32R, offset=at)

        w_hi = rounded("w_hi", 10240, 2, TILE)
        w_lo = over("w_lo", ring_at, RING, TILE)
        hT_hi = over("hT_hi", hT_at, KC, SEQ)
        hT_lo = rounded("hT_lo", 14336, KC, SEQ)
        hid_hi = over("hid_hi", small_b_at, 2, 512)
        hid_lo = rounded("hid_lo", 16384, 2, 512)
        prow = view(17408, 2, P)
        abrow = view(17664, LAYERS, P)
        iot = view(17920, 3, P).bitcast(I32)
        ada_acc = view(0, ADA_SLABS, FB)
        ada_w = view(6144, 2, KC, FB)
        mixT = view(0, KC, SEQ)
        memx = view(19456, T, D)
        memn = view(21504, T, D)
        memT = view(21504, KC, SEQ)
        qk4 = view(6144, 4, 512)
        qkT = view(8192, 4, 2, SEQ)
        v2 = view(10240, 2, T, 256)
        att_p = view(11264, 16, SEQ)
        att_pT = view(15360, 8, T, SEQ)
        xl = view(19456, LC, SEQ + 4)
        xb = view(20496, LC, SEQ)
        lr = view(21520, LC, SEQ)
        li = view(22544, LC, SEQ)
        lt = view(2048, LC, SEQ)
        lt2 = view(3072, LC, SEQ)
        gel = view(5120, LC, SEQ)
        lru_w_all = view(24576, 2, LC, P)
        ada_rows = view(16384, P)
        G = view(0, T, 2, D)
        hq = view(4096, HGH, SEQ)
        hk = view(5120, HGH, SEQ)
        hg = view(6144, HGH, SEQ)
        hf = view(7168, HGH, SEQ)
        scan_f = view(8192, HGH * SEQ)
        scan_b = view(9216, HGH * SEQ)
        hy = view(10240, HGH * SEQ)
        attT = view(11264, 3, HGH, P)
        prod = view(12800, T, HGH, P)
        mlp_p = view(4096, 16, SEQ)
        mlp_pT = view(8192, 8, T, SEQ)
        oaT = view(13312, HGH, SEQ)
        misc = view(14336, T, MISC)
        cT = view(15680, 5, SEQ)
        q96 = view(16960, T, MH, DQK)
        k96 = view(18496, T, MH, DQK)
        vm = view(20032, T, MH, MV)
        qT96 = view(21056, MH, SEQ)
        kT96 = view(23104, MH, SEQ)
        ymT = view(14336, 4, SEQ)
        merged = view(16960, T, D)
        diag = view(19008, KC, P)
        oa = view(8192, T, 512)
        oa_sq = view(9216, 1024)
        fin = view(24576, D)
        scr = small_b[:, :, :].rearrange("p a b -> p (a b)")
        hgate = xn[:, 0, :].rearrange("p (h s) -> p h s", h=HGH)
        vh = xn[:, 1, :].rearrange("p (t c) -> p t c", t=T)
        cb = view(0, NE, SEQ)
        sel = view(4096, NE, P)
        ep = view(6144, 2, 512)
        rt = view(7168, 16, T * NE)
        down_hi = rounded("down_hi", 0, 2, TILE)
        down_hid_lo = rounded("down_hid_lo", 4096, 2, 2 * P)
        xn_parts = rounded("xn_parts", 8192, 2, T, D)
        pos_bc = view(12288, NE, SEQ)
        pick = rounded("pick", 16384, T, 2, P)
        put = rounded("put", 16896, 2, SEQ)
        ye_parts = rounded("ye_parts", 17408, 2, D)
        before = view(22400, P)
        slot_row = view(22528, P)
        sel_r = rounded("sel_r", 20032, NE, P)
        posT = rounded("posT", 22080, SEQ)
        slot_no = view(22336, T * NE)

        acc = bank[0:4]
        two = [b[:, :].rearrange("p (a c) -> p a c", a=2) for b in bank]

        rows, row_loads = {}, []

        def param(tile, name, ap, n):
            at = sum(v[2] for v in rows.values() if v[0] == tile)
            rows[name] = (tile, at, n)
            row_loads.append((tile, at, n, ap))

        def by_row(ap):
            return ap.rearrange("a (r c) -> (a r) c", c=P)

        param(0, "ffn1", by_row(a["ffn1_norm"]), 8)
        param(0, "mix", by_row(a["mix_norm"]), 8)
        param(0, "mem", by_row(a["mem_norm"]), 8)
        param(0, "ffn2", by_row(a["ffn2_norm"]), 8)
        param(0, "n1", by_row(a["norm1_g_2"]), 16)
        param(0, "n2", by_row(a["norm2_g_2"]), 16)
        param(0, "qn", by_row(a["q_norm_g_2"]), 6)
        param(0, "kvn", by_row(a["kv_norm_g_2"]), 4)
        param(0, "hgn", by_row(a["hg_norm_g_2"]), 8)
        param(0, "convw", a["lru_conv_w"].rearrange("a w (r c) -> (a w r) c", c=P), 16)
        param(0, "convb", by_row(a["lru_conv_b"]), 4)
        param(0, "ab", a["lru_a_b"].rearrange("a (r b) c -> (a r) (b c)", b=2), 4)
        param(0, "xb", a["lru_x_b"].rearrange("a (r b) c -> (a r) (b c)", b=2), 4)
        param(0, "lam", by_row(a["lru_lambda"]), 4)
        param(0, "lb", by_row(a["hg_lb_logits_2"]), 8)
        param(1, "c", by_row(a["c_2"]), 8)
        param(1, "heads", None, 4)
        row_loads.pop()
        heads_row = rows["heads"][1]
        HEAD_GAINS = ["moba_q_norm", "moba_k_norm", "mem_q_norm", "mem_k_norm"]
        N_ROW_HW = len(row_loads[0::3]) + len(row_loads[1::3]) + 2 * len(HEAD_GAINS)
        N_ROW_DMA = len(row_loads) + 2 * len(HEAD_GAINS) + LAYERS

        def col(name, i=0, n=1):
            tile, at, _ = rows[name]
            return pcol[:, tile, at + i:at + i + n]

        stream, place, total = [], {}, 0

        def tile(name, src):
            nonlocal total
            stream.append((name, src))
            place[name] = total
            total += 1

        def swiglu_tiles(name, n, gate, up, down):
            nonlocal total
            stream.append((name, n, gate, up, down))
            place[name] = total
            total += 3 * n

        def cols(w, c0, n):
            return w.rearrange("(k p) n -> p k n", p=P)[:, :, bass.ds(c0, n)]

        def rws(w, r0, n):
            return w[bass.ds(r0, n * P), :].rearrange("(k p) n -> p k n", p=P)

        def dense(name, w_in, w_out):
            swiglu_tiles(name, DFF // FB,
                         lambda i, c: cols(w_in, i * (2 * FB) + c * FB, FB),
                         lambda i, c: cols(w_in, i * (2 * FB) + (DFF + c * FB), FB),
                         lambda i, c: rws(w_out, i * (2 * FB) + c * FB, FB // P))

        dense("ffn1", a["ffn1_w_in"][0], a["ffn1_w_out"][0])
        for n in range(2):
            tile(f"mem_kv{n}", cols(a["mem_w_kv"][0], n * FB, FB))
        for n in range(8):
            tile(f"w_in{n}", cols(a["w_in"][0], n * FB, FB))
        for n in range(4):
            tile(f"w_out{n}", rws(a["w_out"][0], n * FB, 2))
        dense("ffn2", a["ffn2_w_in"][0], a["ffn2_w_out"][0])
        for l in range(LAYERS):
            w2 = a["w_in_2"][l]
            for n in (0, 1, 6, 7, 2, 3, 4, 5):
                tile(f"proj{n}.{l}", cols(w2, n * FB, FB))
            for n in range(3):
                tile(f"misc{n}.{l}", cols(w2, 2048 + n * FB, min(FB, MISC - n * FB)))
            for n in range(2):
                tile(f"q_up{n}.{l}", cols(a["w_q_up_2"][l], n * QL, QL))
            tile(f"kv_up.{l}", cols(a["w_kv_up_2"][l], 0, 1024))
            for n in range(8):
                tile(f"gates{n}.{l}", cols(w2, 2048 + MISC + n * FB, FB))
            for n in range(2):
                tile(f"br_a{n}.{l}", rws(a["w_br_a_2"][l], n * FB, 2))
            for n in range(2):
                tile(f"br_b{n}.{l}", rws(a["w_br_b_2"][l], n * FB, 2))
            for n in range(4):
                tile(f"w_out{n}.{l}", rws(a["w_out_2"][l], n * FB, 2))
            wg, wu, wd = a["w_gate_2"][l], a["w_up_2"][l], a["w_down_2"][l]
            swiglu_tiles(f"moe.{l}", NE * DE // FB,
                         lambda i, c, w=wg: w.rearrange("e (k p) n -> p e k n", p=P)[:, i + c // 2, :, (c % 2) * FB:(c % 2 + 1) * FB],
                         lambda i, c, w=wu: w.rearrange("e (k p) n -> p e k n", p=P)[:, i + c // 2, :, (c % 2) * FB:(c % 2 + 1) * FB],
                         lambda i, c, w=wd: w.rearrange("e (k p) n -> p e k n", p=P)[:, i + c // 2, 2 * (c % 2):2 * (c % 2) + 2, :])

        class Signals(dict):
            def __missing__(self, name):
                self[name] = sem(name)
                return self[name]

        s = Signals()
        ring_full = [sem(f"ring_full{i}") for i in range(RING)]
        tiles_used = sem("tiles_used")
        block = ctx.enter_context(nc.Block())

        def slot_view(pos, kind):
            w = ring[:, pos % RING, :]
            if kind == 3 * QL:
                return w[:, 0:3 * QL].rearrange("p (k n) -> p k n", k=3)
            if kind == 1024:
                return w.rearrange("p (k n) -> p k n", k=2)
            return w[:, 0:KC * kind].rearrange("p (k n) -> p k n", k=KC)

        STEPS_1 = 2 * (DFF // FB)

        SLOT_COUNTS = dict(
            act=(("hid_hi", 2 * NE), ("w_hi", 4 * NE), ("xg_act", NE), ("pos_out", NE // 2), ("ye_hi", NE)),
            pe=(("pos_turned", 1), ("gathered", 2 * NE), ("weights", NE // 2), ("pos_bc", NE // 2), ("scattered", NE)),
            v=(("product", 2 * NE), ("w_lo", 2 * NE), ("pick", NE // 2), ("posT", 1), ("xg_dve", NE), ("w_next", NE // 2), ("w_slot", NE // 2),
               ("put", NE), ("ye_lo", NE)))

        def expert_pos(kind, j):
            return ffn_pos(2 * NE, kind, j)

        def ring_tile(buf, pos, kind):
            w = buf[:, pos % buf.shape[1], :]
            return w.rearrange("p (k n) -> p k n", n=kind)

        def loop_shape(n):
            j0 = 3 if n % 2 else 2
            return j0, (n - j0) // 2

        @block.sync
        def _(sp):
            sp.dma_start(x[:, :, :], a["x"][0].rearrange("(t p) d -> p t d", p=P)).then_inc(s["x_in"], 16)

            sp.wait_ge(s["prow_zero"], 1)
            for tile_, at, n, ap in row_loads[1::3]:
                sp.dma_start(prow[at:at + n, tile_, :], ap).then_inc(s["rows_in_hw"], 16)
            for r, name in enumerate(HEAD_GAINS):
                for half in range(2):
                    sp.dma_start(prow[heads_row + r:heads_row + r + 1, 1, half * HD:(half + 1) * HD],
                                 a[name]).then_inc(s["rows_in_hw"], 16)

            def load(pos, src, i=0):
                if not (isinstance(i, int) and pos < RING):
                    sp.wait_ge(tiles_used, RING * i + (pos - RING + 1))
                n, k = src.shape[2], src.shape[1]
                dst = ring[:, pos % RING, 0:n * k].rearrange("p (k n) -> p k n", k=k)
                sp.dma_start(dst, src).then_inc(ring_full[pos % RING], 16)

            for entry in stream:
                pos = place[entry[0]]
                if len(entry) == 2:
                    load(pos, entry[1])
                    continue
                _, n, gate, up, down = entry

                def step(i, c, first=False):
                    load(pos + ffn_pos(n, "gate", c), gate(i, c), i)
                    load(pos + ffn_pos(n, "up", c), up(i, c), i)
                    if not first:
                        load(pos + 3 * (c - 1) + 4, down(i, c - 1), i)

                j0, turns = loop_shape(n)
                step(0, 0, True)
                for c in range(1, j0):
                    step(0, c)
                with sp.Fori(0, turns) as i:
                    step(i, j0)
                    step(i, j0 + 1)
                load(pos + 3 * n - 1, down(turns - 1, j0 + 1))

            sp.wait_ge(s["out_ready"], 1)
            sp.dma_start(a["out"][0].rearrange("(t p) d -> p t d", p=P), xn[:, :, :]).then_inc(s["out_stored"], 16)
            sp.wait_ge(s["out_stored"], 16)

        @block.gpsimd
        def _(pool):
            done = [0]

            def link(ins):
                done[0] += 1
                ins.then_inc(s["pool_chain"], 1)
                pool.wait_ge(s["pool_chain"], done[0])

            pool.wait_ge(s["prow_zero"], 1)
            for tile_, at, n, ap in row_loads[2::3]:
                pool.dma_start(prow[at:at + n, tile_, :], ap).then_inc(s["rows_in"], 16)
            for l in range(LAYERS):
                pool.dma_start(abrow[0:48, l, :], a["ada_b_2"][l].rearrange("(r c) -> r c", c=P)).then_inc(s["rows_in"], 16)
            link(pool.memset(row_pick[:, :], 0.0))
            pool.memset(row_pick[:, 48:49], 1.0)
            link(pool.memset(ident[:, :], 0.0))
            pool.affine_select(out=ident[:, :], in_=ident[:, :], compare_op=ALU.not_equal, fill=1.0,
                               base=0, pattern=[[-1, P]], channel_multiplier=1).then_inc(s["ident"], 1)
            pool.dma_start(pos_i[:, :], a["positions_2"].rearrange("a (t p) -> p (a t)", p=P),
                           allow_slow_non_contiguous=True).then_inc(s["pos_in"], 16)
            for t in range(T):
                ins = pool.iota(dist[:, t, :], [[-1, SEQ]], base=t * P, channel_multiplier=1,
                                allow_small_or_imprecise_dtypes=True)
            link(ins)
            for t in range(T):
                ins = pool.affine_select(out=dist[:, t, :], in_=dist[:, t, :], compare_op=ALU.is_ge, fill=-NEG,
                                         base=t * P, pattern=[[-1, SEQ]], channel_multiplier=1)
            ins.then_inc(s["patterns"], 1)
            link(pool.memset(mla_mask[:, :, :], 0.0))
            link(pool.memset(mla_mask[0:CHUNK, 0, CHUNK:SEQ], NEG))
            link(pool.memset(mla_mask[CHUNK:P, 0, P:SEQ], NEG))
            link(pool.memset(mla_mask[0:CHUNK, 1, P + CHUNK:SEQ], NEG))
            inv = np.float32(10000.0) ** (-np.arange(16, dtype=np.float32) / np.float32(16))
            for n in range(16):
                ins = pool.memset(rope_t[:, 0, 0, n:n + 1], float(inv[n]))
            ins.then_inc(s["inv_freq"], 1)
            pool.dma_start(router[:, :, :], a["w_router_2"].rearrange("(k p) e -> p k e", p=P)).then_inc(s["router_in"], 16)
            pool.dma_start(rbias[:, :], a["router_bias_2"].partition_broadcast(P)).then_inc(s["router_in"], 16)
            pool.wait_ge(s["lru_w_zero"], 1)
            for g, name in ((0, "lru_a_w"), (1, "lru_x_w")):
                for half in range(2):
                    w = lru_w_all[half * HD:(half + 1) * HD, g, :, half * HD:(half + 1) * HD]
                    pool.dma_start(w, a[name][0].rearrange("(c h) i j -> h i c j", h=2)[half]).then_inc(s["lru_w_in"], 16)

            pool.wait_ge(s["csilu"], 1)
            for l in range(LAYERS):
                if l:
                    pool.wait_ge(s["x"], 2)
                w = a["ada_w_2"][l].rearrange("(k p) n -> p k n", p=P)
                pairs = ADA_SLABS // 2

                def slab_load(n, b):
                    pool.dma_start(ada_w[:, b], w[:, :, bass.ds(n * FB, FB)]).then_inc(s[f"ada_in{b}"], 16)

                def even_slab(i, more):
                    pool.wait_ge(s["ada_in0"], 16 * i + 16 * (l * pairs + 1))
                    base = 4 * l * pairs
                    wv = ada_w[:, 0]
                    c_b = csilu[:, :].unsqueeze(2).broadcast_to([P, KC, FB])
                    pool.tensor_tensor(wv, wv, c_b, ALU.mult).then_inc(s["ada_chain"], 1)
                    pool.wait_ge(s["ada_chain"], 4 * i + base + 1)
                    pool.tensor_tensor(wv[:, 0:4], wv[:, 0:4], wv[:, 4:8], ALU.add).then_inc(s["ada_chain"], 1)
                    pool.wait_ge(s["ada_chain"], 4 * i + base + 2)
                    pool.tensor_tensor(wv[:, 0:2], wv[:, 0:2], wv[:, 2:4], ALU.add).then_inc(s["ada_chain"], 1)
                    pool.wait_ge(s["ada_chain"], 4 * i + base + 3)
                    pool.tensor_tensor(ada_acc[:, bass.ds(2 * i, 1), :], wv[:, 0:1], wv[:, 1:2], ALU.add)\
                        .then_inc(s["ada_chain"], 1)
                    if more:
                        pool.wait_ge(s["ada_chain"], 4 * i + base + 4)
                        slab_load(2 * i + 2, 0)
                        pool.wait_ge(s["ada_dve"], KC * i + KC * (l * pairs + 1))
                        slab_load(2 * i + 3, 1)

                slab_load(0, 0)
                slab_load(1, 1)
                with pool.Fori(0, pairs - 1) as i:
                    even_slab(i, True)
                even_slab(pairs - 1, False)
            pool.wait_ge(s["x"], 3)
            pool.iota(iot[:, 0, :], [[0, P]], base=0, channel_multiplier=1)
            pool.iota(iot[:, 1, :], [[1, P]], base=0, channel_multiplier=0)
            pool.iota(view(22000, 1028).bitcast(I32), [[1, 1028]], base=0, channel_multiplier=0).then_inc(s["patterns"], 1)
            for l in range(LAYERS):
                pool.wait_ge(s["x"], 4 + 2 * l)
                pool.iota(slot_row, [[1, P]], base=0, channel_multiplier=0, allow_small_or_imprecise_dtypes=True)
                pool.iota(slot_col[:, 0:1], [[0, 1]], base=0, channel_multiplier=1, allow_small_or_imprecise_dtypes=True)
                link(pool.memset(before, 1.0))
                pool.affine_select(out=before, in_=before, compare_op=ALU.is_ge, fill=0.0, base=-1,
                                   pattern=[[1, P]], channel_multiplier=-1).then_inc(s["slot_patterns"], 1)
                pool.wait_ge(s["xn_hi"], l + 1)
                pool.tensor_tensor(xn_parts[:, 1], xn[:, :, :], xn_parts[:, 0].bitcast(F32), ALU.subtract)\
                    .then_inc(s["xn_lo"], 1)
            pool.dma_start(fin[:, :], a["final_g_2"].partition_broadcast(P)).then_inc(s["final_in"], 16)

        @block.scalar
        def _(act):
            A = act.activation

            def used(name):
                act.wait_ge(tiles_used, place[name] + 1)

            def root(run):
                act.wait_ge(s["ms"], run)
                A(stat[:, 2, :], stat[:, 1, :], ACT.Sqrt).then_inc(s["root"], 1)

            def turn(run, dst, scale, bias):
                act.wait_ge(s["xnT"], run)
                for k in range(KC // 2):
                    src = bank[4 + k // 2][:, (k % 2) * SEQ:(k % 2 + 1) * SEQ]
                    ins = A(dst[:, k, :], src, ACT.Identity, scale=scale(k), bias=bias(k) if bias else 0.0)
                ins.then_inc(s["hT_act"], 1)

            def swiglu(name, n, base):
                pos = place[name]

                def step(i, c, late=True):
                    j = 2 * i + c
                    p = c % 2
                    act.wait_ge(tiles_used, RING * i + (pos + (0 if c == 0 else 3 * c - 1) + 1))
                    if late:
                        act.wait_ge(s["hidden"], j + (base - 1))
                    A(small_a[:, p, :], bank[4 + 2 * p][:, :], ACT.Silu).then_inc(s["silu"], 1)

                j0, turns = loop_shape(n)
                for c in range(j0):
                    step(0, c, base + c >= 2)
                with act.Fori(0, turns) as i:
                    step(i, j0)
                    step(i, j0 + 1)

            def turn_parts(run, scale):
                act.wait_ge(s["xnT"], run)
                for k in range(KC):
                    ins = A(hT_hi[:, k, :], bank[4 + k // 2][:, (k % 2) * SEQ:(k % 2 + 1) * SEQ], ACT.Copy, scale=scale(k))
                    if k % 2:
                        ins.then_inc(s["hT_hi"], 1)

            def ffn(name, n, base):
                pos0 = place[name]

                def split(i, q):
                    act.wait_ge(ring_full[(pos0 + q) % RING], 16 * i + 16 * ((pos0 + q) // RING + 1))
                    if q >= 2:
                        act.wait_ge(tiles_used, RING * i + (pos0 + q - 1))
                    for half in range(2):
                        c = slice(half * TILE // 2, (half + 1) * TILE // 2)
                        A(w_hi[:, q % 2, c], ring[:, (pos0 + q) % RING, c], ACT.Copy).then_inc(s["w_hi"], 1)

                def silu(i, c):
                    p = c % 2
                    act.wait_ge(tiles_used, RING * i + (pos0 + ffn_pos(n, "gate", c) + 1))
                    if base + c >= 2:
                        act.wait_ge(s["hidden"], 2 * i + (base + c - 1))
                    A(small_a[:, p, :], bank[4 + 2 * p][:, :], ACT.Silu).then_inc(s["silu"], 1)

                def hidden(i, c):
                    act.wait_ge(s["product"], 2 * i + (base + c + 1))
                    A(hid_hi[:, c % 2, :], small_a[:, c % 2, :], ACT.Copy).then_inc(s["hid_hi"], 1)

                def step(i, c):
                    q = ffn_pos(n, "gate", c)
                    split(i, q)
                    hidden(i, c - 1)
                    split(i, q + 1)
                    split(i, q + 2)
                    silu(i, c)

                split(0, 0)
                split(0, 1)
                silu(0, 0)
                j0, turns = loop_shape(n)
                for c in range(1, j0):
                    step(0, c)
                with act.Fori(0, turns) as i:
                    step(i, j0)
                    step(i, j0 + 1)
                hidden(0, n - 1)
                split(0, 3 * n - 1)

            def sparse(l):
                pos0 = place[f"moe.{l}"]
                base = 2 * (DFF // FB) + 2 * NE * l

                def parts(i, c):
                    p, at = c % 2, pos0 + expert_pos("down", c)
                    act.wait_ge(s["product"], 4 * i + (base + c + 1))
                    if c >= 2:
                        act.wait_ge(tiles_used, 2 * RING * i + (pos0 + expert_pos("down", c - 2) + 1))
                    A(hid_hi[:, p, 0:2 * P], small_a[:, p, 0:2 * P], ACT.Copy).then_inc(s["hid_hi"], 1)
                    act.wait_ge(ring_full[at % RING], 32 * i + 16 * (at // RING + 1))
                    for half in range(2):
                        cs = slice(half * TILE // 2, (half + 1) * TILE // 2)
                        A(down_hi[:, p, cs], ring[:, at % RING, cs], ACT.Copy).then_inc(s["w_hi"], 1)

                def step(i, c):
                    p = c % 2
                    if c:
                        parts(i, c - 1)
                    act.wait_ge(tiles_used, 2 * RING * i + (pos0 + expert_pos("up", c) + 1))
                    if c >= 2:
                        act.wait_ge(s["hidden"], 4 * i + (base + c - 1))
                    A(small_a[:, p, 0:2 * P], bank[4 + p][:, 0:2 * P], ACT.Silu).then_inc(s["silu"], 1)

                def gathered(i, g):
                    for r in (0, 2):
                        act.wait_ge(s["gathered"], 4 * i + (32 * l + 4 * g + r + 1))
                        for k in (2 * r, 2 * r + 1):
                            ins = A(hT[:, k, :], bank[6][:, (k % 2) * SEQ:(k % 2 + 1) * SEQ], ACT.Identity,
                                    scale=scol[:, l, 1, k:k + 1], bias=modc[:, l, 24 + k:25 + k])
                        ins.then_inc(s["xg_act"], 1)

                def ye(i, e):
                    act.wait_ge(tiles_used, 2 * RING * i + (pos0 + expert_pos("down", 2 * e + 1) + 1))
                    act.wait_ge(s["w_slot"], i + (8 * l + e // 2 + 1))
                    if e:
                        act.wait_ge(s["scattered"], 2 * i + (16 * l + e))
                    for half in range(2):
                        ins = A(ye_parts[:, 0, half * 512:(half + 1) * 512], bank[6 + half][:, :], ACT.Copy,
                                scale=w_slot[:, e % 2:e % 2 + 1])
                    ins.then_inc(s["ye_hi"], 1)

                def pos_copies(b):
                    for n in range(4):
                        act.wait_ge(s["pos_bc"], 8 * l + 4 * b + n + 1)
                        A(pos_bc[:, 8 * b + 2 * n:8 * b + 2 * n + 2, :], two[n], ACT.Copy).then_inc(s["pos_out"], 1)

                def pair(i, g, start=False, last=False):
                    step(i, 4 * g)
                    if not start:
                        ye(i, 2 * g - 1)
                    step(i, 4 * g + 1)
                    if start:
                        pos_copies(1)
                    step(i, 4 * g + 2)
                    ye(i, 2 * g)
                    step(i, 4 * g + 3)
                    if not last:
                        gathered(i, g + 1)

                gathered(0, 0)
                pos_copies(0)
                pair(0, 0, start=True)
                with act.Fori(0, NE // 2 - 2) as i:
                    pair(i, 1)
                pair(0, NE // 2 - 1, last=True)
                parts(0, 2 * NE - 1)
                ye(0, NE - 1)

            def softmax_exp(event, run, src, dst, rows_, scale):
                act.wait_ge(s[event], run)
                for r in rows_:
                    ins = A(dst[:, r, :], src(r), ACT.Exp, bias=stat[:, 4, r:r + 1], scale=scale,
                            accum_out=stat[:, 5, r:r + 1])
                return ins

            def gain(name, off=0):
                return lambda k: col(name, off + k)

            act.wait_ge(s["prow_zero"], 1)
            for tile_, at, n, ap in row_loads[0::3]:
                act.dma_start(prow[at:at + n, tile_, :], ap).then_inc(s["rows_in_hw"], 16)
            act.dma_start(memx[:, :, :], a["mem"][0].rearrange("(t p) d -> p t d", p=P)).then_inc(s["mem_in"], 16)
            roots = iter(range(1, 100))
            root(next(roots))
            root(next(roots))
            act.wait_ge(s["pcol"], 1)
            turn_parts(1, gain("ffn1"))
            A(csilu[:, :], col("c", 0, KC), ACT.Silu).then_inc(s["csilu"], 1)
            n1 = DFF // FB
            ffn("ffn1", n1, 0)

            act.wait_ge(s["xnT"], 2)
            for k in range(KC):
                ins = A(memT[:, k, :], bank[4 + k // 2][:, (k % 2) * SEQ:(k % 2 + 1) * SEQ], ACT.Copy, scale=col("mem", k))
            ins.then_inc(s["memT"], 1)
            root(next(roots))
            used("mem_kv1")
            A(v2[:, 1], two[1], ACT.Copy).then_inc(s["mem_v"], 1)
            act.wait_ge(s["ada_sum"], 1)
            A(ada_rows[0:48, :], bank[2][0:48, 0:P], ACT.Copy).then_inc(s["ada_rows"], 1)
            turn(3, hT, gain("mix"), None)
            act.wait_ge(s["small_in"], 1)
            A(lruc[:, 2, :], lruc[:, 1, :], ACT.Exp, scale=-1.0)
            A(lbc[:, 2, :], lbc[:, 0, :], ACT.Exp)
            A(lbc[:, 3, :], lbc[:, 1, :], ACT.Exp).then_inc(s["small_exp"], 1)
            act.wait_ge(s["xl_zero"], 1)
            for n in range(2):
                used(f"w_in{n}")
                ins = A(xl[:, 2 * n:2 * n + 2, 3:3 + SEQ], two[2 + n], ACT.Copy)
            ins.then_inc(s["xl"], 1)
            for n in range(2):
                used(f"w_in{2 + n}")
                ins = A(gel[:, 2 * n:2 * n + 2, :], two[4 + n], ACT.Gelu_apprx_tanh)
            ins.then_inc(s["gelu"], 1)
            used("w_in6")
            A(v2[:, 0], two[0], ACT.Copy).then_inc(s["moba_v"], 1)
            act.wait_ge(s["lru_gates"], 1)
            for c in range(LC):
                A(lr[:, c, :], bank[2 + c // 2][:, (c % 2) * SEQ:(c % 2 + 1) * SEQ], ACT.Sigmoid, bias=col("ab", c))
                ins = A(li[:, c, :], bank[4 + c // 2][:, (c % 2) * SEQ:(c % 2 + 1) * SEQ], ACT.Sigmoid, bias=col("xb", c))
            ins.then_inc(s["lru_ri"], 1)
            act.wait_ge(s["lru_ri"], 1)
            for c in range(LC):
                A(lt[:, c, :], lr[:, c, :], ACT.Tanh, scale=lruc[:, 9, c:c + 1])
            for c in range(LC):
                ins = A(lt2[:, c, :], lr[:, c, :], ACT.Exp, scale=lruc[:, 8, c:c + 1])
            ins.then_inc(s["lru_a"], 1)
            root(next(roots))
            act.wait_ge(s["lru_m2"], 1)
            A(lt[:, :, :], lt[:, :, :], ACT.Sqrt, scale=2.0).then_inc(s["lru_mult"], 1)
            act.wait_ge(s["qkT"], 1)
            for w in range(2):
                ins = A(qkT[:, w], two[w], ACT.Identity, scale=col("heads", w))
            ins.then_inc(s["qk_act"], 1)
            softmax_exp("att_max", 1, lambda r: att_p[:, r, :], att_p, range(8), HD ** -0.5).then_inc(s["att_exp"], 1)
            act.wait_ge(s["att_max"], 2)
            for r in range(8, 16):
                h, t = (r - 8) // 2, r % 2
                ins = A(att_p[:, r, :], bank[2 * t + h % 2][:, (h // 2) * SEQ:(h // 2 + 1) * SEQ], ACT.Exp,
                        bias=stat[:, 4, r:r + 1], scale=HD ** -0.5, accum_out=stat[:, 5, r:r + 1])
            ins.then_inc(s["att_exp"], 1)
            act.wait_ge(s["att_pT"], 1)
            for h in range(4):
                ins = A(att_pT[:, h], two[4 + h], ACT.Copy)
            ins.then_inc(s["moba_pT_out"], 1)
            act.wait_ge(s["att_pv"], 1)
            A(mixT[:, 4:6, :], two[4], ACT.Copy)
            act.wait_ge(s["att_pv"], 2)
            A(mixT[:, 6:8, :], two[0], ACT.Copy).then_inc(s["mix_heads"], 1)

            root(next(roots))
            turn_parts(4, gain("ffn2"))
            ffn("ffn2", n1, n1)

            for l in range(LAYERS):
                run = l + 1
                root(next(roots))
                if l == 0:
                    act.wait_ge(s["ada_sum"], 2)
                    A(ada_rows[0:48, :], bank[0][0:48, 0:P], ACT.Copy).then_inc(s["ada_rows"], 1)
                turn(5 + 2 * l, hT, lambda k: scol[:, l, 0, k:k + 1], lambda k: modc[:, l, k:k + 1])
                if l == 0:
                    act.wait_ge(s["small_in"], 2)
                    A(rope_t[:, 10], rope_t[:, 8], ACT.Sin)
                    A(rope_t[:, 11], rope_t[:, 9], ACT.Sin).then_inc(s["sincos"], 1)
                for n in range(2):
                    used(f"proj{n}.{l}")
                    ins = A(hq[:, 2 * n:2 * n + 2, :], two[n], ACT.Silu)
                ins.then_inc(s["hq"], 1)
                for n in range(2):
                    used(f"proj{6 + n}.{l}")
                    ins = A(hgate[:, 2 * n:2 * n + 2, :], two[2 + n], ACT.Silu)
                ins.then_inc(s["hgate"], 1)
                for n in range(2):
                    used(f"proj{2 + n}.{l}")
                    ins = A(hf[:, 2 * n:2 * n + 2, :], two[4 + n], ACT.Sigmoid)
                ins.then_inc(s["hf"], 1)
                for n in range(3):
                    w = min(FB, MISC - n * FB)
                    used(f"misc{n}.{l}")
                    ins = A(misc[:, :, n * FB:n * FB + w], bank[n][:, 0:T * w].rearrange("p (t w) -> p t w", t=T), ACT.Copy)
                ins.then_inc(s["misc"], 1)
                act.wait_ge(s["hf_clamped"], run)
                A(hg[:, :, :], hg[:, :, :], ACT.Ln).then_inc(s["hg"], 1)
                root(next(roots))
                act.wait_ge(s["cT"], run)
                for k in range(5):
                    g_col = col("qn", 3 * l + k) if k < 3 else col("kvn", 2 * l + k - 3)
                    ins = A(cT[:, k, :], bank[k // 2][:, (k % 2) * SEQ:(k % 2 + 1) * SEQ], ACT.Identity, scale=g_col)
                ins.then_inc(s["cT_out"], 1)
                used(f"kv_up.{l}")
                for t in range(T):
                    for half in range(2):
                        src = bank[2 * t + half][:, :].rearrange("p (h c) -> p h c", h=4)
                        A(k96[:, t, 4 * half:4 * half + 4, 0:NOPE], src[:, :, 0:NOPE], ACT.Copy)
                        ins = A(vm[:, t, 4 * half:4 * half + 4, :], src[:, :, NOPE:], ACT.Copy)
                ins.then_inc(s["kv_out"], 1)
                for n, L in enumerate(LEVELS):
                    used(f"gates{n}.{l}")
                    ins = A(G[:, :, n // 4, (n % 4) * FB:(n % 4 + 1) * FB],
                            bank[n % 4][:, :].rearrange("p (t c) -> p t c", t=T), ACT.Tanh, scale=0.5)
                    ins.then_inc(s["gates"], 1)
                    act.wait_ge(s["scans"], 8 * l + n + 1)
                    if n:
                        act.wait_ge(s["hy"], 8 * l + n)
                    m = HGH * SEQ // (2 * L)
                    dst = hf[:, :, :].rearrange("p h s -> p (h s)").rearrange("p (m two c) -> p m two c", two=2, c=L)
                    sf = scan_f[:, :].rearrange("p (m two c) -> p m two c", two=2, c=L)
                    sb_ = scan_b[:, :].rearrange("p (m two c) -> p m two c", two=2, c=L)
                    A(dst[:, :, 1, :], sf[:, :, 1, :], ACT.Exp)
                    A(dst[:, :, 0, :], sb_[:, :, 0, :], ACT.Exp).then_inc(s["decay"], 1)
                root(next(roots))
                act.wait_ge(s["mla_qT"], run)
                for n in range(4):
                    ins = A(qT96[0:DQK, 2 * n:2 * n + 2, :], two[n][0:DQK], ACT.Copy)
                ins.then_inc(s["qT_out"], 1)
                for t in range(T):
                    act.wait_ge(s["mla_max"], T * l + t + 1)
                    for r in range(8 * t, 8 * t + 8):
                        ins = A(mlp_p[:, r, :], mlp_p[:, r, :], ACT.Exp, bias=stat[:, 4, r:r + 1],
                                scale=DQK ** -0.5, accum_out=stat[:, 5, r:r + 1])
                    ins.then_inc(s["mla_exp"], 1)
                act.wait_ge(s["mla_pT"], run)
                for h in range(4):
                    ins = A(mlp_pT[:, h], two[h], ACT.Copy)
                ins.then_inc(s["pT_act"], 1)
                act.wait_ge(s["mla_pv"], run)
                for n in range(2):
                    ins = A(ymT[:, 2 * n:2 * n + 2, :], two[n], ACT.Copy)
                ins.then_inc(s["ymT"], 1)
                act.wait_ge(s["mergedT"], run)
                for k in range(KC // 2):
                    ins = A(hT[:, k, :], bank[4 + k // 2][:, (k % 2) * SEQ:(k % 2 + 1) * SEQ], ACT.Copy)
                ins.then_inc(s["mT_act"], 1)
                root(next(roots))
                turn(6 + 2 * l, hT, lambda k: scol[:, l, 1, k:k + 1], lambda k: modc[:, l, 24 + k:25 + k])
                act.wait_ge(s["logits"], run)
                A(rt[:, 0, :], bank[0][:, 0:T * NE], ACT.Sigmoid).then_inc(s["scores"], 1)
                A(xn_parts[:, 0], xn[:, :, :], ACT.Copy).then_inc(s["xn_hi"], 1)
                act.wait_ge(s["overflow"], run)
                full = act.value_load(overflow[0:1, 0:1], min_val=0, max_val=1)
                base = 2 * n1 + 2 * NE * l
                with act.If(full):
                    act.wait_ge(s[f"full_pe.{l}"], 2)
                    for n in range(4):
                        ins = A(cb[:, 2 * n:2 * n + 2, :], two[n], ACT.Copy)
                    ins.then_inc(s[f"cb_act.{l}"], 1)
                    swiglu(f"moe.{l}", 2 * NE, base)
                    if l < LAYERS - 1:
                        for name, n in SLOT_COUNTS["act"]:
                            act.sem_inc(s[name], n)
                with act.Else():
                    sparse(l)
            root(next(roots))

        @block.tensor
        def _(pe):
            mm, tr = pe.matmul, pe.transpose

            def landed(pos, i=0):
                pe.wait_ge(ring_full[pos % RING], 16 * i + 16 * (pos // RING + 1))

            def turn(run, rows_=xn):
                pe.wait_ge(s["xn"], run)
                for k in range(KC):
                    for t in range(T):
                        ins = tr(bank[4 + k // 2][:, (k % 2) * SEQ + t * P:(k % 2) * SEQ + (t + 1) * P],
                                 rows_[:, t, k * P:(k + 1) * P], ident[:, :])
                ins.then_inc(s["xnT"], 1)

            def have_hT(run):
                pe.wait_ge(s["hT_act"], run - (3 if run > 4 else 2))
                pe.wait_ge(s["hT_dve"], run - 1)

            def by_feature(name, out):
                pos = place[name]
                landed(pos)
                w = slot_view(pos, FB)
                for j in range(2):
                    for k in range(KC):
                        ins = mm(out[:, j * SEQ:(j + 1) * SEQ], w[:, k, j * P:(j + 1) * P], hT[:, k, :],
                                 start=k == 0, stop=k == KC - 1)
                ins.then_inc(tiles_used, 1)

            def by_token(name, out, lhs=None, n=FB):
                lhs = hT if lhs is None else lhs
                pos = place[name]
                landed(pos)
                w = slot_view(pos, n)
                for t in range(T):
                    for k in range(KC):
                        ins = mm(out[:, t * n:(t + 1) * n], lhs[:, k, t * P:(t + 1) * P], w[:, k, :],
                                 start=k == 0, stop=k == KC - 1)
                ins.then_inc(tiles_used, 1)

            def rows_product(pos, lhs, out, start, stop, i=0):
                landed(pos, i)
                w = slot_view(pos, 1024)
                for kk in range(2):
                    for t in range(T):
                        for half in range(2):
                            ins = mm(out[2 * t + half][:, :], lhs[:, kk, t * P:(t + 1) * P],
                                     w[:, kk, half * 512:(half + 1) * 512],
                                     start=start and kk == 0, stop=stop and kk == 1)
                ins.then_inc(tiles_used, 1)

            def swiglu(name, n, base):
                pos = place[name]

                def first(i, c, late=True):
                    j, p = 2 * i + c, c % 2
                    if late:
                        pe.wait_ge(s["hidden"], j + (base - 1))
                    for b in range(2):
                        at = pos + (0 if c == 0 else 3 * c - 1) + b
                        landed(at, i)
                        w = slot_view(at, FB)
                        for jj in range(2):
                            for k in range(KC):
                                ins = mm(bank[4 + 2 * p + b][:, jj * SEQ:(jj + 1) * SEQ], w[:, k, jj * P:(jj + 1) * P],
                                         hT[:, k, :], start=k == 0, stop=k == KC - 1)
                        ins.then_inc(tiles_used, 1)

                def second(i, c, at, start=False, stop=False):
                    pe.wait_ge(s["hidden"], 2 * i + (c + base + 1))
                    h = small_b[:, c % 2, :].rearrange("p (k s) -> p k s", k=2)
                    rows_product(pos + at, h, acc, start, stop, i)

                j0, turns = loop_shape(n)
                first(0, 0, base >= 2)
                for c in range(1, j0):
                    first(0, c, base + c >= 2)
                    second(0, c - 1, 3 * (c - 1) + 4, start=c == 1)
                with pe.Fori(0, turns) as i:
                    for c in (j0, j0 + 1):
                        first(i, c)
                        second(i, c - 1, 3 * (c - 1) + 4)
                second(0, n - 1, 3 * n - 1, stop=True)

            PARTS = ((0, 0), (0, 1), (1, 0))

            def ffn(name, n, base):
                pos0 = place[name]
                h_parts = (hT_hi, hT_lo)
                hid_parts = (hid_hi, hid_lo)

                def parts(i, q, kind):
                    pe.wait_ge(s["w_lo"], RING * i + (3 * base + q + 1))
                    return ring_tile(w_hi, q, kind), ring_tile(w_lo, pos0 + q, kind)

                def first(i, c):
                    p = c % 2
                    if base + c >= 2:
                        pe.wait_ge(s["hidden"], 2 * i + (base + c - 1))
                    for b, kind in enumerate(("gate", "up")):
                        w = parts(i, ffn_pos(n, kind, c), FB)
                        for jj in range(2):
                            for k in range(KC):
                                for m, (wp, hp) in enumerate(PARTS):
                                    ins = mm(bank[4 + 2 * p + b][:, jj * SEQ:(jj + 1) * SEQ], w[wp][:, k, jj * P:(jj + 1) * P],
                                             h_parts[hp][:, k, :], start=k == 0 and m == 0, stop=k == KC - 1 and m == 2)
                        ins.then_inc(tiles_used, 1)

                def second(i, c, start=False, stop=False):
                    pe.wait_ge(s["hidden"], 2 * i + (base + c + 1))
                    w = parts(i, 3 * n - 1 if stop else 3 * c + 4, 1024)
                    for kk in range(2):
                        for t in range(T):
                            for m, (hp, wp) in enumerate(PARTS):
                                h = hid_parts[hp][:, c % 2, kk * SEQ + t * P:kk * SEQ + (t + 1) * P]
                                for half in range(2):
                                    ins = mm(acc[2 * t + half][:, :], h, w[wp][:, kk, half * 512:(half + 1) * 512],
                                             start=start and kk == 0 and m == 0, stop=stop and kk == 1 and m == 2)
                    ins.then_inc(tiles_used, 1)

                first(0, 0)
                j0, turns = loop_shape(n)
                for c in range(1, j0):
                    first(0, c)
                    second(0, c - 1, start=c == 1)
                with pe.Fori(0, turns) as i:
                    for c in (j0, j0 + 1):
                        first(i, c)
                        second(i, c - 1)
                second(0, n - 1, stop=True)

            def sparse(l):
                pos0 = place[f"moe.{l}"]
                base = 2 * (DFF // FB) + 2 * NE * l
                comb = rt[:, 15, :].rearrange("p (t e) -> p t e", t=T)

                def first(i, c):
                    p = c % 2
                    if c % 4 == 0:
                        pe.wait_ge(s["xg_act"], 2 * i + (16 * l + c // 2 + 2))
                        pe.wait_ge(s["xg_dve"], 2 * i + (16 * l + c // 2 + 2))
                    if c >= 2:
                        pe.wait_ge(s["hidden"], 4 * i + (base + c - 1))
                    xg = hT[:, :, (c % 4 // 2) * P:(c % 4 // 2 + 1) * P]
                    for b, kind in enumerate(("gate", "up")):
                        at = pos0 + expert_pos(kind, c)
                        landed(at, 2 * i)
                        w = slot_view(at, FB)
                        for jj in range(2):
                            for k in range(KC):
                                ins = mm(bank[4 + p][:, (2 * b + jj) * P:(2 * b + jj + 1) * P], w[:, k, jj * P:(jj + 1) * P],
                                         xg[:, k, :], start=k == 0, stop=k == KC - 1)
                        ins.then_inc(tiles_used, 1)

                def second(i, c):
                    if c % 2 == 0 and c:
                        pe.wait_ge(s["ye_hi"], 2 * i + (16 * l + c // 2))
                        pe.wait_ge(s["ye_lo"], 2 * i + (16 * l + c // 2))
                    pe.wait_ge(s["hidden"], 4 * i + (base + c + 1))
                    pe.wait_ge(s["w_lo"], 4 * i + (3 * STEPS_1 + 2 * NE * l + c + 1))
                    w = (ring_tile(down_hi, c, 1024), ring_tile(w_lo, pos0 + expert_pos("down", c), 1024))
                    h = (hid_hi, down_hid_lo)
                    for kk in range(2):
                        for m, (hp, wp) in enumerate(PARTS):
                            for half in range(2):
                                ins = mm(bank[6 + half][:, :], h[hp][:, c % 2, kk * P:(kk + 1) * P],
                                         w[wp][:, kk, half * 512:(half + 1) * 512],
                                         start=c % 2 == 0 and kk == 0 and m == 0, stop=c % 2 == 1 and kk == 1 and m == 2)
                    ins.then_inc(tiles_used, 1)

                def gather(i, g):
                    pe.wait_ge(s["pick"], i + (8 * l + g + 1))
                    if g:
                        pe.wait_ge(s["ye_hi"], 2 * i + (16 * l + 2 * g - 1))
                        pe.wait_ge(s["ye_lo"], 2 * i + (16 * l + 2 * g - 1))
                    for r in range(4):
                        if r >= 2:
                            pe.wait_ge(s["xg_dve" if r % 2 else "xg_act"], 2 * i + (16 * l + 2 * g + 1))
                        for kk in range(2):
                            k = 2 * r + kk
                            for n, (hl, t) in enumerate(((0, 0), (0, 1), (1, 0), (1, 1))):
                                ins = mm(bank[6 + r % 2][:, kk * SEQ:(kk + 1) * SEQ],
                                         xn_parts[:, hl, t, k * P:(k + 1) * P],
                                         pick[:, t].rearrange("p e s -> p (e s)"), start=n == 0, stop=n == 3)
                        ins.then_inc(s["gathered"], 1)
                    pe.wait_ge(s["xg_act"], 2 * i + (16 * l + 2 * g + 2))
                    for ee in range(2):
                        for t in range(T):
                            ins = mm(bank[6][:, ee:ee + 1], pick[:, t, ee, :].bitcast(F32),
                                     comb[:, t, bass.ds(2 * i + (2 * g + ee), 1)], start=t == 0, stop=t == T - 1)
                    ins.then_inc(s["weights"], 1)

                def gather_read(i, g):
                    pe.wait_ge(s["xg_dve"], 2 * i + (16 * l + 2 * g + 2))
                    pe.wait_ge(s["w_next"], i + (8 * l + g + 1))

                def scatter(i, e):
                    pe.wait_ge(s["put"], 2 * i + (16 * l + e + 1))
                    pe.wait_ge(s["ye_hi"], 2 * i + (16 * l + e + 1))
                    pe.wait_ge(s["ye_lo"], 2 * i + (16 * l + e + 1))
                    for hl in range(2):
                        for t in range(T):
                            for half in range(2):
                                ins = mm(acc[2 * t + half][:, :], put[:, e % 2, t * P:(t + 1) * P],
                                         ye_parts[:, hl, half * 512:(half + 1) * 512],
                                         start=e == 0 and hl == 0, stop=e == NE - 1 and hl == 1)
                    ins.then_inc(s["scattered"], 1)

                def spread(b):
                    for n in range(4):
                        if b:
                            pe.wait_ge(s["pos_out"], 8 * l + n + 1)
                        for ee in range(2):
                            ins = mm(bank[n][:, ee * SEQ:(ee + 1) * SEQ], sel_r[0:NE, 8 * b + 2 * n + ee, :], posT[0:NE, :],
                                     start=True, stop=True)
                        ins.then_inc(s["pos_bc"], 1)

                def pair(i, g, start=False, last=False):
                    first(i, 4 * g)
                    if not start:
                        second(i, 4 * g - 1)
                    first(i, 4 * g + 1)
                    if start:
                        spread(1)
                        gather_read(i, 0)
                    else:
                        scatter(i, 2 * g - 1)
                    second(i, 4 * g)
                    first(i, 4 * g + 2)
                    second(i, 4 * g + 1)
                    first(i, 4 * g + 3)
                    if not last:
                        gather(i, g + 1)
                    if start:
                        pe.wait_ge(s["pos_out"], 8 * l + 8)
                    scatter(i, 2 * g)
                    if not last:
                        gather_read(i, g + 1)
                    second(i, 4 * g + 2)

                pe.wait_ge(s["pos"], l + 1)
                for t in range(T):
                    ins = tr(bank[2][0:NE, t * P:(t + 1) * P], slot_no[:, t * NE:(t + 1) * NE], ident[:, :])
                ins.then_inc(s["pos_turned"], 1)
                pe.wait_ge(s["xn_hi"], l + 1)
                pe.wait_ge(s["xn_lo"], l + 1)
                gather(0, 0)
                pe.wait_ge(s["posT"], l + 1)
                spread(0)
                pair(0, 0, start=True)
                with pe.Fori(0, NE // 2 - 2) as i:
                    pair(i, 1)
                pair(0, NE // 2 - 1, last=True)
                second(0, 2 * NE - 1)
                scatter(0, NE - 1)

            def ada_sums(l, out):
                pe.wait_ge(s["ada_chain"], 4 * (ADA_SLABS // 2) * (l + 1))
                pe.wait_ge(s["ada_dve"], KC * (ADA_SLABS // 2) * (l + 1))
                for c in range(48):
                    ins = mm(out[0:48, 0:P], row_pick[:, 48 - c:96 - c], ada_acc[:, c // 2, (c % 2) * P:(c % 2 + 1) * P],
                             start=c == 0, stop=c == 47)
                ins.then_inc(s["ada_sum"], 1)

            def ada_turn(l, out):
                pe.wait_ge(s["ada_rows"], l + 1)
                tr(out[:, 0:48], ada_rows[0:48, :], ident[0:48, 0:48]).then_inc(s["ada_turned"], 1)

            def gate_rows(run):
                pe.wait_ge(s["diag"], run)
                for half in range(2):
                    ins = mm(bank[4 + half][:, :], ones[:, :], diag[:, 4 * half:4 * half + 4, :], start=True, stop=True)
                ins.then_inc(s["gate_bc"], 1)

            pe.wait_ge(s["ident"], 1)
            pe.wait_ge(s["rows_in"], 16 * (N_ROW_DMA - N_ROW_HW))
            pe.wait_ge(s["rows_in_hw"], 16 * N_ROW_HW)
            for t in range(2):
                tr(bank[0][:, t * P:(t + 1) * P], prow[:, t, :], ident[:, :])
            for l in range(LAYERS):
                ins = tr(bank[1][:, l * 48:(l + 1) * 48], abrow[0:48, l, :], ident[0:48, 0:48])
            ins.then_inc(s["prowT"], 1)
            turn(1)
            pe.wait_ge(s["hT_dve"], 1)
            n1 = DFF // FB
            ffn("ffn1", n1, 0)
            pe.wait_ge(s["product"], n1)
            turn(2, memn)
            pe.wait_ge(s["memT"], 1)
            pe.wait_ge(s["x"], 1)
            by_token("mem_kv0", bank[0], memT)
            by_token("mem_kv1", bank[1], memT)
            ada_sums(0, bank[2])
            turn(3)
            have_hT(3)
            ada_turn(0, bank[3])
            pe.wait_ge(s["mod"], 1)
            by_feature("w_in0", bank[2])
            by_feature("w_in1", bank[3])
            by_feature("w_in2", bank[4])
            by_feature("w_in3", bank[5])
            by_token("w_in4", bank[6])
            by_token("w_in5", bank[7])
            pe.wait_ge(s["mem_k"], 1)
            by_token("w_in6", bank[0])
            pe.wait_ge(s["mem_v"], 1)
            by_token("w_in7", bank[1])
            pe.wait_ge(s["lru_w_in"], 16 * 4)
            pe.wait_ge(s["lru_xb"], 1)
            pe.wait_ge(s["xl"], 1)
            pe.wait_ge(s["gelu"], 1)
            for g in range(2):
                for c in range(LC):
                    ins = mm(bank[2 + 2 * g + c // 2][:, (c % 2) * SEQ:(c % 2 + 1) * SEQ], lru_w_all[:, g, c, :],
                             xb[:, c, :], start=True, stop=True)
            ins.then_inc(s["lru_gates"], 1)
            pe.wait_ge(s["qkn"], 1)
            pe.wait_ge(s["moba_v"], 1)
            pe.wait_ge(s["lru_ri"], 1)
            rows_ = xn[:, :, :].rearrange("p t d -> p (t d)")
            for w in range(4):
                for pair in range(2):
                    for t in range(T):
                        ins = tr(bank[w][:, pair * SEQ + t * P:pair * SEQ + (t + 1) * P],
                                 rows_[:, w * 512 + t * 256 + pair * P:w * 512 + t * 256 + (pair + 1) * P], ident[:, :])
            ins.then_inc(s["qkT"], 1)
            pe.wait_ge(s["qk_act"], 1)
            pe.wait_ge(s["qk_dve"], 1)
            for att in range(2):
                for t in range(T):
                    for par in range(2):
                        out = bank[4 - 4 * att + 2 * t + par]
                        for pair in range(2):
                            ins = mm(out[:, pair * SEQ:(pair + 1) * SEQ],
                                     qkT[par * HD:(par + 1) * HD, 2 * att, pair, t * P:(t + 1) * P],
                                     qkT[par * HD:(par + 1) * HD, 2 * att + 1, pair, :], start=True, stop=True)
                ins.then_inc(s["att_s"], 1)
            for att in range(2):
                pe.wait_ge(s["att_p"], att + 1)
                for h in range(4):
                    for t in range(T):
                        for kb in range(T):
                            ins = tr(bank[4 - 4 * att + h][:, kb * SEQ + t * P:kb * SEQ + (t + 1) * P],
                                     att_p[:, att * 8 + 2 * h + t, kb * P:(kb + 1) * P], ident[:, :])
                ins.then_inc(s["att_pT"], 1)
            for att, name in ((0, "moba"), (1, "mem")):
                pe.wait_ge(s[name + "_pT_out"], 1)
                for h in range(4):
                    for kb in range(T):
                        o = (h % 2) * HD
                        ins = mm(bank[4 - 4 * att][o:o + HD, (h // 2) * SEQ:(h // 2 + 1) * SEQ],
                                 v2[:, att, kb, h * HD:(h + 1) * HD], att_pT[:, att * 4 + h, kb, :],
                                 start=kb == 0, stop=kb == T - 1)
                ins.then_inc(s["att_pv"], 1)
            pe.wait_ge(s["mix_heads"], 1)
            pe.wait_ge(s["mix_lru"], 1)
            for n in range(4):
                rows_product(place[f"w_out{n}"], mixT[:, 2 * n:2 * n + 2, :], acc, n == 0, n == 3)
            turn(4)
            pe.wait_ge(s["hT_dve"], 3)
            ffn("ffn2", n1, n1)
            pe.wait_ge(s["x"], 3)
            ada_sums(1, bank[0])

            for l in range(LAYERS):
                run = l + 1
                turn(5 + 2 * l)
                have_hT(5 + 2 * l)
                if l == 0:
                    ada_turn(1, bank[1])
                by_feature(f"proj0.{l}", bank[0])
                if l == 0:
                    pe.wait_ge(s["mod"], 2)
                by_feature(f"proj1.{l}", bank[1])
                by_feature(f"proj6.{l}", bank[2])
                by_feature(f"proj7.{l}", bank[3])
                by_feature(f"proj2.{l}", bank[4])
                by_feature(f"proj3.{l}", bank[5])
                by_token(f"proj4.{l}", bank[6])
                by_token(f"proj5.{l}", bank[7])
                pe.wait_ge(s["hq"], run)
                by_token(f"misc0.{l}", bank[0])
                by_token(f"misc1.{l}", bank[1])
                pe.wait_ge(s["hgate"], run)
                by_token(f"misc2.{l}", bank[2], n=MISC - 2 * FB)
                pe.wait_ge(s["latents"], run)
                for k in range(5):
                    for t in range(T):
                        ins = tr(bank[k // 2][:, (k % 2) * SEQ + t * P:(k % 2) * SEQ + (t + 1) * P],
                                 misc[:, t, k * P:(k + 1) * P], ident[:, :])
                ins.then_inc(s["cT"], 1)
                pe.wait_ge(s["cT_out"], run)
                pe.wait_ge(s["hf"], run)
                pe.wait_ge(s["vh"], run)
                for n in range(2):
                    pos = place[f"q_up{n}.{l}"]
                    landed(pos)
                    w = slot_view(pos, 3 * QL)
                    for t in range(T):
                        for k in range(3):
                            ins = mm(bank[4 + 2 * n + t][:, 0:QL], cT[:, k, t * P:(t + 1) * P], w[:, k, :],
                                     start=k == 0, stop=k == 2)
                    ins.then_inc(tiles_used, 1)
                pos = place[f"kv_up.{l}"]
                rows_product(pos, cT[:, 3:5, :], bank[0:4], True, True)
                pe.wait_ge(s["kv_out"], run)
                pe.wait_ge(s["q_out"], run)
                for n in range(9):
                    if n < 8:
                        if n >= 4:
                            pe.wait_ge(s["gates"], 8 * l + n - 3)
                        by_token(f"gates{n}.{l}", bank[n % 4])
                    if n == 0:
                        pe.wait_ge(s["hk"], run)
                        pe.wait_ge(s["hq"], run)
                        for t in range(T):
                            for h in range(HGH):
                                ins = mm(bank[4 + t][:, h * P:(h + 1) * P], hk[:, h, t * P:(t + 1) * P],
                                         hq[:, h, t * P:(t + 1) * P], start=True, stop=True)
                        ins.then_inc(s["level"], 1)
                        continue
                    pe.wait_ge(s["hy"], 8 * l + n)
                    y = hy[:, :].rearrange("p (h s) -> p h s", h=HGH)
                    if n < 8:
                        if n >= 2:
                            pe.wait_ge(s["level_added"], 9 * l + n - 1)
                        for t in range(T):
                            for h in range(HGH):
                                ins = mm(bank[4 + 2 * (n % 2) + t][:, h * P:(h + 1) * P], y[:, h, t * P:(t + 1) * P],
                                         y[:, h, t * P:(t + 1) * P], start=True, stop=True)
                    else:
                        pe.wait_ge(s["level_added"], 9 * l + n - 1)
                        for h in range(HGH):
                            ins = mm(bank[4][:, h * P:(h + 1) * P], y[:, h, 0:P], y[:, h, P:SEQ], start=True, stop=True)
                    ins.then_inc(s["level"], 1)
                pe.wait_ge(s["level_added"], 9 * l + 9)
                vh_ = vh[:, :, :].rearrange("p t (h c) -> p t h c", h=HGH)
                for h in range(HGH):
                    mm(bank[6][:, h * P:(h + 1) * P], attT[:, 0, h, :], vh_[:, 0, h, :], start=True, stop=True)
                for h in range(HGH):
                    mm(bank[7][:, h * P:(h + 1) * P], attT[:, 1, h, :], vh_[:, 1, h, :], start=True, stop=False)
                    ins = mm(bank[7][:, h * P:(h + 1) * P], attT[:, 2, h, :], vh_[:, 0, h, :], start=False, stop=True)
                ins.then_inc(s["hg_o"], 1)
                pe.wait_ge(s["gates"], 8 * l + 8)
                pe.wait_ge(s["k_rope"], run)
                for src, b0, ev in ((q96, 0, "mla_qT"), (k96, 4, "mla_kT")):
                    if b0:
                        pe.wait_ge(s["oa_rows"], run)
                    for h in range(MH):
                        for t in range(T):
                            ins = tr(bank[b0 + h // 2][0:DQK, (h % 2) * SEQ + t * P:(h % 2) * SEQ + (t + 1) * P],
                                     src[:, t, h, :], ident[:, :])
                    ins.then_inc(s[ev], 1)
                pe.wait_ge(s["qT_out"], run)
                pe.wait_ge(s["kT_out"], run)
                for h in range(HGH):
                    for t in range(T):
                        ins = tr(bank[4 + h // 2][:, (h % 2) * SEQ + t * P:(h % 2) * SEQ + (t + 1) * P],
                                 oa[:, t, h * P:(h + 1) * P], ident[:, :])
                ins.then_inc(s["oaT"], 1)
                for t in range(T):
                    if t:
                        pe.wait_ge(s["mla_max"], T * l + t)
                    for h in range(MH):
                        ins = mm(bank[h // 2][:, (h % 2) * SEQ:(h % 2 + 1) * SEQ], qT96[0:DQK, h, t * P:(t + 1) * P],
                                 kT96[0:DQK, h, :], start=True, stop=True)
                    ins.then_inc(s["mla_s"], 1)
                pe.wait_ge(s["oaT_out"], run)
                pe.wait_ge(s["mla_p"], run)
                for h in range(MH):
                    for t in range(T):
                        for kb in range(T):
                            ins = tr(bank[h][:, kb * SEQ + t * P:kb * SEQ + (t + 1) * P],
                                     mlp_p[:, t * 8 + h, kb * P:(kb + 1) * P], ident[:, :])
                ins.then_inc(s["mla_pT"], 1)
                pe.wait_ge(s["pT_act"], run)
                pe.wait_ge(s["pT_dve"], run)
                for h in range(MH):
                    for kb in range(T):
                        o = (h % 2) * MV
                        ins = mm(bank[h // 4][o:o + MV, (h // 2 % 2) * SEQ:(h // 2 % 2 + 1) * SEQ],
                                 vm[:, kb, h, :], mlp_pT[:, h, kb, :], start=kb == 0, stop=kb == T - 1)
                ins.then_inc(s["mla_pv"], 1)
                for n in range(2):
                    rows_product(place[f"br_a{n}.{l}"], oaT[:, 2 * n:2 * n + 2, :], bank[4:8], n == 0, n == 1)
                pe.wait_ge(s["ymT"], run)
                for n in range(2):
                    rows_product(place[f"br_b{n}.{l}"], ymT[:, 2 * n:2 * n + 2, :], acc, n == 0, n == 1)
                pe.wait_ge(s["merged"], run)
                for k in range(KC):
                    for t in range(T):
                        ins = tr(bank[4 + k // 2][:, (k % 2) * SEQ + t * P:(k % 2) * SEQ + (t + 1) * P],
                                 merged[:, t, k * P:(k + 1) * P], ident[:, :])
                ins.then_inc(s["mergedT"], 1)
                pe.wait_ge(s["mT_act"], run)
                pe.wait_ge(s["mT_dve"], run)
                gate_rows(2 * l + 1)
                for n in range(4):
                    rows_product(place[f"w_out{n}.{l}"], hT[:, 2 * n:2 * n + 2, :], acc, n == 0, n == 3)

                turn(6 + 2 * l)
                have_hT(6 + 2 * l)
                gate_rows(2 * l + 2)
                pe.wait_ge(s["router_in"], 32)
                for t in range(T):
                    for k in range(KC):
                        ins = mm(bank[0][:, t * NE:(t + 1) * NE], hT[:, k, t * P:(t + 1) * P], router[:, k, :],
                                 start=k == 0, stop=k == KC - 1)
                ins.then_inc(s["logits"], 1)
                pe.wait_ge(s["member"], run)
                pe.wait_ge(s["slot_patterns"], run)
                member = rt[:, 14, :]
                mm(bank[1][:, 0:NE], before, member[:, 0:NE], start=True, stop=True)
                mm(bank[1][:, NE:2 * NE], before, member[:, NE:2 * NE], start=True, stop=False)
                mm(bank[1][:, NE:2 * NE], ones[:, :], member[:, 0:NE], start=False, stop=True)
                mm(bank[1][:, 2 * NE:3 * NE], ones[:, :], member[:, 0:NE], start=True, stop=False)
                mm(bank[1][:, 2 * NE:3 * NE], ones[:, :], member[:, NE:2 * NE], start=False, stop=True)\
                    .then_inc(s["counts"], 1)
                pe.wait_ge(s["overflow"], run)
                pe.wait_ge(s["combine"], run)
                pe.wait_ge(s["gbc"], 2 * l + 2)
                full = pe.value_load(overflow[0:1, 0:1], min_val=0, max_val=1)
                base = 2 * n1 + 2 * NE * l
                with pe.If(full):
                    for t in range(T):
                        ins = tr(bank[2][0:NE, t * P:(t + 1) * P], rt[:, 15, t * NE:(t + 1) * NE], ident[:, :])
                    ins.then_inc(s[f"full_pe.{l}"], 1)
                    pe.wait_ge(s[f"full_dve.{l}"], 1)
                    for e in range(NE):
                        ins = mm(bank[e // 2][:, (e % 2) * SEQ:(e % 2 + 1) * SEQ], sel[0:NE, e, :], combT[:, :],
                                 start=True, stop=True)
                    ins.then_inc(s[f"full_pe.{l}"], 1)
                    pe.wait_ge(s[f"cb_act.{l}"], 1)
                    pe.wait_ge(s[f"full_dve.{l}"], 2)
                    swiglu(f"moe.{l}", 2 * NE, base)
                    if l < LAYERS - 1:
                        for name, n in SLOT_COUNTS["pe"]:
                            pe.sem_inc(s[name], n)
                with pe.Else():
                    sparse(l)

        @block.vector
        def _(v):
            done = [0]

            def link(ins):
                done[0] += 1
                ins.then_inc(s["dve_chain"], 1)
                v.wait_ge(s["dve_chain"], done[0])

            ts, tt, stt, cp = v.tensor_scalar, v.tensor_tensor, v.scalar_tensor_tensor, v.tensor_copy
            M, AD = ALU.mult, ALU.add

            def used(name):
                v.wait_ge(tiles_used, place[name] + 1)

            roots = [0]

            def inverse_root(n, width):
                roots[0] += 1
                ts(stat[:, 1, 0:n], stat[:, 0, 0:n], 1.0 / width, EPS, M, AD).then_inc(s["ms"], 1)
                v.wait_ge(s["root"], roots[0])
                link(v.reciprocal(stat[:, 3, 0:n], stat[:, 2, 0:n]))
                link(tt(stat[:, 6, 0:n], stat[:, 3, 0:n], stat[:, 3, 0:n], M))
                link(tt(stat[:, 6, 0:n], stat[:, 6, 0:n], stat[:, 1, 0:n], M))
                link(ts(stat[:, 6, 0:n], stat[:, 6, 0:n], -0.5, 1.5, M, AD))
                link(tt(stat[:, 3, 0:n], stat[:, 3, 0:n], stat[:, 6, 0:n], M))

            def normalise(src, dst):
                for t in range(T):
                    ins = v.tensor_tensor_reduce(dst[:, t, :], src[:, t, :], src[:, t, :], 1.0, 0.0, M, AD,
                                                 stat[:, 0, t:t + 1])
                link(ins)
                inverse_root(T, D)
                for t in range(T):
                    ins = ts(dst[:, t, :], src[:, t, :], stat[:, 3, t:t + 1], None, M)
                return ins

            def turn(run, dst, scale, bias):
                v.wait_ge(s["xnT"], run)
                for k in range(KC // 2, KC):
                    src = bank[4 + k // 2][:, (k % 2) * SEQ:(k % 2 + 1) * SEQ]
                    if bias:
                        ins = ts(dst[:, k, :], src, scale(k), bias(k), M, AD)
                    else:
                        ins = ts(dst[:, k, :], src, scale(k), None, M)
                ins.then_inc(s["hT_dve"], 1)

            def gain(name, off=0):
                return lambda k: col(name, off + k)

            def swiglu(name, n, base, weighted=""):
                pos = place[name]

                def step(i, c, late=True):
                    j, p = 2 * i + c, c % 2
                    v.wait_ge(s["silu"], j + (base + 1))
                    v.wait_ge(tiles_used, RING * i + (pos + (0 if c == 0 else 3 * c - 1) + 2))
                    if late:
                        v.wait_ge(tiles_used, RING * i + (pos + 3 * (c - 2) + 4 + 1))
                    if not weighted:
                        tt(small_b[:, p, :], small_a[:, p, :], bank[5 + 2 * p][:, :], M).then_inc(s["hidden"], 1)
                    else:
                        tt(ep[:, p, :], small_a[:, p, :], bank[5 + 2 * p][:, :], M).then_inc(s["full_dve" + weighted], 1)
                        v.wait_ge(s["full_dve" + weighted], j + 3)
                        e = cb[:, bass.ds(i + c // 2, 1), :].broadcast_to([P, 2, SEQ])
                        tt(small_b[:, p, :].rearrange("p (k s) -> p k s", k=2),
                           ep[:, p, :].rearrange("p (k s) -> p k s", k=2), e, M).then_inc(s["hidden"], 1)

                j0, turns = loop_shape(n)
                for c in range(j0):
                    step(0, c, c >= 2)
                with v.Fori(0, turns) as i:
                    step(i, j0)
                    step(i, j0 + 1)
                v.wait_ge(tiles_used, pos + 3 * n)

            def turn_parts(run, split_run, scale):
                for k in range(KC):
                    if k % 2 == 0:
                        v.wait_ge(s["hT_hi"], 4 * split_run + k // 2 + 1)
                    ins = stt(hT_lo[:, k, :], bank[4 + k // 2][:, (k % 2) * SEQ:(k % 2 + 1) * SEQ], scale(k),
                              hT_hi[:, k, :].bitcast(F32), M, ALU.subtract)
                ins.then_inc(s["hT_dve"], 1)

            def ffn(name, n, base):
                pos0 = place[name]

                def split(i, q):
                    for half in range(2):
                        v.wait_ge(s["w_hi"], 2 * RING * i + (2 * (3 * base + q) + half + 1))
                        c = slice(half * TILE // 2, (half + 1) * TILE // 2)
                        slot = (pos0 + q) % RING
                        ins = tt(w_lo[:, slot, c], ring[:, slot, c], w_hi[:, q % 2, c].bitcast(F32), ALU.subtract)
                    ins.then_inc(s["w_lo"], 1)

                def product(i, c):
                    p = c % 2
                    v.wait_ge(s["silu"], 2 * i + (base + c + 1))
                    v.wait_ge(tiles_used, RING * i + (pos0 + ffn_pos(n, "up", c) + 1))
                    tt(small_a[:, p, :], small_a[:, p, :], bank[5 + 2 * p][:, :], M).then_inc(s["product"], 1)

                def hidden(i, c):
                    p = c % 2
                    v.wait_ge(s["hid_hi"], 2 * i + (base + c + 1))
                    tt(hid_lo[:, p, :], small_a[:, p, :], hid_hi[:, p, :].bitcast(F32), ALU.subtract).then_inc(s["hidden"], 1)

                def ada(i, m, ks):
                    before = KC * (ADA_SLABS // 2 * l + m)
                    if ks[0] == 0:
                        v.wait_ge(s["ada_in1"], 32 * i + 16 * (ADA_SLABS // 2 * l + m + 1))
                    to = ada_acc[:, bass.ds(4 * i + (2 * m + 1), 1), :]
                    for k in ks:
                        if k:
                            v.wait_ge(s["ada_dve"], 2 * KC * i + (before + k))
                            ins = stt(to, ada_w[:, 1, k:k + 1, :], csilu[:, k:k + 1], to, M, AD)
                        else:
                            ins = ts(to, ada_w[:, 1, 0:1, :], csilu[:, 0:1], None, M)
                        ins.then_inc(s["ada_dve"], 1)

                def step(i, c):
                    q = ffn_pos(n, "gate", c)
                    split(i, q)
                    product(i, c - 1)
                    ada(i, c - 1, range(0, 2))
                    split(i, q + 1)
                    hidden(i, c - 1)
                    ada(i, c - 1, range(2, 4))
                    split(i, q + 2)
                    ada(i, c - 1, range(4, KC))

                l = base // n
                split(0, 0)
                split(0, 1)
                j0, turns = loop_shape(n)
                for c in range(1, j0):
                    step(0, c)
                with v.Fori(0, turns) as i:
                    step(i, j0)
                    step(i, j0 + 1)
                product(0, n - 1)
                hidden(0, n - 1)
                split(0, 3 * n - 1)
                for m in (n - 1, n):
                    ada(0, m, range(KC))
                v.wait_ge(tiles_used, pos0 + 3 * n)

            def sparse(l):
                pos0 = place[f"moe.{l}"]
                base = 2 * (DFF // FB) + 2 * NE * l
                slots = slot_no.rearrange("p (t e) -> p t e", t=T)

                def parts(i, c):
                    p, slot = c % 2, (pos0 + expert_pos("down", c)) % RING
                    v.wait_ge(s["hid_hi"], 4 * i + (base + c + 1))
                    if c >= 2:
                        v.wait_ge(tiles_used, 2 * RING * i + (pos0 + expert_pos("down", c - 2) + 1))
                    tt(down_hid_lo[:, p, :], small_a[:, p, 0:2 * P], hid_hi[:, p, 0:2 * P].bitcast(F32), ALU.subtract)\
                        .then_inc(s["hidden"], 1)
                    for half in range(2):
                        v.wait_ge(s["w_hi"], 8 * i + (6 * STEPS_1 + 4 * NE * l + 2 * c + half + 1))
                        cs = slice(half * TILE // 2, (half + 1) * TILE // 2)
                        ins = tt(w_lo[:, slot, cs], ring[:, slot, cs], down_hi[:, p, cs].bitcast(F32), ALU.subtract)
                    ins.then_inc(s["w_lo"], 1)

                def step(i, c):
                    p = c % 2
                    if c:
                        parts(i, c - 1)
                    v.wait_ge(s["silu"], 4 * i + (base + c + 1))
                    tt(small_a[:, p, 0:2 * P], small_a[:, p, 0:2 * P], bank[4 + p][:, 2 * P:4 * P], M)\
                        .then_inc(s["product"], 1)

                def picks(i, g):
                    if g:
                        v.wait_ge(s["weights"], i + (8 * l + g))
                    for t in range(T):
                        ins = tt(pick[:, t], slot_row.unsqueeze(1).broadcast_to([P, 2, P]),
                                 slots[:, t, bass.ds(2 * i + 2 * g, 2)].unsqueeze(2).broadcast_to([P, 2, P]), ALU.is_equal)
                    ins.then_inc(s["pick"], 1)

                def puts(i, e):
                    if e < 2:
                        v.wait_ge(s["pos_out"], 8 * l + 8)
                    else:
                        v.wait_ge(s["scattered"], 2 * i + (16 * l + e - 1))
                    ts(put[:, e % 2, :], pos_bc[:, bass.ds(2 * i + e, 1), :], slot_col[:, 0:1], None, ALU.is_equal)\
                        .then_inc(s["put"], 1)

                def gathered(i, g):
                    for r in (1, 3):
                        v.wait_ge(s["gathered"], 4 * i + (32 * l + 4 * g + r + 1))
                        for k in (2 * r, 2 * r + 1):
                            ins = ts(hT[:, k, :], bank[7][:, (k % 2) * SEQ:(k % 2 + 1) * SEQ], scol[:, l, 1, k:k + 1],
                                     modc[:, l, 24 + k:25 + k], M, AD)
                        ins.then_inc(s["xg_dve"], 1)
                    v.wait_ge(s["weights"], i + (8 * l + g + 1))
                    if g:
                        v.wait_ge(s["w_slot"], i + (8 * l + g))
                    cp(w_next[:, 0:2], bank[6][:, 0:2]).then_inc(s["w_next"], 1)

                def ye(i, e):
                    v.wait_ge(s["ye_hi"], 2 * i + (16 * l + e + 1))
                    if e:
                        v.wait_ge(s["scattered"], 2 * i + (16 * l + e))
                    for half in range(2):
                        c = slice(half * 512, (half + 1) * 512)
                        ins = stt(ye_parts[:, 1, c], bank[6 + half][:, :], w_slot[:, e % 2:e % 2 + 1],
                                  ye_parts[:, 0, c].bitcast(F32), M, ALU.subtract)
                    ins.then_inc(s["ye_lo"], 1)

                def weights(i, g):
                    v.wait_ge(s["w_next"], i + (8 * l + g + 1))
                    if g:
                        v.wait_ge(s["ye_lo"], 2 * i + (16 * l + 2 * g))
                    cp(w_slot[:, 0:2], w_next[:, 0:2]).then_inc(s["w_slot"], 1)
                    v.wait_ge(s["w_slot"], i + (8 * l + g + 1))

                def pair(i, g, start=False, last=False):
                    step(i, 4 * g)
                    if not start:
                        ye(i, 2 * g - 1)
                    weights(i, g)
                    step(i, 4 * g + 1)
                    if not last:
                        picks(i, g + 1)
                    puts(i, 2 * g)
                    step(i, 4 * g + 2)
                    puts(i, 2 * g + 1)
                    ye(i, 2 * g)
                    step(i, 4 * g + 3)
                    if not last:
                        gathered(i, g + 1)

                picks(0, 0)
                v.wait_ge(s["pos_turned"], l + 1)
                v.wait_ge(s["sel"], l + 1)
                cp(posT[0:NE, :], bank[2][0:NE, 0:SEQ]).then_inc(s["posT"], 1)
                gathered(0, 0)
                pair(0, 0, start=True)
                with v.Fori(0, NE // 2 - 2) as i:
                    pair(i, 1)
                pair(0, NE // 2 - 1, last=True)
                parts(0, 2 * NE - 1)
                ye(0, NE - 1)
                v.wait_ge(s["scattered"], 16 * l + NE)

            def add_to_x(scale):
                for t in range(T):
                    for half in range(2):
                        xs = x[:, t, half * 512:(half + 1) * 512]
                        ins = stt(xs, acc[2 * t + half][:, :], scale, xs, M, AD)
                ins.then_inc(s["x"], 1)

            def add_gated_to_x():
                for t in range(T):
                    for half in range(2):
                        ins = tt(xn[:, t, half * 512:(half + 1) * 512], acc[2 * t + half][:, :],
                                 gbc[:, half * 512:(half + 1) * 512], M)
                link(ins)
                tt(x[:, :, :], x[:, :, :], xn[:, :, :], AD).then_inc(s["x"], 1)

            def modulation(l):
                v.wait_ge(s["ada_turned"], l + 1)
                link(tt(modc[:, l, :], bank[1 if l else 3][:, 0:48], abcol[:, l, :], AD))
                stt(scol[:, l, 0, :], modc[:, l, 8:16], 1.0, col("n1", 8 * l, 8), AD, M)
                stt(scol[:, l, 1, :], modc[:, l, 32:40], 1.0, col("n2", 8 * l, 8), AD, M).then_inc(s["mod"], 1)
                v.wait_ge(s["mod"], l + 1)

            def gate_diag(l, c0):
                tt(diag[:, :, :], ident[:, :].unsqueeze(1).broadcast_to([P, KC, P]),
                   modc[:, l, c0:c0 + KC].unsqueeze(2).broadcast_to([P, KC, P]), M).then_inc(s["diag"], 1)

            def gate_copy(run, scale):
                v.wait_ge(s["gate_bc"], run)
                for half in range(2):
                    ins = ts(gbc[:, half * 512:(half + 1) * 512], bank[4 + half][:, :], scale, None, M)
                ins.then_inc(s["gbc"], 1)

            def negative_max(src, r0, n, scale):
                link(v.tensor_reduce(stat[:, 7, r0:r0 + n], src, AX.X, ALU.max))
                return ts(stat[:, 4, r0:r0 + n], stat[:, 7, r0:r0 + n], -scale, None, M)

            link(v.memset(stat[:, :, :], 1.0))
            v.memset(ones[:, :], 1.0).then_inc(s["ones"], 1)
            v.memset(prow[:, :, :], 0.0).then_inc(s["prow_zero"], 1)
            v.memset(lru_w_all[:, :, :, :], 0.0).then_inc(s["lru_w_zero"], 1)
            v.wait_ge(s["x_in"], 16)
            normalise(x, xn).then_inc(s["xn"], 1)
            v.wait_ge(s["mem_in"], 16)
            normalise(memx, memn).then_inc(s["xn"], 1)
            v.wait_ge(s["prowT"], 1)
            cp(pcol[:, :, :].rearrange("p a b -> p (a b)"), bank[0][:, 0:2 * P])
            cp(abcol[:, :, :].rearrange("p a b -> p (a b)"), bank[1][:, 0:LAYERS * 48]).then_inc(s["pcol"], 1)
            v.wait_ge(s["pcol"], 1)
            turn_parts(1, 0, gain("ffn1"))
            n1 = DFF // FB
            ffn("ffn1", n1, 0)
            add_to_x(0.5)
            v.wait_ge(s["x"], 1)
            normalise(x, xn).then_inc(s["xn"], 1)
            turn(3, hT, gain("mix"), None)
            modulation(0)
            used("mem_kv0")
            cp(qk4[:, 3, :], bank[0][:, :]).then_inc(s["mem_k"], 1)
            l0, l1 = col("lb", 0, 4), col("lb", 4, 4)
            link(tt(lbc[:, 4, :], l0, l1, ALU.max))
            tt(lbc[:, 0, :], l0, lbc[:, 4, :], ALU.subtract)
            tt(lbc[:, 1, :], l1, lbc[:, 4, :], ALU.subtract)
            link(ts(lruc[:, 0, :], col("lam", 0, 4), -1.0, None, M))
            tt(lruc[:, 1, :], lruc[:, 0, :], col("lam", 0, 4), ALU.max).then_inc(s["small_in"], 1)
            v.wait_ge(s["small_exp"], 1)
            link(tt(lbc[:, 4, :], lbc[:, 2, :], lbc[:, 3, :], AD))
            link(v.reciprocal(lbc[:, 4, :], lbc[:, 4, :]))
            tt(lbc[:, 2, :], lbc[:, 2, :], lbc[:, 4, :], M)
            link(tt(lbc[:, 3, :], lbc[:, 3, :], lbc[:, 4, :], M))
            link(tt(lbc[:, 5, :], lbc[:, 2, :], lbc[:, 3, :], AD))
            tt(lbc[:, 0, :], lbc[:, 2, :], lbc[:, 2, :], ALU.subtract)
            link(tt(lbc[:, 1, :], lbc[:, 5, :], lbc[:, 2, :], ALU.subtract))
            for l in range(LAYERS):
                link(ts(lbc[:, 6 + l, :], lbc[:, l, :], -1.0, 1.0, M, AD))
            link(ts(lruc[:, 3, :], lruc[:, 2, :], 2.0, None, AD))
            link(v.reciprocal(lruc[:, 3, :], lruc[:, 3, :]))
            link(tt(lruc[:, 3, :], lruc[:, 2, :], lruc[:, 3, :], M))
            link(tt(lruc[:, 4, :], lruc[:, 3, :], lruc[:, 3, :], M))
            link(ts(lruc[:, 5, :], lruc[:, 4, :], 1.0 / 21, None, M))
            for n in range(19, 2, -2):
                link(stt(lruc[:, 5, :], lruc[:, 5, :], 1.0 / n, lruc[:, 4, :], AD, M))
            link(stt(lruc[:, 6, :], lruc[:, 5, :], 1.0, lruc[:, 3, :], AD, M))
            link(ts(lruc[:, 7, :], lruc[:, 0, :], 0.0, None, ALU.max))
            link(stt(lruc[:, 5, :], lruc[:, 6, :], 2.0, lruc[:, 7, :], M, AD))
            ts(lruc[:, 8, :], lruc[:, 5, :], -LRU_C, None, M)
            link(ts(lruc[:, 9, :], lruc[:, 5, :], LRU_C, None, M))
            used("mem_kv1")
            v.memset(xl[:, :, 0:3], 0.0).then_inc(s["xl_zero"], 1)
            v.wait_ge(s["xl"], 1)
            for j in range(4):
                for c in range(LC):
                    w = col("convw", 4 * j + c)
                    if j == 0:
                        ins = ts(xb[:, c, :], xl[:, c, 0:SEQ], w, col("convb", c), M, AD)
                    else:
                        ins = stt(xb[:, c, :], xl[:, c, j:j + SEQ], w, xb[:, c, :], M, AD)
                if j < 3:
                    link(ins)
            ins.then_inc(s["lru_xb"], 1)
            used("w_in4")
            cp(qk4[:, 0, :], bank[6][:, :])
            used("w_in5")
            cp(qk4[:, 1, :], bank[7][:, :])
            used("w_in7")
            link(cp(qk4[:, 2, :], bank[1][:, :]))
            rows_ = xn[:, :, :].rearrange("p t d -> p (t d)")
            qk_flat = qk4[:, :, :].rearrange("p w c -> p (w c)")
            link(tt(rows_, qk_flat, qk_flat, M))
            link(v.tensor_reduce(stat[:, 0, 0:32], rows_.rearrange("p (r c) -> p r c", c=HD), AX.X, AD))
            inverse_root(32, HD)
            tt(rows_.rearrange("p (r c) -> p r c", c=HD), qk_flat.rearrange("p (r c) -> p r c", c=HD),
               stat[:, 3, 0:32].unsqueeze(2).broadcast_to([P, 32, HD]), M).then_inc(s["qkn"], 1)
            v.wait_ge(s["lru_a"], 1)
            sc = small_a[:, :, :].rearrange("p a b -> p (a b)")
            lt_flat = lt[:, :, :].rearrange("p c s -> p (c s)")
            link(ts(sc, lt_flat, 1.0, None, AD))
            link(v.reciprocal(sc, sc))
            link(tt(sc, sc, lt_flat, M))
            ts(lt_flat, sc, 1.0e-30, None, ALU.max).then_inc(s["lru_m2"], 1)
            v.wait_ge(s["qkT"], 1)
            for w in range(2, 4):
                ins = ts(qkT[:, w].rearrange("p a b -> p (a b)"), bank[w][:, :], col("heads", w), None, M)
            ins.then_inc(s["qk_dve"], 1)
            v.wait_ge(s["att_s"], 1)
            for h in range(4):
                slope = 2.0 ** (-8.0 * (h + 1) / 4)
                for t in range(T):
                    ins = stt(att_p[:, 2 * h + t, :], dist[:, t, :], -slope / HD ** -0.5,
                              bank[4 + 2 * t + h % 2][:, (h // 2) * SEQ:(h // 2 + 1) * SEQ], M, AD)
            link(ins)
            negative_max(att_p[:, 0:8, :], 0, 8, HD ** -0.5).then_inc(s["att_max"], 1)
            v.wait_ge(s["att_s"], 2)
            for t in range(T):
                for par in range(2):
                    for pair in range(2):
                        h = 2 * pair + par
                        ins = v.tensor_reduce(stat[:, 7, 8 + 2 * h + t:9 + 2 * h + t],
                                              bank[2 * t + par][:, pair * SEQ:(pair + 1) * SEQ], AX.X, ALU.max)
            link(ins)
            ts(stat[:, 4, 8:16], stat[:, 7, 8:16], -HD ** -0.5, None, M).then_inc(s["att_max"], 1)
            v.wait_ge(s["lru_mult"], 1)
            v.memset(lt[:, :, 0:1], 1.0)
            v.memset(lt2[:, :, 0:1], 0.0)
            link(tt(li[:, :, :], li[:, :, :], xb[:, :, :], M))
            link(tt(li[:, :, :], li[:, :, :], lt[:, :, :], M))
            link(v.tensor_tensor_scan(lt_flat, lt2[:, :, :].rearrange("p c s -> p (c s)"),
                                      li[:, :, :].rearrange("p c s -> p (c s)"), 0.0, M, AD))
            tt(mixT[:, 0:4, :], lt[:, :, :], gel[:, :, :], M).then_inc(s["mix_lru"], 1)
            for att in range(2):
                v.wait_ge(s["att_exp"], att + 1)
                link(v.reciprocal(stat[:, 6, 8 * att:8 * att + 8], stat[:, 5, 8 * att:8 * att + 8]))
                for r in range(8 * att, 8 * att + 8):
                    ins = ts(att_p[:, r, :], att_p[:, r, :], stat[:, 6, r:r + 1], None, M)
                ins.then_inc(s["att_p"], 1)
            v.wait_ge(s["att_pT"], 2)
            for h in range(4):
                ins = cp(att_pT[:, 4 + h].rearrange("p a b -> p (a b)"), bank[h][:, :])
            ins.then_inc(s["mem_pT_out"], 1)
            used("w_out3")
            add_to_x(1.0)
            v.wait_ge(s["x"], 2)
            normalise(x, xn).then_inc(s["xn"], 1)
            turn_parts(4, 1, gain("ffn2"))
            ffn("ffn2", n1, n1)
            add_to_x(0.5)
            v.wait_ge(s["x"], 3)

            scale = DK ** -0.5

            def before_layers():
                modulation(1)
                v.wait_ge(s["inv_freq"], 1)
                v.wait_ge(s["pos_in"], 16)
                link(cp(stat[:, 7, 0:T], pos_i[:, :]))
                for t in range(T):
                    ins = ts(rope_t[:, 1, t, :], rope_t[:, 0, 0, :], stat[:, 7, t:t + 1], None, M)
                link(ins)
                two_pi = 2 * np.pi
                c1 = 6.28125
                c2 = np.floor((two_pi - c1) * 2 ** 21) / 2 ** 21
                c3 = two_pi - c1 - c2
                for n, quarter in ((0, 0.25), (1, 0.0)):
                    link(ts(rope_t[:, 2], rope_t[:, 1], 1 / two_pi, quarter, M, AD))
                    link(cp(rope_t[:, 3].bitcast(I32), rope_t[:, 2]))
                    link(cp(rope_t[:, 2], rope_t[:, 3].bitcast(I32)))
                    link(stt(rope_t[:, 4], rope_t[:, 2], -c1, rope_t[:, 1], M, AD))
                    link(stt(rope_t[:, 5], rope_t[:, 2], -c2, rope_t[:, 4], M, AD))
                    link(stt(rope_t[:, 6], rope_t[:, 2], -c3, rope_t[:, 5], M, AD))
                    link(ts(rope_t[:, 7], rope_t[:, 6], quarter * two_pi, 3.1415925, AD, ALU.min))
                    link(ts(rope_t[:, 8 + n], rope_t[:, 7], -3.1415925, None, ALU.max))
                cp(stat[:, 6, 0:1], stat[:, 7, 0:1]).then_inc(s["small_in"], 1)
                v.wait_ge(s["patterns"], 2)
                v.wait_ge(s["ident"], 1)
                ts(rank[:, :], iot[:, 1, 0:NE], -1.0, float(NE), M, AD)
                link(tt(iot[:, 2, :], iot[:, 0, :], iot[:, 1, :], ALU.bitwise_xor))
                link(tt(diag[:, 0, :], iot[:, 1, :], iot[:, 0, :], ALU.is_gt))
                for n, L in enumerate(LEVELS[:-1]):
                    link(ts(diag[:, 1, :], iot[:, 2, :], float(L), scale, ALU.is_ge, M))
                    link(stt(diag[:, 2, :], iot[:, 2, :], float(2 * L), diag[:, 1, :], ALU.is_lt, M))
                    link(tt(level_mask[:, n, :], diag[:, 2, :], diag[:, 0, :], M))
                link(ts(level_mask[:, 7, :], ident[:, :], scale, None, M))
                idx, low = view(22000, 1028).bitcast(I32), view(23100, 1028).bitcast(I32)
                for n, L in enumerate(LEVELS):
                    link(ts(low, idx, L - 1, None, ALU.bitwise_and))
                    link(ts(seg[:, n, :], low, 0.0, None, ALU.is_gt))


            for l in range(LAYERS):
                run = l + 1
                normalise(x, xn).then_inc(s["xn"], 1)
                turn(5 + 2 * l, hT, lambda k: scol[:, l, 0, k:k + 1], lambda k: modc[:, l, k:k + 1])
                if l == 0:
                    before_layers()
                v.wait_ge(s["hf"], run)
                for h in range(HGH):
                    ins = ts(hf[:, h, :], hf[:, h, :], lbc[:, 6 + l, h:h + 1], lbc[:, l, h:h + 1], M, AD)
                link(ins)
                ts(hg[:, :, :], hf[:, :, :], 1.0e-19, None, ALU.max).then_inc(s["hf_clamped"], 1)
                ts(hk[:, :, :], hf[:, :, :], -1.0, 1.0, M, AD).then_inc(s["hk"], 1)
                for n in range(2):
                    used(f"proj{4 + n}.{l}")
                    ins = cp(vh[:, :, n * FB:(n + 1) * FB], bank[6 + n][:, :].rearrange("p (t c) -> p t c", t=T))
                ins.then_inc(s["vh"], 1)
                v.wait_ge(s["misc"], run)
                for t in range(T):
                    v.tensor_tensor_reduce(scr[:, 0:QL], misc[:, t, 0:QL], misc[:, t, 0:QL], 1.0, 0.0, M, AD,
                                           stat[:, 0, t:t + 1])
                    ins = v.tensor_tensor_reduce(scr[:, QL:QL + KVL], misc[:, t, QL:QL + KVL], misc[:, t, QL:QL + KVL],
                                                 1.0, 0.0, M, AD, stat[:, 0, 2 + t:3 + t])
                    link(ins)
                link(ts(stat[:, 0, 2:4], stat[:, 0, 2:4], QL / KVL, None, M))
                inverse_root(4, QL)
                for t in range(T):
                    ts(misc[:, t, 0:QL], misc[:, t, 0:QL], stat[:, 3, t:t + 1], None, M)
                    ins = ts(misc[:, t, QL:QL + KVL], misc[:, t, QL:QL + KVL], stat[:, 3, 2 + t:3 + t], None, M)
                ins.then_inc(s["latents"], 1)
                v.wait_ge(s["sincos"], 1)
                half = ROPE // 2
                cos, sin = rope_t[:, 10], rope_t[:, 11]
                k1, k2 = misc[:, :, QL + KVL:QL + KVL + half], misc[:, :, QL + KVL + half:MISC]
                tmp = [scr[:, 256 * n:256 * n + 256] for n in range(4)]
                small = [z[:, 0:T * half].rearrange("p (t c) -> p t c", t=T) for z in tmp]
                tt(small[0], k1, cos, M)
                tt(small[1], k2, sin, M)
                tt(small[2], k1, sin, M)
                link(tt(small[3], k2, cos, M))
                tt(small[0], small[0], small[1], ALU.subtract)
                link(tt(small[2], small[2], small[3], AD))
                for t in range(T):
                    cp(k96[:, t, :, NOPE:NOPE + half], small[0][:, t:t + 1, :].broadcast_to([P, MH, half]))
                    ins = cp(k96[:, t, :, NOPE + half:DQK], small[2][:, t:t + 1, :].broadcast_to([P, MH, half]))
                ins.then_inc(s["k_rope"], 1)
                v.wait_ge(s["k_rope"], run)
                for n in range(2):
                    used(f"q_up{n}.{l}")
                    for t in range(T):
                        ins = cp(q96[:, t, 4 * n:4 * n + 4, :].rearrange("p h c -> p (h c)"), bank[4 + 2 * n + t][:, 0:QL])
                link(ins)
                big = [z.rearrange("p (t h c) -> p t h c", t=T, h=MH) for z in tmp]
                for t in range(T):
                    q1, q2 = q96[:, t, :, NOPE:NOPE + half], q96[:, t, :, NOPE + half:DQK]
                    cb_ = cos[:, t:t + 1, :].broadcast_to([P, MH, half])
                    sb_ = sin[:, t:t + 1, :].broadcast_to([P, MH, half])
                    tt(big[0][:, t], q1, cb_, M)
                    tt(big[1][:, t], q2, sb_, M)
                    tt(big[2][:, t], q1, sb_, M)
                    ins = tt(big[3][:, t], q2, cb_, M)
                link(ins)
                for t in range(T):
                    tt(q96[:, t, :, NOPE:NOPE + half], big[0][:, t], big[1][:, t], ALU.subtract)
                    ins = tt(q96[:, t, :, NOPE + half:DQK], big[2][:, t], big[3][:, t], AD)
                ins.then_inc(s["q_out"], 1)
                v.wait_ge(s["hg"], run)
                v.wait_ge(s["hq"], run)
                g_flat = hg[:, :, :].rearrange("p h s -> p (h s)")
                N = HGH * SEQ

                def add_level(n, mask):
                    v.wait_ge(s["level"], 9 * l + n + 1)
                    m = level_mask[:, mask, :].unsqueeze(1).broadcast_to([P, HGH, P])
                    for t in range(T):
                        src = bank[4 + 2 * (n % 2) + t][:, :].rearrange("p (h c) -> p h c", h=HGH)
                        if n == 0:
                            ins = tt(attT[:, t], src, m, M)
                        else:
                            link(tt(prod[:, t], src, m, M))
                            ins = tt(attT[:, t], attT[:, t], prod[:, t], AD)
                    ins.then_inc(s["level_added"], 1)
                    v.wait_ge(s["level_added"], 9 * l + n + 1)

                for n, L in enumerate(LEVELS):
                    if n:
                        v.wait_ge(s["decay"], 8 * l + n)
                    v.tensor_tensor_scan(scan_f[:, :], seg[:, n, 0:N], g_flat, 0.0, M, AD)
                    v.tensor_tensor_scan(scan_b[:, N - 2::-1], g_flat[:, N - 1:0:-1], seg[:, n, N - 1:0:-1], 0.0, AD, M)\
                        .then_inc(s["scans"], 1)
                    if n:
                        v.wait_ge(s["level"], 9 * l + n + 1)
                        add_level(n, n - 1)
                    else:
                        add_level(0, 7)
                    v.wait_ge(s["decay"], 8 * l + n + 1)
                    by = lambda z: z.rearrange("p (m two c) -> p m two c", two=2, c=L)
                    dec = by(hf[:, :, :].rearrange("p h s -> p (h s)"))
                    y = by(hy[:, :])
                    tt(y[:, :, 1, :], dec[:, :, 1, :], by(hq[:, :, :].rearrange("p h s -> p (h s)"))[:, :, 1, :], M)
                    tt(y[:, :, 0, :], dec[:, :, 0, :], by(hk[:, :, :].rearrange("p h s -> p (h s)"))[:, :, 0, :], M)\
                        .then_inc(s["hy"], 1)
                v.wait_ge(s["level"], 9 * l + 9)
                ts(attT[:, 2], bank[4][:, :].rearrange("p (h c) -> p h c", h=HGH), scale, None, M)\
                    .then_inc(s["level_added"], 1)
                v.wait_ge(s["hg_o"], run)
                for t in range(T):
                    ins = cp(oa[:, t, :], bank[6 + t][:, :])
                link(ins)
                sq = oa_sq[:, :]
                oa_flat = oa[:, :, :].rearrange("p t c -> p (t c)")
                link(tt(sq, oa_flat, oa_flat, M))
                link(v.tensor_reduce(stat[:, 0, 0:8], sq.rearrange("p (r c) -> p r c", c=P), AX.X, AD))
                inverse_root(8, DK)
                tt(oa_flat.rearrange("p (r c) -> p r c", c=P), oa_flat.rearrange("p (r c) -> p r c", c=P),
                   stat[:, 3, 0:8].unsqueeze(2).broadcast_to([P, 8, P]), M).then_inc(s["oa_rows"], 1)
                v.wait_ge(s["mla_kT"], run)
                for n in range(4):
                    ins = cp(kT96[0:DQK, 2 * n:2 * n + 2, :].rearrange("p h s -> p (h s)"), bank[4 + n][0:DQK, :])
                ins.then_inc(s["kT_out"], 1)
                v.wait_ge(s["hgate"], run)
                v.wait_ge(s["oaT"], run)
                for h in range(HGH):
                    ins = stt(oaT[:, h, :], bank[4 + h // 2][:, (h % 2) * SEQ:(h % 2 + 1) * SEQ], col("hgn", 4 * l + h),
                              hgate[:, h, :], M, M)
                ins.then_inc(s["oaT_out"], 1)
                for t in range(T):
                    v.wait_ge(s["mla_s"], T * l + t + 1)
                    for n in range(4):
                        ins = tt(mlp_p[:, 8 * t + 2 * n:8 * t + 2 * n + 2, :],
                                 bank[n][:, :].rearrange("p (h c) -> p h c", h=2),
                                 mla_mask[:, t:t + 1, :].broadcast_to([P, 2, SEQ]), AD)
                    link(ins)
                    negative_max(mlp_p[:, 8 * t:8 * t + 8, :], 8 * t, 8, DQK ** -0.5).then_inc(s["mla_max"], 1)
                v.wait_ge(s["mla_exp"], T * (l + 1))
                link(v.reciprocal(stat[:, 6, 0:16], stat[:, 5, 0:16]))
                for r in range(16):
                    ins = ts(mlp_p[:, r, :], mlp_p[:, r, :], stat[:, 6, r:r + 1], None, M)
                ins.then_inc(s["mla_p"], 1)
                v.wait_ge(s["mla_pT"], run)
                for h in range(4, MH):
                    ins = cp(mlp_pT[:, h].rearrange("p a b -> p (a b)"), bank[h][:, :])
                ins.then_inc(s["pT_dve"], 1)
                used(f"br_a1.{l}")
                for t in range(T):
                    for half_ in range(2):
                        c = slice(half_ * 512, half_ * 512 + 512)
                        ins = stt(merged[:, t, c], G[:, t, 0, c], 1.0, bank[4 + 2 * t + half_][:, :], AD, M)
                link(ins)
                used(f"br_b1.{l}")
                for t in range(T):
                    for half_ in range(2):
                        c = slice(half_ * 512, half_ * 512 + 512)
                        ins = stt(xn[:, t, c], G[:, t, 1, c], 1.0, acc[2 * t + half_][:, :], AD, M)
                link(ins)
                tt(merged[:, :, :], merged[:, :, :], xn[:, :, :], AD).then_inc(s["merged"], 1)
                gate_diag(l, 16)
                v.wait_ge(s["mergedT"], run)
                for k in range(KC // 2, KC):
                    ins = cp(hT[:, k, :], bank[4 + k // 2][:, (k % 2) * SEQ:(k % 2 + 1) * SEQ])
                ins.then_inc(s["mT_dve"], 1)
                gate_copy(2 * l + 1, 0.5)
                used(f"w_out3.{l}")
                v.wait_ge(s["gbc"], 2 * l + 1)
                add_gated_to_x()
                v.wait_ge(s["x"], 4 + 2 * l)

                normalise(x, xn).then_inc(s["xn"], 1)
                gate_diag(l, 40)
                cp(sel_r[0:NE, :, :], ident[0:NE, 0:NE].unsqueeze(2).broadcast_to([NE, NE, P])).then_inc(s["sel"], 1)
                turn(6 + 2 * l, hT, lambda k: scol[:, l, 1, k:k + 1], lambda k: modc[:, l, 24 + k:25 + k])
                gate_copy(2 * l + 2, 1.0)
                v.wait_ge(s["scores"], run)
                v.wait_ge(s["slot_patterns"], run)

                def r(n):
                    return rt[:, n, :].rearrange("p (t e) -> p t e", t=T)

                def rg(n):
                    return rt[:, n, :].rearrange("p (g e) -> p g e", e=EPG)

                link(tt(r(1), r(0), rbias[:, :].unsqueeze(1).broadcast_to([P, T, NE]), AD))
                b_ = rg(1)
                p6 = rt[:, 2:4, :].rearrange("p a b -> p (a b)")[:, 0:6 * T * NG].rearrange("p (g k) -> p g k", k=6)
                tt(p6[:, :, 0:2], b_[:, :, 0:2], b_[:, :, 2:4], AD)
                tt(p6[:, :, 2:3], b_[:, :, 0:1], b_[:, :, 1:2], AD)
                tt(p6[:, :, 3:4], b_[:, :, 2:3], b_[:, :, 3:4], AD)
                tt(p6[:, :, 4:5], b_[:, :, 0:1], b_[:, :, 3:4], AD)
                link(tt(p6[:, :, 5:6], b_[:, :, 1:2], b_[:, :, 2:3], AD))
                gs = rt[:, 4, 0:T * NG].rearrange("p (t g) -> p t g", t=T)
                link(v.tensor_reduce(rt[:, 4, 0:T * NG], p6, AX.X, ALU.max))

                def first_best(scores_, n, rank, mx, out_, eq):
                    link(v.tensor_reduce(mx, scores_, AX.X, ALU.max))
                    link(tt(eq, scores_, mx.unsqueeze(2).broadcast_to([P, T, n]), ALU.is_equal))
                    link(tt(eq, eq, rank.unsqueeze(1).broadcast_to([P, T, n]), M))
                    link(v.tensor_reduce(mx, eq, AX.X, ALU.max))
                    link(tt(out_, eq, mx.unsqueeze(2).broadcast_to([P, T, n]), ALU.is_equal))

                mx = rt[:, 6, 0:T]
                gsel = rt[:, 7, 0:T * NG].rearrange("p (t g) -> p t g", t=T)
                first_best(gs, NG, rank[:, 0:NG], mx, gsel, rt[:, 8, 0:T * NG].rearrange("p (t g) -> p t g", t=T))
                gm = rt[:, 7, 0:T * NG].unsqueeze(2).broadcast_to([P, T * NG, EPG])
                link(tt(rg(9), rg(1), gm, M))
                link(ts(rt[:, 7, 0:T * NG], rt[:, 7, 0:T * NG], -1.0, -NEG, AD, M))
                link(tt(rg(9), rg(9), gm, AD))
                first_best(r(9), NE, rank[:, :], mx, r(10), r(11))
                link(stt(r(12), r(10), 2 * NEG, r(9), M, AD))
                first_best(r(12), NE, rank[:, :], mx, r(13), r(11))
                tt(r(14), r(13), r(10), AD).then_inc(s["member"], 1)
                v.wait_ge(s["member"], run)
                link(tt(r(13), r(14), r(0), M))
                link(v.tensor_reduce(mx, r(13), AX.X, AD))
                link(v.reciprocal(mx, mx))
                tt(r(15), r(13), mx.unsqueeze(2).broadcast_to([P, T, NE]), M).then_inc(s["combine"], 1)
                v.wait_ge(s["counts"], run)
                link(v.tensor_reduce(rt[:, 5, 0:1], bank[1][:, 2 * NE:3 * NE], AX.X, ALU.max))
                ts(overflow[:, 0:1], rt[:, 5, 0:1], float(P), None, ALU.is_gt).then_inc(s["overflow"], 1)
                v.wait_ge(s["overflow"], run)
                link(stt(slot_no, bank[1][:, 0:2 * NE], 1.0, rt[:, 14, :], AD, M))
                ts(slot_no, slot_no, -1.0, None, AD).then_inc(s["pos"], 1)
                v.wait_ge(s["pos"], run)
                full = v.value_load(overflow[0:1, 0:1], min_val=0, max_val=1)
                base = 2 * n1 + 2 * NE * l
                with v.If(full):
                    cp(sel[0:NE, :, :], ident[0:NE, 0:NE].unsqueeze(2).broadcast_to([NE, NE, P]))
                    v.wait_ge(s[f"full_pe.{l}"], 1)
                    cp(combT[:, :], bank[2][0:NE, 0:SEQ]).then_inc(s[f"full_dve.{l}"], 1)
                    v.wait_ge(s[f"full_pe.{l}"], 2)
                    for n in range(4, 8):
                        ins = cp(cb[:, 2 * n:2 * n + 2, :].rearrange("p a b -> p (a b)"), bank[n][:, :])
                    ins.then_inc(s[f"full_dve.{l}"], 1)
                    v.wait_ge(s[f"full_dve.{l}"], 2)
                    v.wait_ge(s["xn_lo"], run)
                    v.wait_ge(s[f"cb_act.{l}"], 1)
                    swiglu(f"moe.{l}", 2 * NE, base, f".{l}")
                    if l < LAYERS - 1:
                        for name, n in SLOT_COUNTS["v"]:
                            v.sem_inc(s[name], n)
                with v.Else():
                    sparse(l)
                add_gated_to_x()
                v.wait_ge(s["x"], 5 + 2 * l)
            link(normalise(x, xn))
            v.wait_ge(s["final_in"], 16)
            tt(xn[:, :, :], xn[:, :, :], fin[:, :].unsqueeze(1).broadcast_to([P, T, D]), M).then_inc(s["out_ready"], 1)


_INS = ["x", "mem", "ffn1_norm", "ffn1_w_in", "ffn1_w_out", "mix_norm", "mem_norm", "w_in", "lru_conv_w", "lru_conv_b",
        "lru_a_w", "lru_a_b", "lru_x_w", "lru_x_b", "lru_lambda", "moba_q_norm", "moba_k_norm", "mem_w_kv",
        "mem_q_norm", "mem_k_norm", "w_out", "ffn2_norm", "ffn2_w_in", "ffn2_w_out", "c_2", "positions_2", "ada_w_2",
        "ada_b_2", "norm1_g_2", "w_in_2", "hg_lb_logits_2", "hg_norm_g_2", "q_norm_g_2", "w_q_up_2", "kv_norm_g_2",
        "w_kv_up_2", "w_br_a_2", "w_br_b_2", "w_out_2", "norm2_g_2", "w_router_2", "router_bias_2", "w_gate_2",
        "w_up_2", "w_down_2", "final_g_2"]


def kernel(**inputs):
    import concourse.bacc as _bacc
    from concourse.bass_utils import run_bass_kernel_spmd as _run

    nc = _bacc.Bacc("TRN2", target_bir_lowering=False, num_devices=1)
    arrays, args = {}, {}
    for name in _INS:
        v = np.ascontiguousarray(inputs[name])
        arrays[f"in_{name}"] = v
        args[name] = nc.dram_tensor(f"in_{name}", v.shape, mybir.dt.from_np(v.dtype), kind="ExternalInput").ap()
    args["out"] = nc.dram_tensor("out_x", (1, SEQ, D), F32, kind="ExternalOutput").ap()
    build(nc, args)
    return _run(nc, [arrays], core_ids=[0]).results[0]["out_x"]
```
